# Optimizing a Trainium2 kernel written in Bass

```python
import jax, jax.numpy as jnp
from jax import lax
import numpy as np

D_MODEL = 1024
BATCH = 1
SEQ = 256
DEPTH = 2

ATT_HEADS = 8
ATT_HEAD_DIM = 64
ATT_WIDTH = ATT_HEADS * ATT_HEAD_DIM
MOBA_BLOCK = 256
MOBA_TOPK = 3
MOBA_Q_CHUNK = 32
RET_HEADS = 4
RET_HEAD_DIM = 128
RET_WIDTH = RET_HEADS * RET_HEAD_DIM
RET_CHUNK = 128
ROPE_BASE = 10000.0
IN_PROJ_WIDTH = 3 * ATT_WIDTH + 4 * RET_WIDTH
D_FF = 2816
N_EXPERTS = 8
TOP_K = 2
EXPERT_D_FF = 2816
MOE_GROUP = 128
EPS = 1e-6


def rms_norm(x, g):
    xf = x.astype(jnp.float32)
    y = xf * lax.rsqrt(jnp.mean(xf * xf, axis=-1, keepdims=True) + EPS)
    return (y * g.astype(jnp.float32)).astype(x.dtype)

def rotary(x):
    s, d = x.shape[1], x.shape[-1]
    half = d // 2
    inv_freq = ROPE_BASE ** (-jnp.arange(half, dtype=jnp.float32) / half)
    ang = jnp.arange(s, dtype=jnp.float32)[:, None] * inv_freq[None, :]
    cos = jnp.cos(ang)[None, :, None, :]
    sin = jnp.sin(ang)[None, :, None, :]
    xf = x.astype(jnp.float32)
    x1, x2 = xf[..., :half], xf[..., half:]
    return jnp.concatenate([x1 * cos - x2 * sin, x1 * sin + x2 * cos], axis=-1).astype(x.dtype)

def moba_attention(q, k, v):
    b, h, s, dh = q.shape
    nb = -(-s // MOBA_BLOCK)
    pad = nb * MOBA_BLOCK - s
    kp = jnp.pad(k, ((0, 0), (0, 0), (0, pad), (0, 0)))
    vp = jnp.pad(v, ((0, 0), (0, 0), (0, pad), (0, 0)))
    kb = kp.reshape(b, h, nb, MOBA_BLOCK, dh)
    vb = vp.reshape(b, h, nb, MOBA_BLOCK, dh)
    scale = dh ** -0.5
    n_sel = min(MOBA_TOPK, nb - 1)
    q_block = jnp.arange(s) // MOBA_BLOCK
    if n_sel > 0:
        k_mean = jnp.mean(kb.astype(jnp.float32), axis=3)
        gate = jnp.einsum('bhsd,bhnd->bhsn', q.astype(jnp.float32), k_mean)
        past = jnp.arange(nb)[None, :] < q_block[:, None]
        gate = jnp.where(past[None, None], gate, -1e30)
        _, sel = lax.top_k(gate, n_sel)
        sel_valid = sel < q_block[None, None, :, None]
    bi = jnp.arange(b)[:, None, None, None]
    hi = jnp.arange(h)[None, :, None, None]

    def chunk_fn(ci):
        start = ci * MOBA_Q_CHUNK
        qc = lax.dynamic_slice_in_dim(q, start, MOBA_Q_CHUNK, axis=2)
        pos = start + jnp.arange(MOBA_Q_CHUNK)
        own = start // MOBA_BLOCK
        k_own = lax.dynamic_index_in_dim(kb, own, axis=2, keepdims=False)
        v_own = lax.dynamic_index_in_dim(vb, own, axis=2, keepdims=False)
        key_pos = own * MOBA_BLOCK + jnp.arange(MOBA_BLOCK)
        s_own = jnp.einsum('bhqd,bhkd->bhqk', qc, k_own).astype(jnp.float32) * scale
        s_own = jnp.where(key_pos[None, :] <= pos[:, None], s_own, -jnp.inf)
        if n_sel > 0:
            sel_c = lax.dynamic_slice_in_dim(sel, start, MOBA_Q_CHUNK, axis=2)
            val_c = lax.dynamic_slice_in_dim(sel_valid, start, MOBA_Q_CHUNK, axis=2)
            k_sel = kb[bi, hi, sel_c]
            v_sel = vb[bi, hi, sel_c]
            s_sel = jnp.einsum('bhqd,bhqnkd->bhqnk', qc, k_sel).astype(jnp.float32) * scale
            s_sel = jnp.where(val_c[..., None], s_sel, -jnp.inf)
            s_sel = s_sel.reshape(b, h, MOBA_Q_CHUNK, n_sel * MOBA_BLOCK)
            p = jax.nn.softmax(jnp.concatenate([s_own, s_sel], axis=-1), axis=-1)
            p_own = p[..., :MOBA_BLOCK].astype(v.dtype)
            p_sel = p[..., MOBA_BLOCK:].reshape(b, h, MOBA_Q_CHUNK, n_sel, MOBA_BLOCK).astype(v.dtype)
            o = (jnp.einsum('bhqk,bhkd->bhqd', p_own, v_own)
                 + jnp.einsum('bhqnk,bhqnkd->bhqd', p_sel, v_sel))
        else:
            p_own = jax.nn.softmax(s_own, axis=-1).astype(v.dtype)
            o = jnp.einsum('bhqk,bhkd->bhqd', p_own, v_own)
        return o

    out = lax.map(chunk_fn, jnp.arange(s // MOBA_Q_CHUNK))
    return jnp.transpose(out, (1, 2, 0, 3, 4)).reshape(b, h, s, dh)

def retention(q, k, v):
    b, h, s, d = q.shape
    c = RET_CHUNK
    nc = s // c
    dt = v.dtype
    lg = jnp.log(1.0 - 2.0 ** (-5.0 - jnp.arange(h, dtype=jnp.float32)))
    idx = jnp.arange(c, dtype=jnp.float32)
    qf = q.astype(jnp.float32).reshape(b, h, nc, c, d)
    kf = (k.astype(jnp.float32) * d ** -0.5).reshape(b, h, nc, c, d)
    vf = v.astype(jnp.float32).reshape(b, h, nc, c, d)
    diff = idx[:, None] - idx[None, :]
    dmask = jnp.where(diff >= 0, jnp.exp(jnp.maximum(diff, 0.0)[None] * lg[:, None, None]), 0.0)
    scores = jnp.einsum('bhncd,bhnmd->bhncm', qf, kf) * dmask[None, :, None]
    inner = jnp.einsum('bhncm,bhnme->bhnce', scores, vf)
    k_dec = kf * jnp.exp((c - 1 - idx)[None, :] * lg[:, None])[None, :, None, :, None]
    kv = jnp.einsum('bhnmd,bhnme->bhnde', k_dec, vf)
    chunk_decay = jnp.exp(c * lg)[None, :, None, None]

    def step(state, kv_n):
        return state * chunk_decay + kv_n, state

    _, r_prev = lax.scan(step, jnp.zeros((b, h, d, d), jnp.float32), jnp.moveaxis(kv, 2, 0))
    r_prev = jnp.moveaxis(r_prev, 0, 2)
    q_dec = qf * jnp.exp((idx + 1.0)[None, :] * lg[:, None])[None, :, None, :, None]
    cross = jnp.einsum('bhncd,bhnde->bhnce', q_dec, r_prev)
    return (inner + cross).reshape(b, h, s, d).astype(dt)

def hybrid_mixer(h, w_in, w_out, att_out_g, ret_out_g):
    b, s, _ = h.shape
    proj = h @ w_in
    A, R = ATT_WIDTH, RET_WIDTH
    q_a, k_a, v_a, q_r, k_r, v_r, g_r = jnp.split(
        proj, [A, 2 * A, 3 * A, 3 * A + R, 3 * A + 2 * R, 3 * A + 3 * R], axis=-1)

    def att_heads(t):
        return t.reshape(b, s, ATT_HEADS, ATT_HEAD_DIM).transpose(0, 2, 1, 3)

    o_a = moba_attention(att_heads(q_a), att_heads(k_a), att_heads(v_a))
    o_a = o_a.transpose(0, 2, 1, 3).reshape(b, s, A)
    o_a = rms_norm(o_a, att_out_g)

    def ret_heads(t):
        return t.reshape(b, s, RET_HEADS, RET_HEAD_DIM)

    qr = rotary(ret_heads(q_r)).transpose(0, 2, 1, 3)
    kr = rotary(ret_heads(k_r)).transpose(0, 2, 1, 3)
    vr = ret_heads(v_r).transpose(0, 2, 1, 3)
    o_r = retention(qr, kr, vr).transpose(0, 2, 1, 3)
    o_r = rms_norm(o_r, ret_out_g.reshape(RET_HEADS, RET_HEAD_DIM)).reshape(b, s, R)
    o_r = jax.nn.silu(g_r) * o_r
    return jnp.concatenate([o_a, o_r], axis=-1) @ w_out

def swiglu(x, w_gate, w_up, w_down):
    return (jax.nn.silu(x @ w_gate) * (x @ w_up)) @ w_down

def moe_ffn(h, w_router, w_gate, w_up, w_down):
    b, s, d = h.shape
    xf = h.reshape(-1, d)
    n = xf.shape[0]
    e_count = w_gate.shape[0]
    g = MOE_GROUP
    logits = (xf @ w_router).astype(jnp.float32)
    top_logits, top_idx = lax.top_k(logits, TOP_K)
    top_w = jax.nn.softmax(top_logits, axis=-1)
    a = n * TOP_K
    e_flat = top_idx.reshape(-1)
    t_flat = jnp.repeat(jnp.arange(n, dtype=jnp.int32), TOP_K)
    w_flat = top_w.reshape(-1)
    order = jnp.argsort(e_flat, stable=True)
    e_sorted = e_flat[order]
    counts = jnp.bincount(e_flat, length=e_count)
    starts = jnp.cumsum(counts) - counts
    padded = (counts + g - 1) // g * g
    pad_ends = jnp.cumsum(padded)
    pad_starts = pad_ends - padded
    dest = pad_starts[e_sorted] + (jnp.arange(a) - starts[e_sorted])
    p_total = (-(-a // g) + e_count) * g
    tok_buf = jnp.full((p_total,), n, jnp.int32).at[dest].set(t_flat[order])
    w_buf = jnp.zeros((p_total,), jnp.float32).at[dest].set(w_flat[order])
    nblk = p_total // g
    blk_e = jnp.minimum(jnp.searchsorted(pad_ends, jnp.arange(nblk) * g, side='right'), e_count - 1)
    x_pad = jnp.concatenate([xf, jnp.zeros((1, d), xf.dtype)], axis=0)
    xb = x_pad[tok_buf].reshape(nblk, g, d)

    def expert_block(args):
        xg, e = args
        return swiglu(xg, w_gate[e], w_up[e], w_down[e])

    yb = lax.map(expert_block, (xb, blk_e)).reshape(p_total, d)
    yb = yb * w_buf[:, None].astype(yb.dtype)
    y = jax.ops.segment_sum(yb, tok_buf, num_segments=n + 1)[:n]
    return y.reshape(b, s, d)

def first_inputs(seed: int = 0) -> dict:
    key = jax.random.key(seed)
    ks = jax.random.split(key, 20)
    n_dense = (DEPTH + 1) // 2
    n_moe = DEPTH // 2
    D = D_MODEL

    def nrm(k, shape, scale):
        return jax.random.normal(k, shape, jnp.float32) * scale

    return {
        "x": nrm(ks[0], (BATCH, SEQ, D), 1.0),
        "c": nrm(ks[1], (BATCH, D), 1.0),
        "norm_mix_g": 1.0 + nrm(ks[2], (DEPTH, D), 0.05),
        "norm_ffn_g": 1.0 + nrm(ks[3], (DEPTH, D), 0.05),
        "ada_w": nrm(ks[4], (DEPTH, D, 6 * D), 0.5 * D ** -0.5),
        "ada_b": nrm(ks[5], (DEPTH, 6 * D), 0.02),
        "w_in": nrm(ks[6], (DEPTH, D, IN_PROJ_WIDTH), D ** -0.5),
        "w_out": nrm(ks[7], (DEPTH, ATT_WIDTH + RET_WIDTH, D), (ATT_WIDTH + RET_WIDTH) ** -0.5),
        "att_out_g": 1.0 + nrm(ks[8], (DEPTH, ATT_WIDTH), 0.05),
        "ret_out_g": 1.0 + nrm(ks[9], (DEPTH, RET_WIDTH), 0.05),
        "ffn_w_gate": nrm(ks[10], (n_dense, D, D_FF), D ** -0.5),
        "ffn_w_up": nrm(ks[11], (n_dense, D, D_FF), D ** -0.5),
        "ffn_w_down": nrm(ks[12], (n_dense, D_FF, D), D_FF ** -0.5),
        "router_w": nrm(ks[13], (n_moe, D, N_EXPERTS), D ** -0.5),
        "moe_w_gate": nrm(ks[14], (n_moe, N_EXPERTS, D, EXPERT_D_FF), D ** -0.5),
        "moe_w_up": nrm(ks[15], (n_moe, N_EXPERTS, D, EXPERT_D_FF), D ** -0.5),
        "moe_w_down": nrm(ks[16], (n_moe, N_EXPERTS, EXPERT_D_FF, D), EXPERT_D_FF ** -0.5),
        "final_norm_g": 1.0 + nrm(ks[17], (D,), 0.05),
    }

def first_block(x, c, norm_mix_g, norm_ffn_g, ada_w, ada_b, w_in, w_out, att_out_g, ret_out_g,
              ffn_w_gate, ffn_w_up, ffn_w_down, router_w, moe_w_gate, moe_w_up, moe_w_down,
              final_norm_g):
    cs = jax.nn.silu(c)
    for l in range(DEPTH):
        mod = cs @ ada_w[l] + ada_b[l]
        sh1, sc1, g1, sh2, sc2, g2 = jnp.split(mod, 6, axis=-1)
        h = rms_norm(x, norm_mix_g[l]) * (1.0 + sc1[:, None]) + sh1[:, None]
        x = x + g1[:, None] * hybrid_mixer(h, w_in[l], w_out[l], att_out_g[l], ret_out_g[l])
        h = rms_norm(x, norm_ffn_g[l]) * (1.0 + sc2[:, None]) + sh2[:, None]
        if l % 2 == 0:
            f = swiglu(h, ffn_w_gate[l // 2], ffn_w_up[l // 2], ffn_w_down[l // 2])
        else:
            f = moe_ffn(h, router_w[l // 2], moe_w_gate[l // 2], moe_w_up[l // 2], moe_w_down[l // 2])
        x = x + g2[:, None] * f
    return rms_norm(x, final_norm_g)


HEAD_DIM = 64
BLOCK_Q = 128
ROPE_THETA = 10000.0
GRID_W = 64
N_EVEN = (DEPTH + 1) // 2
N_ODD = DEPTH // 2
GMLP_GROUPS = 8
GMLP_GROUP_DIM = 64
GMLP_CHUNK = 128
GMLP_WIDTH = GMLP_GROUPS * GMLP_GROUP_DIM
DIFF_HEADS = 4
DIFF_D = 64
DIFF_V = 2 * DIFF_D
MLA_HEADS = 8
MLA_Q_RANK = 256
MLA_KV_RANK = 128
MLA_NOPE = 64
MLA_ROPE = 32
MLA_V = 64
GQA_Q_HEADS = 8
GQA_KV_HEADS = 2
GQA_GROUP = GQA_Q_HEADS // GQA_KV_HEADS
GQA_DIM = 64

EVEN_IN = 2 * GMLP_WIDTH + 2 * DIFF_HEADS * 2 * DIFF_D + DIFF_HEADS * DIFF_V
EVEN_OUT = GMLP_WIDTH + DIFF_HEADS * DIFF_V
ODD_IN = (MLA_Q_RANK + MLA_KV_RANK + MLA_ROPE
          + GQA_Q_HEADS * GQA_DIM + 2 * GQA_KV_HEADS * GQA_DIM)
ODD_OUT = MLA_HEADS * MLA_V + GQA_Q_HEADS * GQA_DIM


def rmsnorm(x, g):
    xf = x.astype(jnp.float32)
    y = xf * lax.rsqrt(jnp.mean(xf * xf, axis=-1, keepdims=True) + EPS)
    return (y * g.astype(jnp.float32)).astype(x.dtype)

def rope_angles(pos, dim):
    inv = ROPE_THETA ** (-jnp.arange(0, dim, 2, dtype=jnp.float32) / dim)
    ang = pos.astype(jnp.float32)[:, None] * inv[None, :]
    return jnp.cos(ang), jnp.sin(ang)

def apply_rope(x, cos, sin):
    shape = (cos.shape[0],) + (1,) * (x.ndim - 3) + (cos.shape[-1],)
    c = cos.reshape(shape)
    s = sin.reshape(shape)
    xf = x.astype(jnp.float32)
    x1, x2 = jnp.split(xf, 2, axis=-1)
    return jnp.concatenate([x1 * c - x2 * s, x1 * s + x2 * c], axis=-1).astype(x.dtype)

def axial_rope(x, row_cs, col_cs):
    half = x.shape[-1] // 2
    return jnp.concatenate([apply_rope(x[..., :half], *row_cs),
                            apply_rope(x[..., half:], *col_cs)], axis=-1)

def to_blocks(t):
    b, s = t.shape[:2]
    t = t.reshape((b, s // BLOCK_Q, BLOCK_Q) + t.shape[2:])
    return jnp.moveaxis(t, 1, 0)

def from_blocks(t):
    t = jnp.moveaxis(t, 0, 1)
    return t.reshape((t.shape[0], t.shape[1] * t.shape[2]) + t.shape[3:])

def gqa_attention(q, k, v):
    scale = q.shape[-1] ** -0.5

    def blk(qb):
        s = jnp.einsum('bqhgd,bshd->bhgqs', qb, k).astype(jnp.float32) * scale
        p = jax.nn.softmax(s, axis=-1).astype(v.dtype)
        return jnp.einsum('bhgqs,bshe->bqhge', p, v)

    return from_blocks(lax.map(blk, to_blocks(q)))

def swiglu_2(h, w_gu, w_down):
    g, u = jnp.split(h @ w_gu, 2, axis=-1)
    return (jax.nn.silu(g) * u) @ w_down

def mixer_gmlp(u, v, sgu_norm, w_s, b_s):
    b, s, _ = v.shape
    vc = v.reshape(b, s // GMLP_CHUNK, GMLP_CHUNK, GMLP_GROUPS, GMLP_GROUP_DIM)
    vc = rmsnorm(vc, sgu_norm)
    mixed = jnp.einsum('gij,bcjgd->bcigd', w_s, vc) + b_s.T[:, :, None]
    return u * mixed.reshape(b, s, GMLP_WIDTH)

def mixer_diff(q, k, v, q_norm, k_norm, lam_q1, lam_k1, lam_q2, lam_k2,
               sub_norm, lam_init, cos, sin):
    b, s = q.shape[:2]
    q = apply_rope(rmsnorm(q, q_norm), cos, sin)
    k = apply_rope(rmsnorm(k, k_norm), cos, sin)
    f32 = jnp.float32
    lam = (jnp.exp(jnp.sum(lam_q1.astype(f32) * lam_k1.astype(f32)))
           - jnp.exp(jnp.sum(lam_q2.astype(f32) * lam_k2.astype(f32))) + lam_init)
    scale = DIFF_D ** -0.5

    def blk(qb):
        sc = jnp.einsum('bqhmd,bshmd->bhmqs', qb, k).astype(f32) * scale
        p = jax.nn.softmax(sc, axis=-1)
        w = (p[:, :, 0] - lam * p[:, :, 1]).astype(v.dtype)
        return jnp.einsum('bhqs,bshe->bqhe', w, v)

    o = from_blocks(lax.map(blk, to_blocks(q)))
    o = rmsnorm(o, sub_norm) * (1.0 - lam_init)
    return o.reshape(b, s, DIFF_HEADS * DIFF_V)

def second_inputs(seed: int = 0) -> dict:
    key = jax.random.key(seed)
    ks = iter(jax.random.split(key, 40))
    f32 = jnp.float32

    def w(shape, fan_in):
        return jax.random.normal(next(ks), shape, f32) * (fan_in ** -0.5)

    def gain(shape):
        return 1.0 + 0.02 * jax.random.normal(next(ks), shape, f32)

    def small(shape, scale):
        return scale * jax.random.normal(next(ks), shape, f32)

    d = D_MODEL
    return {
        "x": jax.random.normal(next(ks), (BATCH, SEQ, d), f32),
        "ffn1_norm": gain((DEPTH, d)),
        "ffn1_w_gu": w((DEPTH, d, 2 * D_FF), d),
        "ffn1_w_down": w((DEPTH, D_FF, d), D_FF),
        "ffn2_norm": gain((DEPTH, d)),
        "ffn2_w_gu": w((DEPTH, d, 2 * D_FF), d),
        "ffn2_w_down": w((DEPTH, D_FF, d), D_FF),
        "ev_norm": gain((N_EVEN, d)),
        "ev_w_in": w((N_EVEN, d, EVEN_IN), d),
        "ev_sgu_norm": gain((N_EVEN, GMLP_GROUPS, GMLP_GROUP_DIM)),
        "ev_w_s": w((N_EVEN, GMLP_GROUPS, GMLP_CHUNK, GMLP_CHUNK), GMLP_CHUNK),
        "ev_b_s": gain((N_EVEN, GMLP_GROUPS, GMLP_CHUNK)),
        "ev_q_norm": gain((N_EVEN, DIFF_D)),
        "ev_k_norm": gain((N_EVEN, DIFF_D)),
        "ev_lam_q1": small((N_EVEN, DIFF_D), 0.1),
        "ev_lam_k1": small((N_EVEN, DIFF_D), 0.1),
        "ev_lam_q2": small((N_EVEN, DIFF_D), 0.1),
        "ev_lam_k2": small((N_EVEN, DIFF_D), 0.1),
        "ev_sub_norm": gain((N_EVEN, DIFF_V)),
        "ev_w_out": w((N_EVEN, EVEN_OUT, d), EVEN_OUT),
        "od_norm": gain((N_ODD, d)),
        "od_w_in": w((N_ODD, d, ODD_IN), d),
        "od_cq_norm": gain((N_ODD, MLA_Q_RANK)),
        "od_ckv_norm": gain((N_ODD, MLA_KV_RANK)),
        "od_w_uq": w((N_ODD, MLA_Q_RANK, MLA_HEADS * (MLA_NOPE + MLA_ROPE)), MLA_Q_RANK),
        "od_w_ukv": w((N_ODD, MLA_KV_RANK, MLA_HEADS * (MLA_NOPE + MLA_V)), MLA_KV_RANK),
        "od_mla_q_norm": gain((N_ODD, MLA_NOPE + MLA_ROPE)),
        "od_mla_k_norm": gain((N_ODD, MLA_NOPE + MLA_ROPE)),
        "od_gqa_q_norm": gain((N_ODD, GQA_DIM)),
        "od_gqa_k_norm": gain((N_ODD, GQA_DIM)),
        "od_w_out": w((N_ODD, ODD_OUT, d), ODD_OUT),
    }

def second_block(x, ffn1_norm, ffn1_w_gu, ffn1_w_down, ffn2_norm, ffn2_w_gu, ffn2_w_down,
              ev_norm, ev_w_in, ev_sgu_norm, ev_w_s, ev_b_s, ev_q_norm, ev_k_norm,
              ev_lam_q1, ev_lam_k1, ev_lam_q2, ev_lam_k2, ev_sub_norm, ev_w_out,
              od_norm, od_w_in, od_cq_norm, od_ckv_norm, od_w_uq, od_w_ukv,
              od_mla_q_norm, od_mla_k_norm, od_gqa_q_norm, od_gqa_k_norm, od_w_out):
    b, s, _ = x.shape
    rows = s // GRID_W
    pos = jnp.arange(s, dtype=jnp.int32)
    row_idx = jnp.repeat(jnp.arange(rows, dtype=jnp.int32), GRID_W)
    col_idx = jnp.tile(jnp.arange(GRID_W, dtype=jnp.int32), rows)
    cs_full = rope_angles(pos, DIFF_D)
    cs_mla = rope_angles(pos, MLA_ROPE)
    cs_row = rope_angles(row_idx, GQA_DIM // 2)
    cs_col = rope_angles(col_idx, GQA_DIM // 2)

    for l in range(DEPTH):
        x = x + 0.5 * swiglu_2(rmsnorm(x, ffn1_norm[l]), ffn1_w_gu[l], ffn1_w_down[l])
        if l % 2 == 0:
            i = l // 2
            proj = rmsnorm(x, ev_norm[i]) @ ev_w_in[i]
            a_uv, bq, bk, bv = jnp.split(
                proj, [2 * GMLP_WIDTH, 2 * GMLP_WIDTH + 2 * DIFF_HEADS * DIFF_D,
                       2 * GMLP_WIDTH + 4 * DIFF_HEADS * DIFF_D], axis=-1)
            u, v = jnp.split(jax.nn.gelu(a_uv), 2, axis=-1)
            out_a = mixer_gmlp(u, v, ev_sgu_norm[i], ev_w_s[i], ev_b_s[i])
            lam_init = 0.8 - 0.6 * float(np.exp(-0.3 * l))
            out_b = mixer_diff(
                bq.reshape(b, s, DIFF_HEADS, 2, DIFF_D),
                bk.reshape(b, s, DIFF_HEADS, 2, DIFF_D),
                bv.reshape(b, s, DIFF_HEADS, DIFF_V),
                ev_q_norm[i], ev_k_norm[i], ev_lam_q1[i], ev_lam_k1[i],
                ev_lam_q2[i], ev_lam_k2[i], ev_sub_norm[i], lam_init, *cs_full)
            mix = jnp.concatenate([out_a, out_b], axis=-1) @ ev_w_out[i]
        else:
            i = l // 2
            proj = rmsnorm(x, od_norm[i]) @ od_w_in[i]
            o1 = MLA_Q_RANK
            o2 = o1 + MLA_KV_RANK
            o3 = o2 + MLA_ROPE
            o4 = o3 + GQA_Q_HEADS * GQA_DIM
            o5 = o4 + GQA_KV_HEADS * GQA_DIM
            c_q, c_kv, k_pe, gq, gk, gv = jnp.split(proj, [o1, o2, o3, o4, o5], axis=-1)
            q = (rmsnorm(c_q, od_cq_norm[i]) @ od_w_uq[i]).reshape(
                b, s, MLA_HEADS, MLA_NOPE + MLA_ROPE)
            kv = (rmsnorm(c_kv, od_ckv_norm[i]) @ od_w_ukv[i]).reshape(
                b, s, MLA_HEADS, MLA_NOPE + MLA_V)
            k_nope, v_c = jnp.split(kv, [MLA_NOPE], axis=-1)
            k = jnp.concatenate(
                [k_nope, jnp.broadcast_to(k_pe[:, :, None, :], (b, s, MLA_HEADS, MLA_ROPE))],
                axis=-1)
            q = rmsnorm(q, od_mla_q_norm[i])
            k = rmsnorm(k, od_mla_k_norm[i])
            q = jnp.concatenate([q[..., :MLA_NOPE], apply_rope(q[..., MLA_NOPE:], *cs_mla)], axis=-1)
            k = jnp.concatenate([k[..., :MLA_NOPE], apply_rope(k[..., MLA_NOPE:], *cs_mla)], axis=-1)
            out_c = gqa_attention(q[:, :, :, None, :], k, v_c).reshape(b, s, MLA_HEADS * MLA_V)
            qd = rmsnorm(gq.reshape(b, s, GQA_KV_HEADS, GQA_GROUP, GQA_DIM), od_gqa_q_norm[i])
            kd = rmsnorm(gk.reshape(b, s, GQA_KV_HEADS, GQA_DIM), od_gqa_k_norm[i])
            vd = gv.reshape(b, s, GQA_KV_HEADS, GQA_DIM)
            qd = axial_rope(qd, cs_row, cs_col)
            kd = axial_rope(kd, cs_row, cs_col)
            out_d = gqa_attention(qd, kd, vd).reshape(b, s, GQA_Q_HEADS * GQA_DIM)
            mix = jnp.concatenate([out_c, out_d], axis=-1) @ od_w_out[i]
        x = x + mix
        x = x + 0.5 * swiglu_2(rmsnorm(x, ffn2_norm[l]), ffn2_w_gu[l], ffn2_w_down[l])
    return x


def setup_inputs(seed=0):
    out = dict(first_inputs(seed))
    for name, value in second_inputs(seed + 1).items():
        if name != "x":
            out[name + "_2"] = value
    return out


def reference(
    x, c, norm_mix_g, norm_ffn_g, ada_w, ada_b, w_in, w_out, att_out_g, ret_out_g, ffn_w_gate,
    ffn_w_up, ffn_w_down, router_w, moe_w_gate, moe_w_up, moe_w_down, final_norm_g, ffn1_norm_2,
    ffn1_w_gu_2, ffn1_w_down_2, ffn2_norm_2, ffn2_w_gu_2, ffn2_w_down_2, ev_norm_2, ev_w_in_2,
    ev_sgu_norm_2, ev_w_s_2, ev_b_s_2, ev_q_norm_2, ev_k_norm_2, ev_lam_q1_2, ev_lam_k1_2,
    ev_lam_q2_2, ev_lam_k2_2, ev_sub_norm_2, ev_w_out_2, od_norm_2, od_w_in_2, od_cq_norm_2,
    od_ckv_norm_2, od_w_uq_2, od_w_ukv_2, od_mla_q_norm_2, od_mla_k_norm_2, od_gqa_q_norm_2,
    od_gqa_k_norm_2, od_w_out_2,
):
    x = first_block(
        x, c, norm_mix_g, norm_ffn_g, ada_w, ada_b, w_in, w_out, att_out_g, ret_out_g,
        ffn_w_gate, ffn_w_up, ffn_w_down, router_w, moe_w_gate, moe_w_up, moe_w_down,
        final_norm_g,
    )
    return second_block(
        x, ffn1_norm_2, ffn1_w_gu_2, ffn1_w_down_2, ffn2_norm_2, ffn2_w_gu_2, ffn2_w_down_2,
        ev_norm_2, ev_w_in_2, ev_sgu_norm_2, ev_w_s_2, ev_b_s_2, ev_q_norm_2, ev_k_norm_2,
        ev_lam_q1_2, ev_lam_k1_2, ev_lam_q2_2, ev_lam_k2_2, ev_sub_norm_2, ev_w_out_2,
        od_norm_2, od_w_in_2, od_cq_norm_2, od_ckv_norm_2, od_w_uq_2, od_w_ukv_2,
        od_mla_q_norm_2, od_mla_k_norm_2, od_gqa_q_norm_2, od_gqa_k_norm_2, od_w_out_2,
    )


_drawn_inputs = setup_inputs


def setup_inputs(seed=0):
    import zlib

    import numpy as np

    out = dict(_drawn_inputs(seed))
    spreads = {}
    factors = {'ret_out_g': 3.069,
     'ffn1_norm_2': 5.212,
     'ffn2_norm_2': 6.627,
     'ev_norm_2': 3.275,
     'ev_sgu_norm_2': 8.0,
     'ev_b_s_2': 7.55,
     'ev_q_norm_2': 8.0,
     'ev_k_norm_2': 8.0,
     'ev_lam_q1_2': 57.346,
     'ev_lam_k1_2': 56.753,
     'ev_lam_q2_2': 8.0,
     'ev_lam_k2_2': 5.119,
     'ev_sub_norm_2': 23.388,
     'od_norm_2': 8.0,
     'od_cq_norm_2': 8.0,
     'od_ckv_norm_2': 8.0,
     'od_mla_q_norm_2': 8.0,
     'od_mla_k_norm_2': 8.0,
     'od_gqa_q_norm_2': 8.0,
     'od_gqa_k_norm_2': 8.0}
    for name, (base, spread) in spreads.items():
        noise = np.random.default_rng([zlib.crc32(name.encode()), seed]).standard_normal(out[name].shape)
        drawn = base * np.exp(spread * noise) if base else spread * noise
        out[name] = __import__('jax').numpy.asarray(drawn.astype(out[name].dtype))
    for name, factor in factors.items():
        out[name] = (out[name] * factor).astype(out[name].dtype)
    return out
```

```python
import numpy as np
import concourse.bass as bass
import concourse.mybir as mybir
from concourse.alu_op_type import AluOpType as ALU

F32 = mybir.dt.float32
F32R = mybir.dt.float32r
BF16 = mybir.dt.bfloat16
U32 = mybir.dt.uint32
ACTF = mybir.ActivationFunctionType
AX = mybir.AxisListType
ds = bass.ds

P = 128
S = 256
NT = S // P
D = 1024
KD = D // P
FF = 2816
STEP_F = 256
STEPS = FF // STEP_F
NE = 8
SLAB = 512
RAW, SPL = 12, 6
UNITS_GU, UNITS_D = 4, 2
FFN_UNITS = STEPS * (UNITS_GU + UNITS_D)
EPS = 1e-6

TABLES = {"ident": P, "causal": NT * S, "decay": 4 * S, "ret_cos": NT * 64, "ret_sin": NT * 64,
          "diff_cos": NT * 32, "diff_sin": NT * 32, "mla_cos": NT * 16, "mla_sin": NT * 16,
          "gqa_cos": NT * 32, "gqa_sin": NT * 32, "iota8": NE}
COLUMNS = [("norm_mix_g", 16), ("norm_ffn_g", 16), ("ffn1_norm_2", 16), ("ffn2_norm_2", 16),
           ("ev_norm_2", 8), ("od_norm_2", 8), ("c", 8), ("att_out_g", 8), ("ret_out_g", 8),
           ("ev_b_s_2", 8), ("ev_sub_norm_2", 1), ("od_cq_norm_2", 2), ("od_ckv_norm_2", 1)]
ROWS = [("ev_q_norm_2", 64), ("ev_k_norm_2", 64), ("ev_sgu_norm_2", 512), ("od_mla_q_norm_2", 96),
        ("od_mla_k_norm_2", 96), ("od_gqa_q_norm_2", 64), ("od_gqa_k_norm_2", 64),
        ("ev_lam_q1_2", 64), ("ev_lam_k1_2", 64), ("ev_lam_q2_2", 64), ("ev_lam_k2_2", 64)]


class Engine:

    def __init__(self, nc, queue, name):
        self.q, self.sem, self.count, self.seen = queue, nc.alloc_semaphore(name), 0, {}

    def need(self, *marks):
        for sem, value in marks:
            if self.seen.get(sem.name, 0) < value:
                self.q.wait_ge(sem, value)
                self.seen[sem.name] = value

    def did(self, ins):
        ins.then_inc(self.sem, 1)
        self.count += 1
        return (self.sem, self.count)

    def run(self, marks, op, *args, **kw):
        self.need(*marks)
        return self.did(op(*args, **kw))


def program(nc, io, out, upto=13):
    sp, act, pe, dve = nc.sync, nc.scalar, nc.tensor, nc.vector
    SP, ACT, PE, DVE = (Engine(nc, q, n) for q, n in
                        ((sp, "sp_count"), (act, "act_count"), (pe, "pe_count"), (dve, "dve_count")))
    compute = (mybir.EngineType.Activation, mybir.EngineType.PE, mybir.EngineType.DVE)

    def sb(name, shape, dt=F32):
        return nc.alloc_sbuf_tensor(name, shape, dt)

    def over(name, shape, base, skip=0, dt=F32):
        return nc.alloc_sbuf_tensor_at(name, shape, dt, offset=base + skip)

    def sem(name):
        return nc.alloc_semaphore(name)

    raw = [sb(f"raw{i}", [P, 1024]) for i in range(RAW)]
    hi = [sb(f"hi{i}", [P, 1024], F32R) for i in range(SPL)]
    lo = [sb(f"lo{i}", [P, 1024], F32R) for i in range(SPL)]
    x = sb("x_res", [P, NT, D])
    gates = sb("gates", [P, 2, D])
    at_gates = nc.sbuf_base - 8192
    xn = sb("xn", [P, NT, D])
    at_xn = nc.sbuf_base - 8192
    aT = [sb("aT_hi", [P, KD, S], F32R), sb("aT_lo", [P, KD, S], F32R)]
    at = nc.sbuf_base
    proj = sb("proj", [P, NT, 3584])
    at_proj = at
    at = nc.sbuf_base
    qkT = sb("qkT", [P, 16, S])
    at_qkT = at
    at = nc.sbuf_base
    probs = sb("probs", [P, 2, NT * S])
    at_probs = at
    probsT = sb("probsT", [P, 2, NT * S])
    tables = sb("tables_sb", [P, sum(TABLES.values())])
    cols = sb("cols_sb", [P, P])
    rows = sb("rows", [P, sum(n for _, n in ROWS)])
    small = sb("small", [P, 256])
    gain_cols = sb("gain_cols", [P, 16])
    mod_cols = sb("mod_cols", [P, 32])
    zeros = sb("zeros", [1, SLAB], BF16)
    ones = sb("ones", [1, P])
    mod_rows = over("mod_rows", [P, 6 * D], at_proj)
    cs_wide = over("cs_wide", [P, KD, P], at_proj, 24 * 1024)
    silu_g = over("silu_g", [P, NT, STEP_F], at_proj)
    hid = over("hid", [P, NT, STEP_F], at_proj, 2048)
    hidT = [over("hidT_hi", [P, 2 * S], at_proj, 4096, F32R), over("hidT_lo", [P, 2 * S], at_proj, 6144, F32R)]
    cT = [over("cT_hi", [P, KD, P], at_qkT, 0, F32R), over("cT_lo", [P, KD, P], at_qkT, 4096, F32R)]
    vec_rows = over("vec_rows", [P, P], at_proj)
    bias_row = over("bias_row", [1, 2 * D], at_qkT, 8192)
    bias_ss2 = over("bias_ss2", [1, 2 * D], at_probs)
    rope_tmp = over("rope_tmp", [P, 2048], at_probs)
    k_full = over("k_full", [P, NT, 768], at_gates)
    probs_d = over("probs_d", [P, 4, NT * S], at_gates)
    gq_pairs = over("gq_pairs", [P, NT, 4, P], at_gates)
    expert_w = sb("expert_w", [P, 2 * NE])
    top_idx = sb("top_idx", [P, 8], U32)
    bias_g1 = over("bias_g1", [1, D], at_xn + 8192)
    bias_g2 = over("bias_g2", [1, D], at_xn)
    router = over("router_sb", [P, KD, NE], at_probs)
    hT_full = over("hT_full", [P, KD, S], at_qkT)
    w_s = over("w_s", [P, 8, P], at_probs)
    w_sT = over("w_sT", [P, 8, P], at_probs, 4096)
    final_g = over("final_g", [P, D], at_probs)
    psum = [nc.alloc_psum_tensor(f"bank{i}", [P, 512], F32) for i in range(8)]

    col_at, n = {}, 0
    for name, k in COLUMNS:
        col_at[name] = n
        n += k
    n_cols = n
    row_at, n = {}, 0
    for name, k in ROWS:
        row_at[name] = n
        n += k
    tab_at, n = {}, 0
    for name, k in TABLES.items():
        tab_at[name] = n
        n += k

    def table(name):
        return tables[:, tab_at[name]:tab_at[name] + TABLES[name]]

    def col(name, k):
        return cols[:, col_at[name] + k:col_at[name] + k + 1]

    def row(name):
        return rows[:, row_at[name]:row_at[name] + dict(ROWS)[name]]

    ident = table("ident")

    small_used = [0]

    def tiny(n):
        if small_used[0] + n > 256:
            small_used[0] = 0
        a = small[:, small_used[0]:small_used[0] + n]
        small_used[0] += n
        return a

    raw_full = [sem(f"raw_full{i}") for i in range(RAW)]
    hi_done, lo_done, unit_free = sem("hi_done"), sem("lo_done"), sem("unit_free")
    stage_units = [48, 36, FFN_UNITS, 48, 36, NE * FFN_UNITS, 0, FFN_UNITS, 28, FFN_UNITS, FFN_UNITS, 23, FFN_UNITS]
    total = sum(stage_units[:upto])
    st = {"load": 0, "split": 0, "use": 0, "lap": 0, "sp_lap": 0}

    def load(*parts):
        u, lap = st["load"], st["sp_lap"]
        st["load"] += 1
        slot = u % RAW
        if u >= RAW:
            sp.wait_ge(lo_done, u - RAW + 1 + 12 * lap)
        for dst, src in parts:
            sp.dma_start(dst(raw[slot]), src).then_inc(raw_full[slot], 32 // len(parts))

    def split_one():
        u, lap = st["split"], st["lap"]
        st["split"] += 1
        act.wait_ge(raw_full[u % RAW], 32 * (u // RAW + 1) + 32 * lap)
        if u >= SPL:
            act.wait_ge(unit_free, u - SPL + 1 + 12 * lap)
        act.activation(hi[u % SPL][:, :], raw[u % RAW][:, :], ACTF.Copy).then_inc(hi_done, 1)
        dve.wait_ge(hi_done, u + 1 + 12 * lap)
        dve.tensor_tensor(lo[u % SPL][:, :], raw[u % RAW][:, :], hi[u % SPL][:, :].bitcast(F32),
                          ALU.subtract).then_inc(lo_done, 1)

    def split_to(n):
        while st["split"] < min(n, total):
            split_one()

    def unit(u, k=2, width=512):
        return [s[u % SPL][:, 0:k * width].rearrange("p (k n) -> p k n", k=k) for s in (hi, lo)]

    def passes(bank, left, right, first, last):
        for n, (a, b) in enumerate(((0, 0), (0, 1), (1, 0))):
            ins = pe.matmul(bank, left[a], right[b], start=first and n == 0, stop=last and n == 2)
        return ins

    def proj_load(w, c0, width, kd=KD):
        v = w[:, c0:c0 + width].rearrange("(k p) n -> p k n", p=P)
        for k in range(0, kd, 2):
            load((lambda r: r[:, :].rearrange("p (k n) -> p k n", k=2)[:, :, 0:width], v[:, k:k + 2, :]))

    bank_mark = [()] * 8

    def slab(width, evacuate, marks=(), kd=KD):
        u = st["use"]
        n_units = kd // 2
        split_to(u + n_units)
        for t in range(NT):
            PE.need(*bank_mark[t])
            for j in range(n_units):
                if t == 0:
                    pe.wait_ge(lo_done, u + j + 1)
                w = unit(u + j)
                for kk in range(2):
                    k = 2 * j + kk
                    if t == 0 and marks:
                        PE.need(marks[k])
                    ins = passes(psum[t][:, 0:width], [a[:, k, t * P:(t + 1) * P] for a in aT],
                                 [r[:, kk, 0:width] for r in w], k == 0, k == kd - 1)
                if t == NT - 1:
                    ins.then_inc(unit_free, 1)
            if t == 0:
                mark0 = PE.did(ins)
                bank_mark[0] = evacuate(0, psum[0][:, 0:width], mark0)
                st["use"] += n_units
                split_to(u + n_units + 4)
        bank_mark[1] = evacuate(1, psum[1][:, 0:width], (unit_free, u + n_units))

    gu_done, silu_done, hid_done = sem("gu_done"), sem("silu_done"), sem("hid_done")
    turned, hidT_hi_done, hidT_lo_done = sem("turned"), sem("hidT_hi_done"), sem("hidT_lo_done")
    ffn = {"g": 0}

    def pe_gate_up(t, u, g, lap, marks=()):
        if g > 0:
            pe.wait_ge(hid_done, 2 * (g - 1) + t + 1 + 4 * lap)
        for j in range(UNITS_GU):
            if t == 0:
                pe.wait_ge(lo_done, u + j + 1 + 12 * lap)
            w = unit(u + j)
            for kk in range(2):
                k = 2 * j + kk
                if marks:
                    PE.need(marks[k])
                ins = passes(psum[t][:, :], [a[:, k, t * P:(t + 1) * P] for a in aT],
                             [r[:, kk, :] for r in w], k == 0, k == KD - 1)
            if t == 1:
                ins.then_inc(unit_free, 1)
        if t == 0:
            ins.then_inc(gu_done, 1)

    def silu_mul(t, u_end, g, lap, weight):
        if t == 0:
            act.wait_ge(gu_done, g + 1 + 2 * lap)
        else:
            act.wait_ge(unit_free, u_end + 12 * lap)
        if g > 0:
            act.wait_ge(hid_done, 2 * (g - 1) + t + 1 + 4 * lap)
        act.activation(silu_g[:, t, :], psum[t][:, 0:STEP_F], ACTF.Silu).then_inc(silu_done, 1)
        dve.wait_ge(silu_done, 2 * g + t + 1 + 4 * lap)
        if g > 0:
            dve.wait_ge(turned, g + 2 * lap)
        up = psum[t][:, STEP_F:2 * STEP_F]
        if weight is None:
            ins = dve.tensor_tensor(hid[:, t, :], silu_g[:, t, :], up, ALU.mult)
        else:
            ins = dve.scalar_tensor_tensor(out=hid[:, t, :], in0=silu_g[:, t, :], scalar=weight(t),
                                           in1=up, op0=ALU.mult, op1=ALU.mult)
        ins.then_inc(hid_done, 1)

    def pe_turn(g, lap):
        pe.wait_ge(hid_done, 2 * g + 2 + 4 * lap)
        if g > 0:
            pe.wait_ge(hidT_lo_done, g + 2 * lap)
        for f in range(2):
            for t in range(NT):
                ins = pe.transpose(psum[2][:, f * S + t * P:f * S + (t + 1) * P],
                                   hid[:, t, f * P:(f + 1) * P], ident)
        ins.then_inc(turned, 1)

    def hidT_split(u_before, g, lap):
        act.wait_ge(turned, g + 1 + 2 * lap)
        act.wait_ge(unit_free, u_before + 12 * lap)
        act.activation(hidT[0][:, :], psum[2][:, :], ACTF.Copy).then_inc(hidT_hi_done, 1)
        dve.wait_ge(hidT_hi_done, g + 1 + 2 * lap)
        dve.tensor_tensor(hidT[1][:, :], psum[2][:, :], hidT[0][:, :].bitcast(F32),
                          ALU.subtract).then_inc(hidT_lo_done, 1)

    def pe_down(u, g, lap, last=False):
        pe.wait_ge(hidT_lo_done, g + 1 + 2 * lap)
        for f in range(2):
            pe.wait_ge(lo_done, u + f + 1 + 12 * lap)
            w = [s[(u + f) % SPL] for s in (hi, lo)]
            for t in range(NT):
                for half in range(2):
                    ins = passes(psum[4 + 2 * t + half][:, :],
                                 [a[:, f * S + t * P:f * S + (t + 1) * P] for a in hidT],
                                 [r[:, half * SLAB:(half + 1) * SLAB] for r in w], False,
                                 last and f == 1)
            ins.then_inc(unit_free, 1)

    def ffn_load(gate, up, down):
        def gu(c):
            for k in range(UNITS_GU):
                load((lambda r: r[:, :].rearrange("p (k n) -> p k n", k=2)[:, :, 0:STEP_F], gate(c, 2 * k)),
                     (lambda r: r[:, :].rearrange("p (k n) -> p k n", k=2)[:, :, STEP_F:], up(c, 2 * k)))

        def dn(c):
            for f in range(2):
                load((lambda r: r[:, :], down(c, f)))

        gu(0)
        base, lap = st["load"], st["sp_lap"]
        with sp.Fori(0, (STEPS - 1) // 2) as i:
            st["sp_lap"] = lap + i
            for b in range(2):
                gu(2 * i + b + 1)
                dn(2 * i + b)
        st["load"], st["sp_lap"] = base + 12 * ((STEPS - 1) // 2), lap
        dn(STEPS - 1)

    def zero_y(marks):
        PE.need(*marks)
        for b in range(4, 8):
            pe.matmul(psum[b][:, :], zeros[:, 0:P], zeros[:, :], start=True, stop=False)

    def close_y():
        for b in range(4, 8):
            ins = pe.matmul(psum[b][:, :], zeros[:, 0:P], zeros[:, :], start=False, stop=True)
        return PE.did(ins)

    def ffn_steps(marks=(), weight=None, final=False):
        g0, u0, lap = ffn["g"], st["use"], st["lap"]
        rounds = (STEPS - 1) // 2
        looped = rounds - 1 if final else rounds

        def look_ahead(n):
            for _ in range(n):
                if st["split"] < total:
                    split_one()

        def step(g, u, lap):
            pe_gate_up(0, u, g, lap)
            silu_mul(1, u, g - 1, lap, weight)
            look_ahead(UNITS_D)
            pe_turn(g - 1, lap)
            hidT_split(u, g - 1, lap)
            pe_gate_up(1, u, g, lap)
            silu_mul(0, None, g, lap, weight)
            look_ahead(UNITS_GU)
            pe_down(u + UNITS_GU, g - 1, lap)

        def round_of(g, u, lap):
            for b in range(2):
                step(g + b, u + b * (UNITS_GU + UNITS_D), lap)

        pe_gate_up(0, u0, g0, lap, marks)
        silu_mul(0, None, g0, lap, weight)
        pe_gate_up(1, u0, g0, lap)
        look_ahead(UNITS_GU)
        g, u, split = g0 + 1, u0 + UNITS_GU, st["split"]
        with nc.Fori(0, looped, engines=compute) as i:
            st["lap"] = lap + i
            round_of(g, u, lap + i)
        st["lap"], st["split"] = lap, split + RAW * looped
        g, u = g + 2 * looped, u + RAW * looped
        if final:
            round_of(g, u, lap)
            g, u = g + 2, u + RAW
        silu_mul(1, u, g - 1, lap, weight)
        pe_turn(g - 1, lap)
        hidT_split(u, g - 1, lap)
        look_ahead(UNITS_D)
        pe_down(u, g - 1, lap)
        ffn["g"], st["use"] = g, u + UNITS_D


    x_mark = []
    mod_marks = []

    def fetch(name, *copies):
        landed = sem(name)
        ACT.need(*x_mark)
        for dst, src in copies:
            act.dma_start(dst, src).then_inc(landed, 16)
        return (landed, 16 * len(copies))

    def flat(name):
        v = io[name]
        return v.rearrange({1: "a -> a", 2: "a b -> (a b)", 3: "a b c -> (a b c)"}[len(v.shape)])

    start = fetch("small_in",
                  (tables[:, :], io["tables"]), (x[:, :, :], io["x"][0].rearrange("(t p) d -> p t d", p=P)),
                  *((vec_rows[col_at[n]:col_at[n] + k, :], flat(n).rearrange("(k p) -> k p", p=P)) for n, k in COLUMNS),
                  *((rows[:, row_at[n]:row_at[n] + k], flat(n).rearrange("(a n) -> a n", a=1).to_broadcast([P, k]))
                    for n, k in ROWS))
    z = DVE.did(dve.memset(zeros[:, :], 0.0))
    o = DVE.did(dve.memset(ones[:, :], 1.0))
    PE.need(z, o, start)
    m = PE.did(pe.transpose(psum[3][:, 0:n_cols], vec_rows[0:n_cols, :], ident[0:n_cols, 0:n_cols]))
    cols_in = DVE.run([m], dve.tensor_copy, cols[:, 0:n_cols], psum[3][:, 0:n_cols])
    bank_mark[3] = (cols_in,)
    x_mark[:] = [start]

    def rstd_of(ss, n, width, marks):
        v, r = tiny(width), tiny(width)
        a = DVE.run(marks, dve.tensor_scalar, v, ss, 1.0 / n, EPS, ALU.mult, ALU.add)
        b = ACT.run([a], act.activation, v, v, ACTF.Sqrt)
        return r, DVE.run([b], dve.reciprocal, r, v)

    def turn_to_aT(src, nk, marks, gain, bias=None, full=None, free=()):
        PE.need(*marks)
        for b in range(4, 8):
            PE.need(*bank_mark[b])
        done = []
        for k0 in range(0, nk, 2):
            b = 4 + k0 // 2
            ks = range(k0, min(k0 + 2, nk))
            bank = {k: psum[b][:, (k - k0) * S:(k - k0 + 1) * S] for k in ks}
            for k in ks:
                for t in range(NT):
                    ins = pe.transpose(bank[k][:, t * P:(t + 1) * P], src(t, k), ident)
            m = PE.did(ins)
            if bias is None:
                for k in ks:
                    h = ACT.run([m, *free], act.activation, aT[0][:, k, :], bank[k], ACTF.Identity, scale=gain(k))
                for k in ks:
                    done.append(DVE.run([h], dve.scalar_tensor_tensor, out=aT[1][:, k, :], in0=bank[k],
                                        scalar=gain(k), in1=aT[0][:, k, :].bitcast(F32), op0=ALU.mult,
                                        op1=ALU.subtract))
                bank_mark[b] = (done[-1],)
            else:
                for k in ks:
                    a = DVE.run([m, *free], dve.tensor_scalar, full[:, k, :], bank[k], gain(k), bias(k),
                                ALU.mult, ALU.add)
                bank_mark[b] = (a,)
                for k in ks:
                    h = ACT.run([a], act.activation, aT[0][:, k, :], full[:, k, :], ACTF.Copy)
                    done.append(DVE.run([h], dve.tensor_tensor, aT[1][:, k, :], full[:, k, :],
                                        aT[0][:, k, :].bitcast(F32), ALU.subtract))
        return done

    def normed(gain, bias=None, free=()):
        ss = tiny(NT)
        sq = [ACT.run([x_mark[0], *free], act.activation, xn[:, t, :], x[:, t, :], ACTF.Square,
                      accum_out=ss[:, t:t + 1]) for t in range(NT)]
        r, m = rstd_of(ss, D, NT, sq)
        for t in range(NT):
            m = DVE.run([m], dve.tensor_scalar, xn[:, t, :], x[:, t, :], r[:, t:t + 1], None, ALU.mult)
        return turn_to_aT(lambda t, k: xn[:, t, k * P:(k + 1) * P], KD, [m], gain, bias,
                          hT_full if bias else None)

    def gated_add(t, half, bank, mark, gate=None, factor=1.0):
        xs = x[:, t, half * SLAB:(half + 1) * SLAB]
        if gate is None:
            x_mark[0] = DVE.run([mark, x_mark[0]], dve.scalar_tensor_tensor, out=xs, in0=bank,
                                scalar=factor, in1=xs, op0=ALU.mult, op1=ALU.add)
        else:
            tmp = xn[:, t, half * SLAB:(half + 1) * SLAB]
            a = DVE.run([mark], dve.tensor_tensor, tmp, bank,
                        gates[:, gate, half * SLAB:(half + 1) * SLAB], ALU.mult)
            x_mark[0] = DVE.run([a, x_mark[0]], dve.tensor_tensor, xs, xs, tmp, ALU.add)
        return (x_mark[0],)

    def add_ffn(mark, gate=None, factor=1.0):
        for t in range(NT):
            for half in range(2):
                b = 4 + 2 * t + half
                bank_mark[b] = gated_add(t, half, psum[b][:, :], mark, gate, factor)
        for b in range(3):
            bank_mark[b] = bank_mark[7]

    def dense_ffn(gate, up, down, marks, g=None, factor=1.0):
        final = st["use"] + FFN_UNITS == total
        ffn_load(gate, up, down)
        zero_y([m for b in range(4, 8) for m in bank_mark[b]])
        for b in range(3):
            PE.need(*bank_mark[b])
        ffn_steps(marks, final=final)
        add_ffn(close_y(), g, factor)

    def cols_of(w, c, k, c0=0):
        return w[k * P:(k + 2) * P, ds(c * STEP_F + c0, STEP_F)].rearrange("(k p) n -> p k n", p=P)

    def rows_of(w, c, f):
        return w[ds(c * STEP_F + f * P, P), :]

    mod_done = sem("mod_done")
    def conditioning(layer):
        w = io["ada_w"][layer]
        def load_round(c):
            for s in range(3):
                v = w[:, ds((3 * c + s) * SLAB, SLAB)].rearrange("(k p) n -> p k n", p=P)
                for k in range(0, KD, 2):
                    load((lambda r: r[:, :].rearrange("p (k n) -> p k n", k=2), v[:, k:k + 2, :]))
        n_rounds = 6 * D // SLAB // 3
        load_round(0)
        base, sp_lap = st["load"], st["sp_lap"]
        with sp.Fori(0, n_rounds - 1) as i:
            st["sp_lap"] = sp_lap + i
            load_round(i + 1)
        st["load"], st["sp_lap"] = base + 12 * (n_rounds - 1), sp_lap

        c8 = cols[:, col_at["c"]:col_at["c"] + KD]
        cs = tiny(KD)
        a = ACT.run([cols_in, x_mark[0]], act.activation, cs, c8, ACTF.Silu)
        a = DVE.run([a], dve.tensor_copy, cs_wide[:, :, :], cs.unsqueeze(2).to_broadcast([P, KD, P]))
        h = ACT.run([a, *bank_mark[0], *bank_mark[1]], act.activation, cT[0][:, :, :], cs_wide[:, :, :], ACTF.Copy)
        left_mark = DVE.run([h], dve.tensor_tensor, cT[1][:, :, :], cs_wide[:, :, :],
                            cT[0][:, :, :].bitcast(F32), ALU.subtract)
        ACT.need(x_mark[0])
        b_row = fetch(f"bias_in{layer}", *((dst[:, :], io["ada_b"][layer:layer + 1, D * c0:D * c1]) for dst, c0, c1 in
                      ((bias_row, 0, 2), (bias_g1, 2, 3), (bias_ss2, 3, 5), (bias_g2, 5, 6))))
        PE.need(left_mark)
        m0 = layer * 12
        def round_of(c, n, u, lap):
            for s in range(3):
                bank = psum[s]
                nn = m0 + n * 3 + s
                if nn >= 3:
                    pe.wait_ge(mod_done, nn - 2 + 3 * lap)
                for j in range(4):
                    pe.wait_ge(lo_done, u + 4 * s + j + 1 + 12 * lap)
                    wv = unit(u + 4 * s + j)
                    for kk in range(2):
                        k = 2 * j + kk
                        ins = passes(bank[:, :], [a[:, k, :] for a in cT], [r[:, kk, :] for r in wv],
                                     k == 0, k == KD - 1)
                    ins.then_inc(unit_free, 1)
                for _ in range(4):
                    split_one()
                act.wait_ge(unit_free, u + 4 * s + 4 + 12 * lap)
                act.activation(mod_rows[:, ds((3 * c + s) * SLAB, SLAB)], bank[:, :], ACTF.Copy).then_inc(mod_done, 1)
        for b in range(3):
            PE.need(*bank_mark[b])
        u = st["use"]
        split_to(u + 4)
        round_of(0, 0, u, st["lap"])
        split = st["split"]
        with nc.Fori(0, n_rounds - 1, engines=compute) as i:
            st["lap"] = i
            round_of(i + 1, 1, u + 12, i)
        st["lap"], st["split"] = 0, split + 12 * (n_rounds - 1)
        st["use"] = u + 12 * n_rounds
        rows_in = (mod_done, m0 + 12)
        PE.need(rows_in, b_row)
        PE.need(*bank_mark[3])
        for k in range(32):
            src = (k if k < 16 else k + 8) * P
            pe.matmul(psum[3][:, k:k + 1], mod_rows[0:1, src:src + P], ones[:, 0:1], start=True, stop=False)
            b = (bias_row if k < 16 else bias_ss2)[:, (k % 16) * P:(k % 16 + 1) * P]
            ins = pe.matmul(psum[3][:, k:k + 1], b, ones[:, 0:1], start=False, stop=True)
        m = PE.did(ins)
        cm = DVE.run([m], dve.tensor_copy, mod_cols[:, :], psum[3][:, 0:32])
        bank_mark[3] = (cm,)
        for b in range(4, 8):
            PE.need(*bank_mark[b])
        for g in range(2):
            for half in range(2):
                bank = psum[4 + 2 * g + half]
                br = (bias_g1, bias_g2)[g]
                m = PE.did(pe.matmul(bank[:, :], ones[:, :], br[:, half * SLAB:(half + 1) * SLAB],
                                     start=True, stop=True))
                src = (2 + 3 * g) * D + half * SLAB
                m = DVE.run([m, rows_in], dve.tensor_tensor, gates[:, g, half * SLAB:(half + 1) * SLAB],
                            bank[:, :], mod_rows[:, src:src + SLAB], ALU.add)
                bank_mark[4 + 2 * g + half] = (m,)
        mod_marks[:] = [m]
        for b in range(3):
            bank_mark[b] = (rows_in,)
        gm = DVE.run([cm], dve.scalar_tensor_tensor, out=gain_cols[:, 0:8], in0=mod_cols[:, 8:16], scalar=1.0,
                     in1=cols[:, col_at["norm_mix_g"] + 8 * layer:col_at["norm_mix_g"] + 8 * layer + 8],
                     op0=ALU.add, op1=ALU.mult)
        gm = DVE.run([gm], dve.scalar_tensor_tensor, out=gain_cols[:, 8:16], in0=mod_cols[:, 24:32], scalar=1.0,
                       in1=cols[:, col_at["norm_ffn_g"] + 8 * layer:col_at["norm_ffn_g"] + 8 * layer + 8],
                       op0=ALU.add, op1=ALU.mult)
        mod_marks.append(gm)

    def store_x():
        y = out[0].rearrange("(t p) d -> p t d", p=P)
        SP.need(x_mark[0])
        sp.dma_start(y, x[:, :, :]).then_inc(out_sem, 16)
        sp.wait_ge(out_sem, 16)
    out_sem = sem("out_stored")
    def project(w, width, marks, kd=KD, at=0, func=None):
        c = 0
        while c < width:
            n = min(SLAB, width - c)
            proj_load(w, c, n, kd)
            f = func(c) if func else None

            def out_of_bank(t, bank, mark, c=c, n=n, f=f):
                dst = proj[:, t, at + c:at + c + n]
                if f is not None or t == 0:
                    m = ACT.run([mark], act.activation, dst, bank, f or ACTF.Copy)
                else:
                    m = DVE.run([mark], dve.tensor_copy, dst, bank)
                out_marks.append(m)
                return (m,)
            slab(n, out_of_bank, marks, kd)
            marks = ()
            c += n

    def project_out(w, marks, gate=None):
        for half in range(2):
            proj_load(w, half * SLAB, SLAB)
            slab(SLAB, lambda t, bank, mark, half=half: gated_add(t, half, bank, mark, gate), marks)
            marks = ()

    def turn_heads(src, n, width, marks, at=0):
        done = []
        PE.need(*marks)
        for j in range(0, n, 2):
            b = 4 + (j // 2) % 4
            k = min(2, n - j)
            PE.need(*bank_mark[b])
            for jj in range(k):
                for t in range(NT):
                    ins = pe.transpose(psum[b][0:width, jj * S + t * P:jj * S + (t + 1) * P],
                                       src(t, j + jj), ident)
            m = PE.did(ins)
            dst = qkT[0:width, at + j:at + j + k, :].rearrange("p j s -> p (j s)")
            if (j // 2) % 2:
                m = ACT.run([m, *marks], act.activation, dst, psum[b][0:width, 0:k * S], ACTF.Copy)
            else:
                m = DVE.run([m, *marks], dve.tensor_copy, dst, psum[b][0:width, 0:k * S])
            bank_mark[b] = (m,)
            done.append(m)
        return done

    def rope(x1, x2, cos, sin, shape, marks):
        n = int(np.prod(shape[1:]))
        names = {3: "p (a b) -> p a b", 4: "p (a b c) -> p a b c"}[len(shape)]
        dims = dict(zip("abc", shape[1:]))
        tmp = [rope_tmp[:, i * n:(i + 1) * n].rearrange(names, **dims) for i in range(4)]
        a = [DVE.run(marks, dve.tensor_tensor, tmp[i], p, q, ALU.mult)
             for i, (p, q) in enumerate(((x1, cos), (x2, sin), (x1, sin), (x2, cos)))]
        DVE.run(a, dve.tensor_tensor, x1, tmp[0], tmp[1], ALU.subtract)
        return DVE.run(a, dve.tensor_tensor, x2, tmp[2], tmp[3], ALU.add)

    def group_norm(view, n, d, marks, gains=()):
        sq = xn[:, :, 0:n * d].rearrange("p t (n d) -> p t n d", n=n)
        a = [ACT.run(marks, act.activation, sq[:, t], view[:, t], ACTF.Square) for t in range(NT)]
        ss = tiny(NT * n)
        m = DVE.run(a, dve.reduce_sum, ss.rearrange("p (t n) -> p t n", t=NT), sq, axis=AX.X)
        r, m = rstd_of(ss, d, NT * n, [m])
        r = r.rearrange("p (t n) -> p t n", t=NT).unsqueeze(3).to_broadcast([P, NT, n, d])
        m = DVE.run([m], dve.tensor_tensor, view, view, r, ALU.mult)
        done = [m]
        for v, g in gains:
            done.append(DVE.run([m], dve.tensor_tensor, v, v, g, ALU.mult))
        return done

    def attention(n, width, q, k, v, scale, dst, marks, causal=False, pair=None):
        maps = 2 if pair is not None else 1
        bufs = [probs_d[:, i, :] for i in range(4)] if maps == 2 else [probs[:, i, :] for i in range(2)]
        rs, rr = tiny(NT * n * maps), tiny(NT * n * maps)
        nmax = tiny(2 * NT * maps)
        turned_of, pv_of, ready = {}, {}, {}

        def scores(h):
            for mp in range(maps):
                i = (h * maps + mp) % len(bufs)
                b = 4 + (h * maps + mp) % 2
                e = bufs[i].rearrange("p (t s) -> p t s", t=NT)
                PE.need(*bank_mark[b], *(marks if h == 0 else ()))
                for t in range(NT):
                    ins = pe.matmul(psum[b][:, t * S:(t + 1) * S], q(h, mp, t), k(h, mp), start=True, stop=True)
                m = PE.did(ins)
                sc = psum[b][:, :].rearrange("p (t s) -> p t s", t=NT)
                old = turned_of.get(h - len(bufs) // maps, ())
                nm = nmax[:, (i % (2 * maps)) * NT:(i % (2 * maps)) * NT + NT]
                olde = ready.get(h - 2, ())
                if causal:
                    m = DVE.run([m, *old], dve.scalar_tensor_tensor, out=e, in0=sc, scalar=scale,
                                in1=table("causal").rearrange("p (t s) -> p t s", t=NT), op0=ALU.mult, op1=ALU.add)
                    bank_mark[b] = (m,)
                    m = DVE.run([m, *olde], dve.tensor_reduce, nm, e, AX.X, ALU.max, negate=True)
                    src, k_scale = e, 1.0
                else:
                    m = DVE.run([m, *olde], dve.tensor_reduce, nm, sc, AX.X, ALU.max, negate=True)
                    m = DVE.run([m], dve.tensor_scalar, nm, nm, scale, None, ALU.mult)
                    src, k_scale = sc, scale
                ex = []
                for t in range(NT):
                    j = (t * maps + mp) * n + h
                    ex.append(ACT.run([m, *old], act.activation, e[:, t, :], src[:, t, :], ACTF.Exp,
                                      bias=nm[:, t:t + 1], scale=k_scale, accum_out=rs[:, j:j + 1]))
                if not causal:
                    bank_mark[b] = (ex[-1],)
                ready[h] = (*ready.get(h, ()), *ex) if mp else tuple(ex)
            if maps == 2:
                i = (h * 2) % len(bufs)
                w = []
                for t in range(NT):
                    j0, j1 = (t * 2) * n + h, (t * 2 + 1) * n + h
                    a0 = DVE.run(ready[h], dve.reciprocal, rr[:, j0:j0 + 1], rs[:, j0:j0 + 1])
                    a1 = DVE.run(ready[h], dve.reciprocal, rr[:, j1:j1 + 1], rs[:, j1:j1 + 1])
                    a1 = DVE.run([a1], dve.tensor_tensor, rr[:, j1:j1 + 1], rr[:, j1:j1 + 1], pair, ALU.mult)
                    e0, e1 = (bufs[i + z].rearrange("p (t s) -> p t s", t=NT)[:, t, :] for z in (0, 1))
                    a1 = DVE.run([a1], dve.tensor_scalar, e1, e1, rr[:, j1:j1 + 1], None, ALU.mult)
                    w.append(DVE.run([a0, a1], dve.scalar_tensor_tensor, out=e0, in0=e0,
                                     scalar=rr[:, j0:j0 + 1], in1=e1, op0=ALU.mult, op1=ALU.subtract))
                ready[h] = tuple(w)

        def turn(h):
            b = 2 + h % 2
            e = bufs[(h * maps) % len(bufs)]
            PE.need(*ready[h], *bank_mark[b])
            for kc in range(NT):
                for t in range(NT):
                    ins = pe.transpose(psum[b][:, kc * S + t * P:kc * S + (t + 1) * P],
                                       e[:, t * S + kc * P:t * S + (kc + 1) * P], ident)
            m = PE.did(ins)
            turned_of[h] = (m,)
            old = pv_of.get(h - 2, ())
            if causal:
                m = ACT.run([m, *old], act.activation, probsT[:, h % 2, :], psum[b][:, :], ACTF.Copy)
            else:
                m = DVE.run([m, *old], dve.tensor_copy, probsT[:, h % 2, :], psum[b][:, :])
            bank_mark[b] = (m,)

        def values(h):
            PE.need(*bank_mark[2 + h % 2])
            if h == 0:
                PE.need(*bank_mark[6], *bank_mark[7])
            for t in range(NT):
                last = t if causal else NT - 1
                for kc in range(last + 1):
                    ins = pe.matmul(psum[6 + t][:, h * width:(h + 1) * width],
                                    probsT[:, h % 2, kc * S + t * P:kc * S + (t + 1) * P], v(h, kc),
                                    start=kc == 0, stop=kc == last)
            pv_of[h] = (PE.did(ins),)

        for h in range(n + 2):
            if h < n:
                scores(h)
            if 1 <= h <= n:
                turn(h - 1)
            if h >= 2:
                values(h - 2)
        done = []
        if maps == 1:
            a = DVE.run(ready[n - 1], dve.reciprocal, rr, rs)
            for t in range(NT):
                r = rr[:, t * n:(t + 1) * n].unsqueeze(2).to_broadcast([P, n, width])
                m = DVE.run([a, *pv_of[n - 1]], dve.tensor_tensor,
                            dst(t).rearrange("p (n w) -> p n w", n=n),
                            psum[6 + t][:, 0:n * width].rearrange("p (n w) -> p n w", n=n), r, ALU.mult)
                bank_mark[6 + t] = (m,)
                done.append(m)
            return done
        return list(pv_of[n - 1])

    def bank_group_norm(n, d, dst, marks):
        ss = tiny(NT * n)
        a = [ACT.run(marks, act.activation, dst(t), psum[6 + t][:, 0:n * d], ACTF.Square) for t in range(NT)]
        s = [DVE.run([a[t]], dve.reduce_sum, ss[:, t * n:(t + 1) * n],
                     dst(t).rearrange("p (n d) -> p n d", n=n), axis=AX.X) for t in range(NT)]
        r, m = rstd_of(ss, d, NT * n, s)
        done = []
        for t in range(NT):
            rb = r[:, t * n:(t + 1) * n].unsqueeze(2).to_broadcast([P, n, d])
            m = DVE.run([m], dve.tensor_tensor, dst(t).rearrange("p (n d) -> p n d", n=n),
                        psum[6 + t][:, 0:n * d].rearrange("p (n d) -> p n d", n=n), rb, ALU.mult)
            bank_mark[6 + t] = (m,)
            done.append(m)
        return done

    out_marks = []

    def tab2(name, k):
        return table(name).rearrange("p (t k) -> p t k", t=NT)

    def hybrid_mixer(layer):
        marks = normed(lambda k: gain_cols[:, k:k + 1], lambda k: mod_cols[:, k:k + 1], mod_marks)
        del out_marks[:]
        project(io["w_in"][layer], 3584, marks)
        m = out_marks
        t8 = turn_heads(lambda t, j: proj[:, t, j * P:(j + 1) * P], 8, P, m[0:4])
        gate_silu = [ACT.run([*m], act.activation, proj[:, t, 3072:3584], proj[:, t, 3072:3584], ACTF.Silu)
                     for t in range(NT)]
        o_a = attention(8, 64, lambda h, mp, t: qkT[64 * (h % 2):64 * (h % 2) + 64, h // 2, t * P:(t + 1) * P],
                        lambda h, mp: qkT[64 * (h % 2):64 * (h % 2) + 64, 4 + h // 2, :],
                        lambda h, kc: proj[:, kc, 1024 + 64 * h:1024 + 64 * (h + 1)],
                        64 ** -0.5, lambda t: xn[:, t, 0:SLAB], [*t8, *m[4:6]], causal=True)
        ss = tiny(NT)
        a = [ACT.run([o_a[t]], act.activation, xn[:, t, SLAB:], xn[:, t, 0:SLAB], ACTF.Square,
                     accum_out=ss[:, t:t + 1]) for t in range(NT)]
        r, a2 = rstd_of(ss, SLAB, NT, a)
        o_a = [DVE.run([a2], dve.tensor_scalar, xn[:, t, 0:SLAB], xn[:, t, 0:SLAB], r[:, t:t + 1], None, ALU.mult)
               for t in range(NT)]
        rt = []
        for t in range(NT):
            v4 = proj[:, t, 1536:2560].rearrange("p (n d) -> p n d", n=8)
            c, s = (tab2(n, 64)[:, t, :].unsqueeze(1).to_broadcast([P, 8, 64]) for n in ("ret_cos", "ret_sin"))
            rt.append(rope(v4[:, :, 0:64], v4[:, :, 64:128], c, s, [P, 8, 64], [*m, *o_a, *rt]))
        t8 = turn_heads(lambda t, j: proj[:, t, 1536 + j * P:1536 + (j + 1) * P], 8, P, rt)
        pv = {}
        PE.need(*t8)

        def ret_scores(h):
            b = 4 + h % 2
            PE.need(*bank_mark[b])
            pe.matmul(psum[b][:, 0:S], qkT[:, 4 + h, 0:P], qkT[:, h, :], start=True, stop=True)
            mk = PE.did(pe.matmul(psum[b][:, S:S + P], qkT[:, 4 + h, P:S], qkT[:, h, P:S], start=True, stop=True))
            dec = table("decay").rearrange("p (h s) -> p h s", h=4)[:, h, :]
            a = DVE.run([mk, *pv.get(h - 2, ())], dve.tensor_tensor, probsT[:, h % 2, 0:S], psum[b][:, 0:S], dec, ALU.mult)
            a = DVE.run([mk], dve.tensor_tensor, probsT[:, h % 2, S:S + P], psum[b][:, S:S + P], dec[:, 0:P], ALU.mult)
            bank_mark[b] = (a,)
            return a

        def ret_values(h, mark):
            PE.need(mark, *bank_mark[6], *bank_mark[7]) if h == 0 else PE.need(mark)
            vr = [proj[:, kc, 2560 + h * P:2560 + (h + 1) * P] for kc in range(NT)]
            sT = probsT[:, h % 2, :]
            pe.matmul(psum[6][:, h * P:(h + 1) * P], sT[:, 0:P], vr[0], start=True, stop=True)
            pe.matmul(psum[7][:, h * P:(h + 1) * P], sT[:, P:S], vr[0], start=True, stop=False)
            pv[h] = (PE.did(pe.matmul(psum[7][:, h * P:(h + 1) * P], sT[:, S:S + P], vr[1], start=False, stop=True)),)

        mk = {0: ret_scores(0)}
        for h in range(4):
            if h < 3:
                mk[h + 1] = ret_scores(h + 1)
            ret_values(h, mk[h])
        o_r = bank_group_norm(4, P, lambda t: xn[:, t, SLAB:], [*pv[3], *o_a])
        o_r = [DVE.run([o_r[t], *gate_silu], dve.tensor_tensor, xn[:, t, SLAB:], xn[:, t, SLAB:],
                       proj[:, t, 3072:3584], ALU.mult) for t in range(NT)]
        marks = turn_to_aT(lambda t, k: xn[:, t, k * P:(k + 1) * P], KD, [*o_a, *o_r],
                           lambda k: col("att_out_g", 4 * layer + k) if k < 4 else col("ret_out_g", 4 * layer + k - 4))
        project_out(io["w_out"][layer], marks, gate=0)

    def even_mixer():
        marks = normed(lambda k: col("ev_norm_2", k))
        ws_in = fetch("w_s_in", (w_s[:, :, :], io["ev_w_s_2"][0].rearrange("g i j -> i g j")))
        del out_marks[:]
        project(io["ev_w_in_2"][0], 2560, marks, func=lambda c: ACTF.Gelu_apprx_tanh if c < 1024 else None)
        m = list(out_marks)
        PE.need(ws_in, *bank_mark[2], *bank_mark[3])
        for g in range(8):
            ins = pe.transpose(psum[2 + g // 4][:, (g % 4) * P:(g % 4 + 1) * P], w_s[:, g, :], ident)
        a = PE.did(ins)
        wT = [DVE.run([a], dve.tensor_copy, w_sT[:, 4 * i:4 * i + 4, :].rearrange("p g j -> p (g j)"), psum[2 + i][:, :])
              for i in range(2)]
        vv = proj[:, :, 512:1024].rearrange("p t (n d) -> p t n d", n=8)
        vn = group_norm(vv, 8, 64, m, [(proj[:, :, 512:1024], row("ev_sgu_norm_2").unsqueeze(1).to_broadcast([P, NT, 512]))])
        PE.need(*wT, *vn)
        for g in range(8):
            ins = pe.matmul(psum[2 + g // 4][:, (g % 4) * P:(g % 4 + 1) * P], w_sT[:, g, :],
                            proj[:, :, 512 + 64 * g:512 + 64 * (g + 1)], start=True, stop=True)
        a = PE.did(ins)
        qk = proj[:, :, 1024:2048].rearrange("p t (n d) -> p t n d", n=16)
        gains = []
        for i, g in enumerate(("ev_q_norm_2", "ev_k_norm_2")):
            for t in range(NT):
                gains.append((qk[:, t, 8 * i:8 * i + 8, :], row(g).unsqueeze(1).to_broadcast([P, 8, 64])))
        qn = group_norm(qk, 16, 64, m, gains)
        rt = []
        for t in range(NT):
            c, s = (tab2(n, 32)[:, t, :].unsqueeze(1).to_broadcast([P, 16, 32]) for n in ("diff_cos", "diff_sin"))
            rt.append(rope(qk[:, t, :, 0:32], qk[:, t, :, 32:64], c, s, [P, 16, 32], [*qn, *rt, a]))
        ga = []
        for g in range(8):
            mixed = psum[2 + g // 4][:, (g % 4) * P:(g % 4 + 1) * P].rearrange("p (t d) -> p t d", t=NT)
            ga.append(DVE.run([a, *qn], dve.scalar_tensor_tensor, out=xn[:, :, 64 * g:64 * (g + 1)], in0=mixed,
                              scalar=col("ev_b_s_2", g), in1=proj[:, :, 64 * g:64 * (g + 1)], op0=ALU.add, op1=ALU.mult))
        bank_mark[2] = bank_mark[3] = (ga[-1],)
        lam_init = 0.8 - 0.6 * float(np.exp(-0.3 * 0))
        lam, pr = tiny(2), xn[:, 0, SLAB:SLAB + P]
        for i in range(2):
            a = DVE.run([*qn], dve.tensor_tensor, pr[:, 64 * i:64 * (i + 1)], row(f"ev_lam_q{i + 1}_2"),
                        row(f"ev_lam_k{i + 1}_2"), ALU.mult)
        a = DVE.run([a], dve.reduce_sum, lam, pr.rearrange("p (i d) -> p i d", i=2), axis=AX.X)
        a = ACT.run([a], act.activation, lam, lam, ACTF.Exp)
        a = DVE.run([a], dve.tensor_tensor, lam[:, 0:1], lam[:, 0:1], lam[:, 1:2], ALU.subtract)
        a = DVE.run([a], dve.tensor_scalar, lam[:, 0:1], lam[:, 0:1], lam_init, None, ALU.add)
        t8 = turn_heads(lambda t, j: proj[:, t, 1024 + j * P:1024 + (j + 1) * P], 8, P, rt)
        pv = attention(4, P, lambda h, mp, t: qkT[64 * mp:64 * mp + 64, h, t * P:(t + 1) * P],
                       lambda h, mp: qkT[64 * mp:64 * mp + 64, 4 + h, :],
                       lambda h, kc: proj[:, kc, 2048 + h * P:2048 + (h + 1) * P], 64 ** -0.5, None,
                       [*t8, *m, a], pair=lam[:, 0:1])
        o_b = bank_group_norm(4, P, lambda t: xn[:, t, SLAB:], [*pv, a])
        sub = tiny(1)
        sm = DVE.run([cols_in], dve.tensor_scalar, sub, col("ev_sub_norm_2", 0), 1.0 - lam_init, None, ALU.mult)
        marks = turn_to_aT(lambda t, k: xn[:, t, k * P:(k + 1) * P], KD, [*ga, *o_b, sm],
                           lambda k: 1.0 if k < 4 else sub)
        project_out(io["ev_w_out_2"][0], marks)

    def odd_mixer():
        marks = normed(lambda k: col("od_norm_2", k))
        del out_marks[:]
        project(io["od_w_in_2"][0], 1184, marks)
        m = list(out_marks)
        CQ, CKV, KPE, GQ, GK, GV, UQ, UKV = 0, 256, 384, 416, 928, 1056, 1184, 1952
        ss = tiny(2 * NT)
        a = [ACT.run(m, act.activation, xn[:, t, SLAB + c0:SLAB + c0 + n], proj[:, t, c0:c0 + n], ACTF.Square,
                     accum_out=ss[:, NT * i + t:NT * i + t + 1])
             for i, (c0, n) in enumerate(((CQ, 256), (CKV, 128))) for t in range(NT)]
        cn = []
        for i, (c0, n) in enumerate(((CQ, 256), (CKV, 128))):
            r, mk = rstd_of(ss[:, NT * i:NT * (i + 1)], n, NT, a)
            for t in range(NT):
                cn.append(DVE.run([mk], dve.tensor_scalar, xn[:, t, c0:c0 + n], proj[:, t, c0:c0 + n],
                                  r[:, t:t + 1], None, ALU.mult))
        marks = turn_to_aT(lambda t, k: xn[:, t, k * P:(k + 1) * P], 3, cn,
                           lambda k: col("od_cq_norm_2", k) if k < 2 else col("od_ckv_norm_2", 0))
        project(io["od_w_uq_2"][0], 768, marks, kd=2, at=UQ)
        load((lambda r: r[:, :], io["od_w_ukv_2"][0]))
        u = st["use"]
        split_to(u + 1)
        PE.need(marks[2])
        pe.wait_ge(lo_done, u + 1)
        kvm = []
        for i in range(4):
            half, t = i // 2, i % 2
            PE.need(*bank_mark[i])
            ins = passes(psum[i][:, :], [z[:, 2, t * P:(t + 1) * P] for z in aT],
                         [z[:, half * SLAB:(half + 1) * SLAB] for z in unit(u, 1, 1024)[0:2]]
                         if False else [z[u % SPL][:, half * SLAB:(half + 1) * SLAB] for z in (hi, lo)], True, True)
            if i < 3:
                mk = PE.did(ins)
            else:
                ins.then_inc(unit_free, 1)
                mk = (unit_free, u + 1)
                st["use"] += 1
            dst = proj[:, t, UKV + half * SLAB:UKV + (half + 1) * SLAB]
            kvm.append(ACT.run([mk], act.activation, dst, psum[i][:, :], ACTF.Copy) if t == 0 else
                       DVE.run([mk], dve.tensor_copy, dst, psum[i][:, :]))
            bank_mark[i] = (kvm[-1],)
        split_to(u + 1 + 4)
        m2 = [*out_marks, *kvm]
        kf = k_full[:, :, :].rearrange("p t (n d) -> p t n d", n=8)
        kv = proj[:, :, UKV:UKV + 1024].rearrange("p t (n d) -> p t n d", n=8)
        km = []
        for t in range(NT):
            km.append(DVE.run(m2, dve.tensor_copy, kf[:, t, :, 0:64], kv[:, t, :, 0:64]))
            km.append(ACT.run(m2, act.activation, kf[:, t, :, 64:96],
                              proj[:, t, KPE:KPE + 32].unsqueeze(1).to_broadcast([P, 8, 32]), ACTF.Copy))
        qv = proj[:, :, UQ:UQ + 768].rearrange("p t (n d) -> p t n d", n=8)
        rt, prev = [], m2
        for v, g in ((qv, "od_mla_q_norm_2"), (kf, "od_mla_k_norm_2")):
            gn = group_norm(v, 8, 96, [*prev, *km], [(v[:, t], row(g).unsqueeze(1).to_broadcast([P, 8, 96])) for t in range(NT)])
            for t in range(NT):
                c, s = (tab2(n, 16)[:, t, :].unsqueeze(1).to_broadcast([P, 8, 16]) for n in ("mla_cos", "mla_sin"))
                rt.append(rope(v[:, t, :, 64:80], v[:, t, :, 80:96], c, s, [P, 8, 16], [*gn, *rt]))
            prev = rt
        gv = proj[:, :, GQ:GV].rearrange("p t (n d) -> p t n d", n=10)
        gn = group_norm(gv, 10, 64, [*m, *rt],
                        [(gv[:, t, a0:a1], row(g).unsqueeze(1).to_broadcast([P, a1 - a0, 64])) for t in range(NT)
                         for a0, a1, g in ((0, 8, "od_gqa_q_norm_2"), (8, 10, "od_gqa_k_norm_2"))])
        for t in range(NT):
            for part in range(2):
                c, s = (tab2(n, 32)[:, t, 16 * part:16 * part + 16].unsqueeze(1).to_broadcast([P, 10, 16])
                        for n in ("gqa_cos", "gqa_sin"))
                o = 32 * part
                rt.append(rope(gv[:, t, :, o:o + 16], gv[:, t, :, o + 16:o + 32], c, s, [P, 10, 16], [*gn, *rt]))
        tq = turn_heads(lambda t, j: qv[:, t, j, :], 8, 96, rt)
        tk = turn_heads(lambda t, j: kf[:, t, j, :], 8, 96, rt, at=8)
        o_c = attention(8, 64, lambda h, mp, t: qkT[0:96, h, t * P:(t + 1) * P], lambda h, mp: qkT[0:96, 8 + h, :],
                        lambda h, kc: kv[:, kc, h, 64:128], 96 ** -0.5, lambda t: xn[:, t, 0:SLAB], [*tq, *tk, *m2])
        tq = turn_heads(lambda t, j: gq_pairs[:, t, j, :], 4, P, repack(gv, rt))
        tk = turn_heads(lambda t, j: proj[:, t, GK:GK + P], 1, P, rt, at=4)
        o_d = attention(8, 64, lambda h, mp, t: qkT[64 * (h // 4):64 * (h // 4) + 64, h % 4, t * P:(t + 1) * P],
                        lambda h, mp: qkT[64 * (h // 4):64 * (h // 4) + 64, 4, :],
                        lambda h, kc: proj[:, kc, GV + 64 * (h // 4):GV + 64 * (h // 4) + 64], 64 ** -0.5,
                        lambda t: xn[:, t, SLAB:], [*tq, *tk, *o_c])
        marks = turn_to_aT(lambda t, k: xn[:, t, k * P:(k + 1) * P], KD, [*o_c, *o_d], lambda k: 1.0)
        project_out(io["od_w_out_2"][0], marks)

    def repack(gv, marks):
        src = gv[:, :, 0:8, :]
        return [DVE.run(marks, dve.tensor_copy, gq_pairs[:, t, :, :].rearrange("p c (r d) -> p c r d", r=2),
                        src[:, t].rearrange("p (r c) d -> p c r d", r=2)) for t in range(NT)]

    def route():
        rm = fetch("router_in", (router[:, :, :], io["router_w"][0].rearrange("(k p) e -> p k e", p=P)))
        marks = normed(lambda k: gain_cols[:, 8 + k:9 + k], lambda k: mod_cols[:, 16 + k:17 + k])
        PE.need(rm, *marks, *bank_mark[3])
        for t in range(NT):
            for k in range(KD):
                ins = pe.matmul(psum[3][:, t * NE:(t + 1) * NE], hT_full[:, k, t * P:(t + 1) * P],
                                router[:, k, :], start=k == 0, stop=k == KD - 1)
        m = PE.did(ins)
        for t in range(NT):
            lg, top, idx = tiny(NE), tiny(NE), tiny(NE)
            a = DVE.run([m], dve.tensor_copy, lg, psum[3][:, t * NE:(t + 1) * NE])
            b = DVE.run([a], dve.max, top, lg)
            iu = top_idx[:, :]
            b = DVE.run([b], dve.max_index, iu, top, lg)
            b = DVE.run([b], dve.tensor_copy, idx, iu)
            e, r = tiny(2), tiny(2)
            a = DVE.run([b], dve.tensor_tensor, e[:, 0:1], top[:, 1:2], top[:, 0:1], ALU.subtract)
            a = ACT.run([a], act.activation, e[:, 0:1], e[:, 0:1], ACTF.Exp)
            a = DVE.run([a], dve.tensor_scalar, e[:, 1:2], e[:, 0:1], 1.0, None, ALU.add)
            a = DVE.run([a], dve.reciprocal, r[:, 0:1], e[:, 1:2])
            a = DVE.run([a], dve.tensor_tensor, r[:, 1:2], r[:, 0:1], e[:, 0:1], ALU.mult)
            w = [tiny(NE), tiny(NE)]
            for i in range(2):
                a = DVE.run([a, b], dve.tensor_scalar, w[i], table("iota8"), idx[:, i:i + 1], r[:, i:i + 1],
                            ALU.is_equal, ALU.mult)
            wt = DVE.run([a], dve.tensor_tensor, expert_w[:, t:2 * NE:2], w[0], w[1], ALU.add)
        bank_mark[3] = (a,)
        return [*marks, wt]

    def moe(marks):
        gate, up, down = (io[n][0].rearrange("(q z) r c -> q z r c", z=2) for n in ("moe_w_gate", "moe_w_up", "moe_w_down"))
        pair_rounds = 2 * FFN_UNITS // RAW
        base, sp_lap = st["load"], st["sp_lap"]
        with sp.Fori(0, NE // 2) as q:
            st["sp_lap"] = sp_lap + pair_rounds * q
            for z in range(2):
                ffn_load(*(lambda c, k, w=w: w[ds(q, 1), z, k * P:(k + 2) * P, ds(c * STEP_F, STEP_F)]
                           .rearrange("a (k p) n -> p (a k) n", p=P) for w in (gate, up)),
                         lambda c, f: down[ds(q, 1), z, ds(c * STEP_F + f * P, P), :].rearrange("a p n -> p (a n)"))
        st["load"], st["sp_lap"] = base + NE * FFN_UNITS, sp_lap
        zero_y([m for b in range(8) for m in bank_mark[b]])
        PE.need(*marks)
        DVE.need(*marks)
        g, u, split = ffn["g"], st["use"], st["split"]
        with nc.Fori(0, NE // 2, engines=compute) as q:
            for z in range(2):
                st["lap"] = pair_rounds * q
                ffn_steps(weight=lambda t: expert_w[:, ds(4 * q + 2 * z + t, 1)])
        st["lap"], st["split"], st["use"] = 0, split + NE * FFN_UNITS, u + NE * FFN_UNITS
        ffn["g"] = g + NE * STEPS
        add_ffn(close_y(), 1)

    def final_norm():
        fm = fetch("final_g_in", (final_g[:, :], io["final_norm_g"].rearrange("(a n) -> a n", a=1).to_broadcast([P, D])))
        ss = tiny(NT)
        sq = [ACT.run([x_mark[0]], act.activation, xn[:, t, :], x[:, t, :], ACTF.Square,
                      accum_out=ss[:, t:t + 1]) for t in range(NT)]
        r, m = rstd_of(ss, D, NT, sq)
        for t in range(NT):
            x_mark[0] = DVE.run([m, fm], dve.scalar_tensor_tensor, out=x[:, t, :], in0=x[:, t, :],
                                scalar=r[:, t:t + 1], in1=final_g[:, :], op0=ALU.mult, op1=ALU.mult)

    def ffn_2(name, layer):
        marks = normed(lambda k: col(f"{name}_norm_2", 8 * layer + k))
        gu, dn = io[f"{name}_w_gu_2"][layer], io[f"{name}_w_down_2"][layer]
        dense_ffn(lambda c, k: cols_of(gu, c, k), lambda c, k: cols_of(gu, c, k, FF),
                  lambda c, f: rows_of(dn, c, f), marks, factor=0.5)

    def block_1_ffn():
        marks = normed(lambda k: gain_cols[:, 8 + k:9 + k], lambda k: mod_cols[:, 16 + k:17 + k])
        dense_ffn(lambda c, k: cols_of(io["ffn_w_gate"][0], c, k), lambda c, k: cols_of(io["ffn_w_up"][0], c, k),
                  lambda c, f: rows_of(io["ffn_w_down"][0], c, f), marks, g=1)

    stages = [lambda: conditioning(0), lambda: hybrid_mixer(0), block_1_ffn,
              lambda: conditioning(1), lambda: hybrid_mixer(1), lambda: moe(route()), final_norm,
              lambda: ffn_2("ffn1", 0), even_mixer, lambda: ffn_2("ffn2", 0),
              lambda: ffn_2("ffn1", 1), odd_mixer, lambda: ffn_2("ffn2", 1)]
    for stage in stages[:upto]:
        stage()
    assert st["use"] == st["load"] == st["split"] == total, (st, total)
    store_x()


def tables_of_shapes():
    f = np.float32
    pos = np.arange(S)
    out = {"ident": np.eye(P, dtype=f)}
    causal = np.where(pos[None, :] <= pos[:, None], 0.0, -1e30).astype(f)
    out["causal"] = causal.reshape(NT, P, S).transpose(1, 0, 2)
    gamma = np.log(1.0 - 2.0 ** (-5.0 - np.arange(4, dtype=np.float64)))
    diff = pos[None, :] - np.arange(P)[:, None]
    out["decay"] = (np.where(diff >= 0, np.exp(np.maximum(diff, 0)[None] * gamma[:, None, None]), 0.0)
                    * P ** -0.5).astype(f).transpose(1, 0, 2)

    def angles(p, dim):
        inv = f(10000.0) ** (-np.arange(dim // 2, dtype=f) / f(dim // 2))
        ang = p.astype(f)[:, None] * inv.astype(f)[None, :]
        return [g(ang).astype(f).reshape(NT, P, dim // 2).transpose(1, 0, 2) for g in (np.cos, np.sin)]

    for name, dim in (("ret", 128), ("diff", 64), ("mla", 32)):
        out[name + "_cos"], out[name + "_sin"] = angles(pos, dim)
    row_angle, col_angle = angles(pos // 64, 32), angles(pos % 64, 32)
    for i, n in enumerate(("gqa_cos", "gqa_sin")):
        out[n] = np.concatenate([row_angle[i], col_angle[i]], axis=2)
    out["iota8"] = np.tile(np.arange(NE, dtype=f), (P, 1))
    return np.concatenate([np.ascontiguousarray(out[n]).reshape(P, -1) for n in TABLES], axis=1).astype(f)


def kernel(**inputs):
    import concourse.bacc as bacc
    from concourse.bass_utils import run_bass_kernel_spmd

    nc = bacc.Bacc("TRN2", target_bir_lowering=False, num_devices=1)
    arrays = {name: np.ascontiguousarray(a) for name, a in inputs.items()}
    arrays["tables"] = tables_of_shapes()
    io = {name: nc.dram_tensor(name, a.shape, mybir.dt.from_np(a.dtype), kind="ExternalInput").ap()
          for name, a in arrays.items()}
    out = nc.dram_tensor("out", (1, S, D), F32, kind="ExternalOutput").ap()
    program(nc, io, out)
    result = run_bass_kernel_spmd(nc, [arrays], core_ids=[0])
    return result.results[0]["out"]
```

```python
import numpy as np
import concourse.bass as bass
import concourse.mybir as mybir
from concourse.alu_op_type import AluOpType as ALU

F32 = mybir.dt.float32
F32R = mybir.dt.float32r
BF16 = mybir.dt.bfloat16
U32 = mybir.dt.uint32
ACTF = mybir.ActivationFunctionType
AX = mybir.AxisListType
ds = bass.ds

P = 128
S = 256
NT = S // P
D = 1024
KD = D // P
FF = 2816
STEP_F = 256
STEPS = FF // STEP_F
NE = 8
SLAB = 512
RAW, SPL = 12, 6
UNITS_GU, UNITS_D = 4, 2
FFN_UNITS = STEPS * (UNITS_GU + UNITS_D)
EPS = 1e-6
SLOTS = P

TABLES = {"ident": P, "causal": NT * S, "decay": 4 * S, "ret_cos": NT * 64, "ret_sin": NT * 64,
          "diff_cos": NT * 32, "diff_sin": NT * 32, "mla_cos": NT * 16, "mla_sin": NT * 16,
          "gqa_cos": NT * 32, "gqa_sin": NT * 32, "iota8": NE,
          "iota": P, "before": P}
COLUMNS = [("norm_mix_g", 16), ("norm_ffn_g", 16), ("ffn1_norm_2", 16), ("ffn2_norm_2", 16),
           ("ev_norm_2", 8), ("od_norm_2", 8), ("c", 8), ("att_out_g", 8), ("ret_out_g", 8),
           ("ev_b_s_2", 8), ("ev_sub_norm_2", 1), ("od_cq_norm_2", 2), ("od_ckv_norm_2", 1)]
ROWS = [("ev_q_norm_2", 64), ("ev_k_norm_2", 64), ("ev_sgu_norm_2", 512), ("od_mla_q_norm_2", 96),
        ("od_mla_k_norm_2", 96), ("od_gqa_q_norm_2", 64), ("od_gqa_k_norm_2", 64),
        ("ev_lam_q1_2", 64), ("ev_lam_k1_2", 64), ("ev_lam_q2_2", 64), ("ev_lam_k2_2", 64)]


class Rounds:

    def __init__(self, nc, queue, name, per_round):
        self.q, self.sem, self.per_round, self.count, self.round = queue, nc.alloc_semaphore(name), per_round, 0, 0

    def need(self, *marks):
        for sem, value in marks:
            self.q.wait_ge(sem, value)

    def run(self, marks, op, *args, **kw):
        self.need(*marks)
        return self.did(op(*args, **kw))

    def did(self, ins):
        ins.then_inc(self.sem, 1)
        self.count += 1
        return (self.sem, self.count + self.per_round * self.round)


class Engine:

    def __init__(self, nc, queue, name):
        self.q, self.sem, self.count, self.seen = queue, nc.alloc_semaphore(name), 0, {}

    def need(self, *marks):
        for sem, value in marks:
            if self.seen.get(sem.name, 0) < value:
                self.q.wait_ge(sem, value)
                self.seen[sem.name] = value

    def did(self, ins):
        ins.then_inc(self.sem, 1)
        self.count += 1
        return (self.sem, self.count)

    def run(self, marks, op, *args, **kw):
        self.need(*marks)
        return self.did(op(*args, **kw))


def program(nc, io, out, upto=13):
    sp, act, pe, dve = nc.sync, nc.scalar, nc.tensor, nc.vector
    SP, ACT, PE, DVE = (Engine(nc, q, n) for q, n in
                        ((sp, "sp_count"), (act, "act_count"), (pe, "pe_count"), (dve, "dve_count")))
    compute = (mybir.EngineType.Activation, mybir.EngineType.PE, mybir.EngineType.DVE)

    def sb(name, shape, dt=F32):
        return nc.alloc_sbuf_tensor(name, shape, dt)

    def over(name, shape, base, skip=0, dt=F32):
        return nc.alloc_sbuf_tensor_at(name, shape, dt, offset=base + skip)

    def sem(name):
        return nc.alloc_semaphore(name)

    raw = [sb(f"raw{i}", [P, 1024]) for i in range(RAW)]
    hi = [sb(f"hi{i}", [P, 1024], F32R) for i in range(SPL)]
    lo = [sb(f"lo{i}", [P, 1024], F32R) for i in range(SPL)]
    x = sb("x_res", [P, NT, D])
    gates = sb("gates", [P, 2, D])
    at_gates = nc.sbuf_base - 8192
    xn = sb("xn", [P, NT, D])
    at_xn = nc.sbuf_base - 8192
    aT = [sb("aT_hi", [P, KD, S], F32R), sb("aT_lo", [P, KD, S], F32R)]
    at = nc.sbuf_base
    proj = sb("proj", [P, NT, 3584])
    at_proj = at
    at = nc.sbuf_base
    qkT = sb("qkT", [P, 16, S])
    at_qkT = at
    at = nc.sbuf_base
    probs = sb("probs", [P, 2, NT * S])
    at_probs = at
    probsT = sb("probsT", [P, 2, NT * S])
    tables = sb("tables_sb", [P, sum(TABLES.values())])
    cols = sb("cols_sb", [P, P])
    rows = sb("rows", [P, sum(n for _, n in ROWS)])
    small = sb("small", [P, 256])
    gain_cols = sb("gain_cols", [P, 16])
    mod_cols = sb("mod_cols", [P, 32])
    zeros = sb("zeros", [1, SLAB], BF16)
    ones = sb("ones", [1, P])
    mod_rows = over("mod_rows", [P, 6 * D], at_proj)
    cs_wide = over("cs_wide", [P, KD, P], at_proj, 24 * 1024)
    silu_g = over("silu_g", [P, NT, STEP_F], at_proj)
    hid = over("hid", [P, NT, STEP_F], at_proj, 2048)
    hidT = [over("hidT_hi", [P, 2 * S], at_proj, 4096, F32R), over("hidT_lo", [P, 2 * S], at_proj, 6144, F32R)]
    cT = [over("cT_hi", [P, KD, P], at_qkT, 0, F32R), over("cT_lo", [P, KD, P], at_qkT, 4096, F32R)]
    vec_rows = over("vec_rows", [P, P], at_proj)
    bias_row = over("bias_row", [1, 2 * D], at_qkT, 8192)
    bias_ss2 = over("bias_ss2", [1, 2 * D], at_probs)
    rope_tmp = over("rope_tmp", [P, 2048], at_probs)
    k_full = over("k_full", [P, NT, 768], at_gates)
    probs_d = over("probs_d", [P, 4, NT * S], at_gates)
    gq_pairs = over("gq_pairs", [P, NT, 4, P], at_gates)
    expert_w = sb("expert_w", [P, 2 * NE + 2])
    top_idx = sb("top_idx", [P, 8], U32)
    xn_split = [over("xn_hi", [P, NT, D], at_proj, 8192, F32R), over("xn_lo", [P, NT, D], at_proj, 16384, F32R)]
    onehot = over("onehot", [P, 2, NT, P], at_proj, 24576, F32R)
    onehotT = over("onehotT", [P, 2 * NT * P], at_proj, 26624, F32R)
    x_full = over("x_full", [P, KD, P], at_probs, 4096)
    ysum = over("ysum", [P, NT, D], at_qkT)
    y_split = [over("y_hi", [P, D], at_qkT, 8192, F32R), over("y_lo", [P, D], at_qkT, 12288, F32R)]
    ones_sq = sb("ones_sq", [P, P])
    picked = sb("picked", [P, 2 * NE + 2])
    slot_of = sb("slot_of", [P, 2 * NE + 2])
    busiest = sb("busiest", [P, 1])
    busiest_i = sb("busiest_i", [P, 1], mybir.dt.int32)
    next_w = sb("next_w", [P, NT])
    slot_w = sb("slot_w", [P, 2])
    bias_g1 = over("bias_g1", [1, D], at_xn + 8192)
    bias_g2 = over("bias_g2", [1, D], at_xn)
    router = over("router_sb", [P, KD, NE], at_probs)
    hT_full = over("hT_full", [P, KD, S], at_qkT)
    w_s = over("w_s", [P, 8, P], at_probs)
    w_sT = over("w_sT", [P, 8, P], at_probs, 4096)
    final_g = over("final_g", [P, D], at_probs)
    psum = [nc.alloc_psum_tensor(f"bank{i}", [P, 512], F32) for i in range(8)]

    col_at, n = {}, 0
    for name, k in COLUMNS:
        col_at[name] = n
        n += k
    n_cols = n
    row_at, n = {}, 0
    for name, k in ROWS:
        row_at[name] = n
        n += k
    tab_at, n = {}, 0
    for name, k in TABLES.items():
        tab_at[name] = n
        n += k

    def table(name):
        return tables[:, tab_at[name]:tab_at[name] + TABLES[name]]

    def col(name, k):
        return cols[:, col_at[name] + k:col_at[name] + k + 1]

    def row(name):
        return rows[:, row_at[name]:row_at[name] + dict(ROWS)[name]]

    ident = table("ident")

    small_used = [0]

    def tiny(n):
        if small_used[0] + n > 256:
            small_used[0] = 0
        a = small[:, small_used[0]:small_used[0] + n]
        small_used[0] += n
        return a

    raw_full = [sem(f"raw_full{i}") for i in range(RAW)]
    hi_done, lo_done, unit_free = sem("hi_done"), sem("lo_done"), sem("unit_free")
    stage_units = [48, 36, FFN_UNITS, 48, 36, NE * FFN_UNITS, 0, FFN_UNITS, 28, FFN_UNITS, FFN_UNITS, 23, FFN_UNITS]
    total = sum(stage_units[:upto])
    st = {"load": 0, "split": 0, "use": 0, "lap": 0, "sp_lap": 0}

    def load(*parts):
        u, lap = st["load"], st["sp_lap"]
        st["load"] += 1
        slot = u % RAW
        if u >= RAW:
            sp.wait_ge(lo_done, u - RAW + 1 + 12 * lap)
        for dst, src in parts:
            sp.dma_start(dst(raw[slot]), src).then_inc(raw_full[slot], 32 // len(parts))

    def split_one():
        u, lap = st["split"], st["lap"]
        st["split"] += 1
        act.wait_ge(raw_full[u % RAW], 32 * (u // RAW + 1) + 32 * lap)
        if u >= SPL:
            act.wait_ge(unit_free, u - SPL + 1 + 12 * lap)
        act.activation(hi[u % SPL][:, :], raw[u % RAW][:, :], ACTF.Copy).then_inc(hi_done, 1)
        dve.wait_ge(hi_done, u + 1 + 12 * lap)
        dve.tensor_tensor(lo[u % SPL][:, :], raw[u % RAW][:, :], hi[u % SPL][:, :].bitcast(F32),
                          ALU.subtract).then_inc(lo_done, 1)

    def split_to(n):
        while st["split"] < min(n, total):
            split_one()

    def unit(u, k=2, width=512):
        return [s[u % SPL][:, 0:k * width].rearrange("p (k n) -> p k n", k=k) for s in (hi, lo)]

    def passes(bank, left, right, first, last):
        for n, (a, b) in enumerate(((0, 0), (0, 1), (1, 0))):
            ins = pe.matmul(bank, left[a], right[b], start=first and n == 0, stop=last and n == 2)
        return ins

    def proj_load(w, c0, width, kd=KD):
        v = w[:, c0:c0 + width].rearrange("(k p) n -> p k n", p=P)
        for k in range(0, kd, 2):
            load((lambda r: r[:, :].rearrange("p (k n) -> p k n", k=2)[:, :, 0:width], v[:, k:k + 2, :]))

    bank_mark = [()] * 8

    def slab(width, evacuate, marks=(), kd=KD):
        u = st["use"]
        n_units = kd // 2
        split_to(u + n_units)
        for t in range(NT):
            PE.need(*bank_mark[t])
            for j in range(n_units):
                if t == 0:
                    pe.wait_ge(lo_done, u + j + 1)
                w = unit(u + j)
                for kk in range(2):
                    k = 2 * j + kk
                    if t == 0 and marks:
                        PE.need(marks[k])
                    ins = passes(psum[t][:, 0:width], [a[:, k, t * P:(t + 1) * P] for a in aT],
                                 [r[:, kk, 0:width] for r in w], k == 0, k == kd - 1)
                if t == NT - 1:
                    ins.then_inc(unit_free, 1)
            if t == 0:
                mark0 = PE.did(ins)
                bank_mark[0] = evacuate(0, psum[0][:, 0:width], mark0)
                st["use"] += n_units
                split_to(u + n_units + 4)
        bank_mark[1] = evacuate(1, psum[1][:, 0:width], (unit_free, u + n_units))

    class Events:

        def __init__(self, name):
            self.gu, self.silu, self.hid = sem(name + "_gu"), sem(name + "_silu"), sem(name + "_hid")
            self.turned, self.hi, self.lo = sem(name + "_turned"), sem(name + "_hidT_hi"), sem(name + "_hidT_lo")

    ev_dense, ev_all, ev_slots = Events("dense"), Events("all_tokens"), Events("slots")
    ffn = {"g": 0, "ev": ev_dense}

    def pe_gate_up(t, u, g, lap, marks=()):
        if g > 0:
            pe.wait_ge(ffn["ev"].hid, 2 * (g - 1) + t + 1 + 4 * lap)
        for j in range(UNITS_GU):
            if t == 0:
                pe.wait_ge(lo_done, u + j + 1 + 12 * lap)
            w = unit(u + j)
            for kk in range(2):
                k = 2 * j + kk
                if marks:
                    PE.need(marks[k])
                ins = passes(psum[t][:, :], [a[:, k, t * P:(t + 1) * P] for a in aT],
                             [r[:, kk, :] for r in w], k == 0, k == KD - 1)
            if t == 1:
                ins.then_inc(unit_free, 1)
        if t == 0:
            ins.then_inc(ffn["ev"].gu, 1)

    def silu_mul(t, u_end, g, lap, weight):
        if t == 0:
            act.wait_ge(ffn["ev"].gu, g + 1 + 2 * lap)
        else:
            act.wait_ge(unit_free, u_end + 12 * lap)
        if g > 0:
            act.wait_ge(ffn["ev"].hid, 2 * (g - 1) + t + 1 + 4 * lap)
        act.activation(silu_g[:, t, :], psum[t][:, 0:STEP_F], ACTF.Silu).then_inc(ffn["ev"].silu, 1)
        dve.wait_ge(ffn["ev"].silu, 2 * g + t + 1 + 4 * lap)
        if g > 0:
            dve.wait_ge(ffn["ev"].turned, g + 2 * lap)
        up = psum[t][:, STEP_F:2 * STEP_F]
        if weight is None:
            ins = dve.tensor_tensor(hid[:, t, :], silu_g[:, t, :], up, ALU.mult)
        else:
            ins = dve.scalar_tensor_tensor(out=hid[:, t, :], in0=silu_g[:, t, :], scalar=weight(t),
                                           in1=up, op0=ALU.mult, op1=ALU.mult)
        ins.then_inc(ffn["ev"].hid, 1)

    def pe_turn(g, lap):
        pe.wait_ge(ffn["ev"].hid, 2 * g + 2 + 4 * lap)
        if g > 0:
            pe.wait_ge(ffn["ev"].lo, g + 2 * lap)
        for f in range(2):
            for t in range(NT):
                ins = pe.transpose(psum[2][:, f * S + t * P:f * S + (t + 1) * P],
                                   hid[:, t, f * P:(f + 1) * P], ident)
        ins.then_inc(ffn["ev"].turned, 1)

    def hidT_split(u_before, g, lap):
        act.wait_ge(ffn["ev"].turned, g + 1 + 2 * lap)
        act.wait_ge(unit_free, u_before + 12 * lap)
        act.activation(hidT[0][:, :], psum[2][:, :], ACTF.Copy).then_inc(ffn["ev"].hi, 1)
        dve.wait_ge(ffn["ev"].hi, g + 1 + 2 * lap)
        dve.tensor_tensor(hidT[1][:, :], psum[2][:, :], hidT[0][:, :].bitcast(F32),
                          ALU.subtract).then_inc(ffn["ev"].lo, 1)

    def pe_down(u, g, lap, last=False):
        pe.wait_ge(ffn["ev"].lo, g + 1 + 2 * lap)
        for f in range(2):
            pe.wait_ge(lo_done, u + f + 1 + 12 * lap)
            w = [s[(u + f) % SPL] for s in (hi, lo)]
            for t in range(NT):
                for half in range(2):
                    ins = passes(psum[4 + 2 * t + half][:, :],
                                 [a[:, f * S + t * P:f * S + (t + 1) * P] for a in hidT],
                                 [r[:, half * SLAB:(half + 1) * SLAB] for r in w], False,
                                 last and f == 1)
            ins.then_inc(unit_free, 1)

    def ffn_load(gate, up, down):
        def gu(c):
            for k in range(UNITS_GU):
                load((lambda r: r[:, :].rearrange("p (k n) -> p k n", k=2)[:, :, 0:STEP_F], gate(c, 2 * k)),
                     (lambda r: r[:, :].rearrange("p (k n) -> p k n", k=2)[:, :, STEP_F:], up(c, 2 * k)))

        def dn(c):
            for f in range(2):
                load((lambda r: r[:, :], down(c, f)))

        gu(0)
        base, lap = st["load"], st["sp_lap"]
        with sp.Fori(0, (STEPS - 1) // 2) as i:
            st["sp_lap"] = lap + i
            for b in range(2):
                gu(2 * i + b + 1)
                dn(2 * i + b)
        st["load"], st["sp_lap"] = base + 12 * ((STEPS - 1) // 2), lap
        dn(STEPS - 1)

    def look_ahead(n):
        for _ in range(n):
            if st["split"] < total:
                split_one()

    def zero_y(marks, banks=range(4, 8)):
        for mark in marks:
            pe.wait_ge(*mark)
        for b in banks:
            pe.matmul(psum[b][:, :], zeros[:, 0:P], zeros[:, :], start=True, stop=False)

    def close_y(counter, banks=range(4, 8)):
        for b in banks:
            ins = pe.matmul(psum[b][:, :], zeros[:, 0:P], zeros[:, :], start=False, stop=True)
        return counter.did(ins)

    def ffn_steps(marks=(), weight=None, final=False):
        g0, u0, lap = ffn["g"], st["use"], st["lap"]
        rounds = (STEPS - 1) // 2
        looped = rounds - 1 if final else rounds

        def step(g, u, lap):
            pe_gate_up(0, u, g, lap)
            silu_mul(1, u, g - 1, lap, weight)
            look_ahead(UNITS_D)
            pe_turn(g - 1, lap)
            hidT_split(u, g - 1, lap)
            pe_gate_up(1, u, g, lap)
            silu_mul(0, None, g, lap, weight)
            look_ahead(UNITS_GU)
            pe_down(u + UNITS_GU, g - 1, lap)

        def round_of(g, u, lap):
            for b in range(2):
                step(g + b, u + b * (UNITS_GU + UNITS_D), lap)

        pe_gate_up(0, u0, g0, lap, marks)
        silu_mul(0, None, g0, lap, weight)
        pe_gate_up(1, u0, g0, lap)
        look_ahead(UNITS_GU)
        g, u, split = g0 + 1, u0 + UNITS_GU, st["split"]
        with nc.Fori(0, looped, engines=compute) as i:
            st["lap"] = lap + i
            round_of(g, u, lap + i)
        st["lap"], st["split"] = lap, split + RAW * looped
        g, u = g + 2 * looped, u + RAW * looped
        if final:
            round_of(g, u, lap)
            g, u = g + 2, u + RAW
        silu_mul(1, u, g - 1, lap, weight)
        pe_turn(g - 1, lap)
        hidT_split(u, g - 1, lap)
        look_ahead(UNITS_D)
        pe_down(u, g - 1, lap)
        ffn["g"], st["use"] = g, u + UNITS_D


    x_mark = []
    mod_marks = []

    def fetch(name, *copies):
        landed = sem(name)
        ACT.need(*x_mark)
        for dst, src in copies:
            act.dma_start(dst, src).then_inc(landed, 16)
        return (landed, 16 * len(copies))

    def flat(name):
        v = io[name]
        return v.rearrange({1: "a -> a", 2: "a b -> (a b)", 3: "a b c -> (a b c)"}[len(v.shape)])

    start = fetch("small_in",
                  (tables[:, :], io["tables"]), (x[:, :, :], io["x"][0].rearrange("(t p) d -> p t d", p=P)),
                  *((vec_rows[col_at[n]:col_at[n] + k, :], flat(n).rearrange("(k p) -> k p", p=P)) for n, k in COLUMNS),
                  *((rows[:, row_at[n]:row_at[n] + k], flat(n).rearrange("(a n) -> a n", a=1).to_broadcast([P, k]))
                    for n, k in ROWS))
    z = DVE.did(dve.memset(zeros[:, :], 0.0))
    DVE.did(dve.memset(ones_sq[:, :], 1.0))
    DVE.did(dve.memset(expert_w[:, 2 * NE:], 0.0))
    o = DVE.did(dve.memset(ones[:, :], 1.0))
    PE.need(z, o, start)
    m = PE.did(pe.transpose(psum[3][:, 0:n_cols], vec_rows[0:n_cols, :], ident[0:n_cols, 0:n_cols]))
    cols_in = DVE.run([m], dve.tensor_copy, cols[:, 0:n_cols], psum[3][:, 0:n_cols])
    bank_mark[3] = (cols_in,)
    x_mark[:] = [start]

    def rstd_of(ss, n, width, marks):
        v, r = tiny(width), tiny(width)
        a = DVE.run(marks, dve.tensor_scalar, v, ss, 1.0 / n, EPS, ALU.mult, ALU.add)
        b = ACT.run([a], act.activation, v, v, ACTF.Sqrt)
        return r, DVE.run([b], dve.reciprocal, r, v)

    def turn_to_aT(src, nk, marks, gain, bias=None, full=None, free=()):
        PE.need(*marks)
        for b in range(4, 8):
            PE.need(*bank_mark[b])
        done = []
        for k0 in range(0, nk, 2):
            b = 4 + k0 // 2
            ks = range(k0, min(k0 + 2, nk))
            bank = {k: psum[b][:, (k - k0) * S:(k - k0 + 1) * S] for k in ks}
            for k in ks:
                for t in range(NT):
                    ins = pe.transpose(bank[k][:, t * P:(t + 1) * P], src(t, k), ident)
            m = PE.did(ins)
            if bias is None:
                for k in ks:
                    h = ACT.run([m, *free], act.activation, aT[0][:, k, :], bank[k], ACTF.Identity, scale=gain(k))
                for k in ks:
                    done.append(DVE.run([h], dve.scalar_tensor_tensor, out=aT[1][:, k, :], in0=bank[k],
                                        scalar=gain(k), in1=aT[0][:, k, :].bitcast(F32), op0=ALU.mult,
                                        op1=ALU.subtract))
                bank_mark[b] = (done[-1],)
            else:
                for k in ks:
                    a = DVE.run([m, *free], dve.tensor_scalar, full[:, k, :], bank[k], gain(k), bias(k),
                                ALU.mult, ALU.add)
                bank_mark[b] = (a,)
                for k in ks:
                    h = ACT.run([a], act.activation, aT[0][:, k, :], full[:, k, :], ACTF.Copy)
                    done.append(DVE.run([h], dve.tensor_tensor, aT[1][:, k, :], full[:, k, :],
                                        aT[0][:, k, :].bitcast(F32), ALU.subtract))
        return done

    def normed(gain, bias=None, free=()):
        ss = tiny(NT)
        sq = [ACT.run([x_mark[0], *free], act.activation, xn[:, t, :], x[:, t, :], ACTF.Square,
                      accum_out=ss[:, t:t + 1]) for t in range(NT)]
        r, m = rstd_of(ss, D, NT, sq)
        for t in range(NT):
            m = DVE.run([m], dve.tensor_scalar, xn[:, t, :], x[:, t, :], r[:, t:t + 1], None, ALU.mult)
        return turn_to_aT(lambda t, k: xn[:, t, k * P:(k + 1) * P], KD, [m], gain, bias,
                          hT_full if bias else None)

    def gated_add(t, half, bank, mark, gate=None, factor=1.0):
        xs = x[:, t, half * SLAB:(half + 1) * SLAB]
        if gate is None:
            x_mark[0] = DVE.run([mark, x_mark[0]], dve.scalar_tensor_tensor, out=xs, in0=bank,
                                scalar=factor, in1=xs, op0=ALU.mult, op1=ALU.add)
        else:
            tmp = xn[:, t, half * SLAB:(half + 1) * SLAB]
            a = DVE.run([mark], dve.tensor_tensor, tmp, bank,
                        gates[:, gate, half * SLAB:(half + 1) * SLAB], ALU.mult)
            x_mark[0] = DVE.run([a, x_mark[0]], dve.tensor_tensor, xs, xs, tmp, ALU.add)
        return (x_mark[0],)

    def add_ffn(mark, gate=None, factor=1.0):
        for t in range(NT):
            for half in range(2):
                b = 4 + 2 * t + half
                bank_mark[b] = gated_add(t, half, psum[b][:, :], mark, gate, factor)
        for b in range(3):
            bank_mark[b] = bank_mark[7]

    def dense_ffn(gate, up, down, marks, g=None, factor=1.0):
        final = st["use"] + FFN_UNITS == total
        ffn_load(gate, up, down)
        zero_y([m for b in range(4, 8) for m in bank_mark[b]])
        for b in range(3):
            PE.need(*bank_mark[b])
        ffn_steps(marks, final=final)
        add_ffn(close_y(PE), g, factor)

    def cols_of(w, c, k, c0=0):
        return w[k * P:(k + 2) * P, ds(c * STEP_F + c0, STEP_F)].rearrange("(k p) n -> p k n", p=P)

    def rows_of(w, c, f):
        return w[ds(c * STEP_F + f * P, P), :]

    mod_done = sem("mod_done")
    def conditioning(layer):
        w = io["ada_w"][layer]
        def load_round(c):
            for s in range(3):
                v = w[:, ds((3 * c + s) * SLAB, SLAB)].rearrange("(k p) n -> p k n", p=P)
                for k in range(0, KD, 2):
                    load((lambda r: r[:, :].rearrange("p (k n) -> p k n", k=2), v[:, k:k + 2, :]))
        n_rounds = 6 * D // SLAB // 3
        load_round(0)
        base, sp_lap = st["load"], st["sp_lap"]
        with sp.Fori(0, n_rounds - 1) as i:
            st["sp_lap"] = sp_lap + i
            load_round(i + 1)
        st["load"], st["sp_lap"] = base + 12 * (n_rounds - 1), sp_lap

        c8 = cols[:, col_at["c"]:col_at["c"] + KD]
        cs = tiny(KD)
        a = ACT.run([cols_in, x_mark[0]], act.activation, cs, c8, ACTF.Silu)
        a = DVE.run([a], dve.tensor_copy, cs_wide[:, :, :], cs.unsqueeze(2).to_broadcast([P, KD, P]))
        h = ACT.run([a, *bank_mark[0], *bank_mark[1]], act.activation, cT[0][:, :, :], cs_wide[:, :, :], ACTF.Copy)
        left_mark = DVE.run([h], dve.tensor_tensor, cT[1][:, :, :], cs_wide[:, :, :],
                            cT[0][:, :, :].bitcast(F32), ALU.subtract)
        ACT.need(x_mark[0])
        b_row = fetch(f"bias_in{layer}", *((dst[:, :], io["ada_b"][layer:layer + 1, D * c0:D * c1]) for dst, c0, c1 in
                      ((bias_row, 0, 2), (bias_g1, 2, 3), (bias_ss2, 3, 5), (bias_g2, 5, 6))))
        PE.need(left_mark)
        m0 = layer * 12
        def round_of(c, n, u, lap):
            for s in range(3):
                bank = psum[s]
                nn = m0 + n * 3 + s
                if nn >= 3:
                    pe.wait_ge(mod_done, nn - 2 + 3 * lap)
                for j in range(4):
                    pe.wait_ge(lo_done, u + 4 * s + j + 1 + 12 * lap)
                    wv = unit(u + 4 * s + j)
                    for kk in range(2):
                        k = 2 * j + kk
                        ins = passes(bank[:, :], [a[:, k, :] for a in cT], [r[:, kk, :] for r in wv],
                                     k == 0, k == KD - 1)
                    ins.then_inc(unit_free, 1)
                for _ in range(4):
                    split_one()
                act.wait_ge(unit_free, u + 4 * s + 4 + 12 * lap)
                act.activation(mod_rows[:, ds((3 * c + s) * SLAB, SLAB)], bank[:, :], ACTF.Copy).then_inc(mod_done, 1)
        for b in range(3):
            PE.need(*bank_mark[b])
        u = st["use"]
        split_to(u + 4)
        round_of(0, 0, u, st["lap"])
        split = st["split"]
        with nc.Fori(0, n_rounds - 1, engines=compute) as i:
            st["lap"] = i
            round_of(i + 1, 1, u + 12, i)
        st["lap"], st["split"] = 0, split + 12 * (n_rounds - 1)
        st["use"] = u + 12 * n_rounds
        rows_in = (mod_done, m0 + 12)
        PE.need(rows_in, b_row)
        PE.need(*bank_mark[3])
        for k in range(32):
            src = (k if k < 16 else k + 8) * P
            pe.matmul(psum[3][:, k:k + 1], mod_rows[0:1, src:src + P], ones[:, 0:1], start=True, stop=False)
            b = (bias_row if k < 16 else bias_ss2)[:, (k % 16) * P:(k % 16 + 1) * P]
            ins = pe.matmul(psum[3][:, k:k + 1], b, ones[:, 0:1], start=False, stop=True)
        m = PE.did(ins)
        cm = DVE.run([m], dve.tensor_copy, mod_cols[:, :], psum[3][:, 0:32])
        bank_mark[3] = (cm,)
        for b in range(4, 8):
            PE.need(*bank_mark[b])
        for g in range(2):
            for half in range(2):
                bank = psum[4 + 2 * g + half]
                br = (bias_g1, bias_g2)[g]
                m = PE.did(pe.matmul(bank[:, :], ones[:, :], br[:, half * SLAB:(half + 1) * SLAB],
                                     start=True, stop=True))
                src = (2 + 3 * g) * D + half * SLAB
                m = DVE.run([m, rows_in], dve.tensor_tensor, gates[:, g, half * SLAB:(half + 1) * SLAB],
                            bank[:, :], mod_rows[:, src:src + SLAB], ALU.add)
                bank_mark[4 + 2 * g + half] = (m,)
        mod_marks[:] = [m]
        for b in range(3):
            bank_mark[b] = (rows_in,)
        gm = DVE.run([cm], dve.scalar_tensor_tensor, out=gain_cols[:, 0:8], in0=mod_cols[:, 8:16], scalar=1.0,
                     in1=cols[:, col_at["norm_mix_g"] + 8 * layer:col_at["norm_mix_g"] + 8 * layer + 8],
                     op0=ALU.add, op1=ALU.mult)
        gm = DVE.run([gm], dve.scalar_tensor_tensor, out=gain_cols[:, 8:16], in0=mod_cols[:, 24:32], scalar=1.0,
                       in1=cols[:, col_at["norm_ffn_g"] + 8 * layer:col_at["norm_ffn_g"] + 8 * layer + 8],
                       op0=ALU.add, op1=ALU.mult)
        mod_marks.append(gm)

    def store_x():
        y = out[0].rearrange("(t p) d -> p t d", p=P)
        SP.need(x_mark[0])
        sp.dma_start(y, x[:, :, :]).then_inc(out_sem, 16)
        sp.wait_ge(out_sem, 16)
    out_sem = sem("out_stored")
    def project(w, width, marks, kd=KD, at=0, func=None):
        c = 0
        while c < width:
            n = min(SLAB, width - c)
            proj_load(w, c, n, kd)
            f = func(c) if func else None

            def out_of_bank(t, bank, mark, c=c, n=n, f=f):
                dst = proj[:, t, at + c:at + c + n]
                if f is not None or t == 0:
                    m = ACT.run([mark], act.activation, dst, bank, f or ACTF.Copy)
                else:
                    m = DVE.run([mark], dve.tensor_copy, dst, bank)
                out_marks.append(m)
                return (m,)
            slab(n, out_of_bank, marks, kd)
            marks = ()
            c += n

    def project_out(w, marks, gate=None):
        for half in range(2):
            proj_load(w, half * SLAB, SLAB)
            slab(SLAB, lambda t, bank, mark, half=half: gated_add(t, half, bank, mark, gate), marks)
            marks = ()

    def turn_heads(src, n, width, marks, at=0):
        done = []
        PE.need(*marks)
        for j in range(0, n, 2):
            b = 4 + (j // 2) % 4
            k = min(2, n - j)
            PE.need(*bank_mark[b])
            for jj in range(k):
                for t in range(NT):
                    ins = pe.transpose(psum[b][0:width, jj * S + t * P:jj * S + (t + 1) * P],
                                       src(t, j + jj), ident)
            m = PE.did(ins)
            dst = qkT[0:width, at + j:at + j + k, :].rearrange("p j s -> p (j s)")
            if (j // 2) % 2:
                m = ACT.run([m, *marks], act.activation, dst, psum[b][0:width, 0:k * S], ACTF.Copy)
            else:
                m = DVE.run([m, *marks], dve.tensor_copy, dst, psum[b][0:width, 0:k * S])
            bank_mark[b] = (m,)
            done.append(m)
        return done

    def rope(x1, x2, cos, sin, shape, marks):
        n = int(np.prod(shape[1:]))
        names = {3: "p (a b) -> p a b", 4: "p (a b c) -> p a b c"}[len(shape)]
        dims = dict(zip("abc", shape[1:]))
        tmp = [rope_tmp[:, i * n:(i + 1) * n].rearrange(names, **dims) for i in range(4)]
        a = [DVE.run(marks, dve.tensor_tensor, tmp[i], p, q, ALU.mult)
             for i, (p, q) in enumerate(((x1, cos), (x2, sin), (x1, sin), (x2, cos)))]
        DVE.run(a, dve.tensor_tensor, x1, tmp[0], tmp[1], ALU.subtract)
        return DVE.run(a, dve.tensor_tensor, x2, tmp[2], tmp[3], ALU.add)

    def group_norm(view, n, d, marks, gains=()):
        sq = xn[:, :, 0:n * d].rearrange("p t (n d) -> p t n d", n=n)
        a = [ACT.run(marks, act.activation, sq[:, t], view[:, t], ACTF.Square) for t in range(NT)]
        ss = tiny(NT * n)
        m = DVE.run(a, dve.reduce_sum, ss.rearrange("p (t n) -> p t n", t=NT), sq, axis=AX.X)
        r, m = rstd_of(ss, d, NT * n, [m])
        r = r.rearrange("p (t n) -> p t n", t=NT).unsqueeze(3).to_broadcast([P, NT, n, d])
        m = DVE.run([m], dve.tensor_tensor, view, view, r, ALU.mult)
        done = [m]
        for v, g in gains:
            done.append(DVE.run([m], dve.tensor_tensor, v, v, g, ALU.mult))
        return done

    def attention(n, width, q, k, v, scale, dst, marks, causal=False, pair=None):
        maps = 2 if pair is not None else 1
        bufs = [probs_d[:, i, :] for i in range(4)] if maps == 2 else [probs[:, i, :] for i in range(2)]
        rs, rr = tiny(NT * n * maps), tiny(NT * n * maps)
        nmax = tiny(2 * NT * maps)
        turned_of, pv_of, ready = {}, {}, {}

        def scores(h):
            for mp in range(maps):
                i = (h * maps + mp) % len(bufs)
                b = 4 + (h * maps + mp) % 2
                e = bufs[i].rearrange("p (t s) -> p t s", t=NT)
                PE.need(*bank_mark[b], *(marks if h == 0 else ()))
                for t in range(NT):
                    ins = pe.matmul(psum[b][:, t * S:(t + 1) * S], q(h, mp, t), k(h, mp), start=True, stop=True)
                m = PE.did(ins)
                sc = psum[b][:, :].rearrange("p (t s) -> p t s", t=NT)
                old = turned_of.get(h - len(bufs) // maps, ())
                nm = nmax[:, (i % (2 * maps)) * NT:(i % (2 * maps)) * NT + NT]
                olde = ready.get(h - 2, ())
                if causal:
                    m = DVE.run([m, *old], dve.scalar_tensor_tensor, out=e, in0=sc, scalar=scale,
                                in1=table("causal").rearrange("p (t s) -> p t s", t=NT), op0=ALU.mult, op1=ALU.add)
                    bank_mark[b] = (m,)
                    m = DVE.run([m, *olde], dve.tensor_reduce, nm, e, AX.X, ALU.max, negate=True)
                    src, k_scale = e, 1.0
                else:
                    m = DVE.run([m, *olde], dve.tensor_reduce, nm, sc, AX.X, ALU.max, negate=True)
                    m = DVE.run([m], dve.tensor_scalar, nm, nm, scale, None, ALU.mult)
                    src, k_scale = sc, scale
                ex = []
                for t in range(NT):
                    j = (t * maps + mp) * n + h
                    ex.append(ACT.run([m, *old], act.activation, e[:, t, :], src[:, t, :], ACTF.Exp,
                                      bias=nm[:, t:t + 1], scale=k_scale, accum_out=rs[:, j:j + 1]))
                if not causal:
                    bank_mark[b] = (ex[-1],)
                ready[h] = (*ready.get(h, ()), *ex) if mp else tuple(ex)
            if maps == 2:
                i = (h * 2) % len(bufs)
                w = []
                for t in range(NT):
                    j0, j1 = (t * 2) * n + h, (t * 2 + 1) * n + h
                    a0 = DVE.run(ready[h], dve.reciprocal, rr[:, j0:j0 + 1], rs[:, j0:j0 + 1])
                    a1 = DVE.run(ready[h], dve.reciprocal, rr[:, j1:j1 + 1], rs[:, j1:j1 + 1])
                    a1 = DVE.run([a1], dve.tensor_tensor, rr[:, j1:j1 + 1], rr[:, j1:j1 + 1], pair, ALU.mult)
                    e0, e1 = (bufs[i + z].rearrange("p (t s) -> p t s", t=NT)[:, t, :] for z in (0, 1))
                    a1 = DVE.run([a1], dve.tensor_scalar, e1, e1, rr[:, j1:j1 + 1], None, ALU.mult)
                    w.append(DVE.run([a0, a1], dve.scalar_tensor_tensor, out=e0, in0=e0,
                                     scalar=rr[:, j0:j0 + 1], in1=e1, op0=ALU.mult, op1=ALU.subtract))
                ready[h] = tuple(w)

        def turn(h):
            b = 2 + h % 2
            e = bufs[(h * maps) % len(bufs)]
            PE.need(*ready[h], *bank_mark[b])
            for kc in range(NT):
                for t in range(NT):
                    ins = pe.transpose(psum[b][:, kc * S + t * P:kc * S + (t + 1) * P],
                                       e[:, t * S + kc * P:t * S + (kc + 1) * P], ident)
            m = PE.did(ins)
            turned_of[h] = (m,)
            old = pv_of.get(h - 2, ())
            if causal:
                m = ACT.run([m, *old], act.activation, probsT[:, h % 2, :], psum[b][:, :], ACTF.Copy)
            else:
                m = DVE.run([m, *old], dve.tensor_copy, probsT[:, h % 2, :], psum[b][:, :])
            bank_mark[b] = (m,)

        def values(h):
            PE.need(*bank_mark[2 + h % 2])
            if h == 0:
                PE.need(*bank_mark[6], *bank_mark[7])
            for t in range(NT):
                last = t if causal else NT - 1
                for kc in range(last + 1):
                    ins = pe.matmul(psum[6 + t][:, h * width:(h + 1) * width],
                                    probsT[:, h % 2, kc * S + t * P:kc * S + (t + 1) * P], v(h, kc),
                                    start=kc == 0, stop=kc == last)
            pv_of[h] = (PE.did(ins),)

        for h in range(n + 2):
            if h < n:
                scores(h)
            if 1 <= h <= n:
                turn(h - 1)
            if h >= 2:
                values(h - 2)
        done = []
        if maps == 1:
            a = DVE.run(ready[n - 1], dve.reciprocal, rr, rs)
            for t in range(NT):
                r = rr[:, t * n:(t + 1) * n].unsqueeze(2).to_broadcast([P, n, width])
                m = DVE.run([a, *pv_of[n - 1]], dve.tensor_tensor,
                            dst(t).rearrange("p (n w) -> p n w", n=n),
                            psum[6 + t][:, 0:n * width].rearrange("p (n w) -> p n w", n=n), r, ALU.mult)
                bank_mark[6 + t] = (m,)
                done.append(m)
            return done
        return list(pv_of[n - 1])

    def bank_group_norm(n, d, dst, marks):
        ss = tiny(NT * n)
        a = [ACT.run(marks, act.activation, dst(t), psum[6 + t][:, 0:n * d], ACTF.Square) for t in range(NT)]
        s = [DVE.run([a[t]], dve.reduce_sum, ss[:, t * n:(t + 1) * n],
                     dst(t).rearrange("p (n d) -> p n d", n=n), axis=AX.X) for t in range(NT)]
        r, m = rstd_of(ss, d, NT * n, s)
        done = []
        for t in range(NT):
            rb = r[:, t * n:(t + 1) * n].unsqueeze(2).to_broadcast([P, n, d])
            m = DVE.run([m], dve.tensor_tensor, dst(t).rearrange("p (n d) -> p n d", n=n),
                        psum[6 + t][:, 0:n * d].rearrange("p (n d) -> p n d", n=n), rb, ALU.mult)
            bank_mark[6 + t] = (m,)
            done.append(m)
        return done

    out_marks = []

    def tab2(name, k):
        return table(name).rearrange("p (t k) -> p t k", t=NT)

    def hybrid_mixer(layer):
        marks = normed(lambda k: gain_cols[:, k:k + 1], lambda k: mod_cols[:, k:k + 1], mod_marks)
        del out_marks[:]
        project(io["w_in"][layer], 3584, marks)
        m = out_marks
        t8 = turn_heads(lambda t, j: proj[:, t, j * P:(j + 1) * P], 8, P, m[0:4])
        gate_silu = [ACT.run([*m], act.activation, proj[:, t, 3072:3584], proj[:, t, 3072:3584], ACTF.Silu)
                     for t in range(NT)]
        o_a = attention(8, 64, lambda h, mp, t: qkT[64 * (h % 2):64 * (h % 2) + 64, h // 2, t * P:(t + 1) * P],
                        lambda h, mp: qkT[64 * (h % 2):64 * (h % 2) + 64, 4 + h // 2, :],
                        lambda h, kc: proj[:, kc, 1024 + 64 * h:1024 + 64 * (h + 1)],
                        64 ** -0.5, lambda t: xn[:, t, 0:SLAB], [*t8, *m[4:6]], causal=True)
        ss = tiny(NT)
        a = [ACT.run([o_a[t]], act.activation, xn[:, t, SLAB:], xn[:, t, 0:SLAB], ACTF.Square,
                     accum_out=ss[:, t:t + 1]) for t in range(NT)]
        r, a2 = rstd_of(ss, SLAB, NT, a)
        o_a = [DVE.run([a2], dve.tensor_scalar, xn[:, t, 0:SLAB], xn[:, t, 0:SLAB], r[:, t:t + 1], None, ALU.mult)
               for t in range(NT)]
        rt = []
        for t in range(NT):
            v4 = proj[:, t, 1536:2560].rearrange("p (n d) -> p n d", n=8)
            c, s = (tab2(n, 64)[:, t, :].unsqueeze(1).to_broadcast([P, 8, 64]) for n in ("ret_cos", "ret_sin"))
            rt.append(rope(v4[:, :, 0:64], v4[:, :, 64:128], c, s, [P, 8, 64], [*m, *o_a, *rt]))
        t8 = turn_heads(lambda t, j: proj[:, t, 1536 + j * P:1536 + (j + 1) * P], 8, P, rt)
        pv = {}
        PE.need(*t8)

        def ret_scores(h):
            b = 4 + h % 2
            PE.need(*bank_mark[b])
            pe.matmul(psum[b][:, 0:S], qkT[:, 4 + h, 0:P], qkT[:, h, :], start=True, stop=True)
            mk = PE.did(pe.matmul(psum[b][:, S:S + P], qkT[:, 4 + h, P:S], qkT[:, h, P:S], start=True, stop=True))
            dec = table("decay").rearrange("p (h s) -> p h s", h=4)[:, h, :]
            a = DVE.run([mk, *pv.get(h - 2, ())], dve.tensor_tensor, probsT[:, h % 2, 0:S], psum[b][:, 0:S], dec, ALU.mult)
            a = DVE.run([mk], dve.tensor_tensor, probsT[:, h % 2, S:S + P], psum[b][:, S:S + P], dec[:, 0:P], ALU.mult)
            bank_mark[b] = (a,)
            return a

        def ret_values(h, mark):
            PE.need(mark, *bank_mark[6], *bank_mark[7]) if h == 0 else PE.need(mark)
            vr = [proj[:, kc, 2560 + h * P:2560 + (h + 1) * P] for kc in range(NT)]
            sT = probsT[:, h % 2, :]
            pe.matmul(psum[6][:, h * P:(h + 1) * P], sT[:, 0:P], vr[0], start=True, stop=True)
            pe.matmul(psum[7][:, h * P:(h + 1) * P], sT[:, P:S], vr[0], start=True, stop=False)
            pv[h] = (PE.did(pe.matmul(psum[7][:, h * P:(h + 1) * P], sT[:, S:S + P], vr[1], start=False, stop=True)),)

        mk = {0: ret_scores(0)}
        for h in range(4):
            if h < 3:
                mk[h + 1] = ret_scores(h + 1)
            ret_values(h, mk[h])
        o_r = bank_group_norm(4, P, lambda t: xn[:, t, SLAB:], [*pv[3], *o_a])
        o_r = [DVE.run([o_r[t], *gate_silu], dve.tensor_tensor, xn[:, t, SLAB:], xn[:, t, SLAB:],
                       proj[:, t, 3072:3584], ALU.mult) for t in range(NT)]
        marks = turn_to_aT(lambda t, k: xn[:, t, k * P:(k + 1) * P], KD, [*o_a, *o_r],
                           lambda k: col("att_out_g", 4 * layer + k) if k < 4 else col("ret_out_g", 4 * layer + k - 4))
        project_out(io["w_out"][layer], marks, gate=0)

    def even_mixer():
        marks = normed(lambda k: col("ev_norm_2", k))
        ws_in = fetch("w_s_in", (w_s[:, :, :], io["ev_w_s_2"][0].rearrange("g i j -> i g j")))
        del out_marks[:]
        project(io["ev_w_in_2"][0], 2560, marks, func=lambda c: ACTF.Gelu_apprx_tanh if c < 1024 else None)
        m = list(out_marks)
        PE.need(ws_in, *bank_mark[2], *bank_mark[3])
        for g in range(8):
            ins = pe.transpose(psum[2 + g // 4][:, (g % 4) * P:(g % 4 + 1) * P], w_s[:, g, :], ident)
        a = PE.did(ins)
        wT = [DVE.run([a], dve.tensor_copy, w_sT[:, 4 * i:4 * i + 4, :].rearrange("p g j -> p (g j)"), psum[2 + i][:, :])
              for i in range(2)]
        vv = proj[:, :, 512:1024].rearrange("p t (n d) -> p t n d", n=8)
        vn = group_norm(vv, 8, 64, m, [(proj[:, :, 512:1024], row("ev_sgu_norm_2").unsqueeze(1).to_broadcast([P, NT, 512]))])
        PE.need(*wT, *vn)
        for g in range(8):
            ins = pe.matmul(psum[2 + g // 4][:, (g % 4) * P:(g % 4 + 1) * P], w_sT[:, g, :],
                            proj[:, :, 512 + 64 * g:512 + 64 * (g + 1)], start=True, stop=True)
        a = PE.did(ins)
        qk = proj[:, :, 1024:2048].rearrange("p t (n d) -> p t n d", n=16)
        gains = []
        for i, g in enumerate(("ev_q_norm_2", "ev_k_norm_2")):
            for t in range(NT):
                gains.append((qk[:, t, 8 * i:8 * i + 8, :], row(g).unsqueeze(1).to_broadcast([P, 8, 64])))
        qn = group_norm(qk, 16, 64, m, gains)
        rt = []
        for t in range(NT):
            c, s = (tab2(n, 32)[:, t, :].unsqueeze(1).to_broadcast([P, 16, 32]) for n in ("diff_cos", "diff_sin"))
            rt.append(rope(qk[:, t, :, 0:32], qk[:, t, :, 32:64], c, s, [P, 16, 32], [*qn, *rt, a]))
        ga = []
        for g in range(8):
            mixed = psum[2 + g // 4][:, (g % 4) * P:(g % 4 + 1) * P].rearrange("p (t d) -> p t d", t=NT)
            ga.append(DVE.run([a, *qn], dve.scalar_tensor_tensor, out=xn[:, :, 64 * g:64 * (g + 1)], in0=mixed,
                              scalar=col("ev_b_s_2", g), in1=proj[:, :, 64 * g:64 * (g + 1)], op0=ALU.add, op1=ALU.mult))
        bank_mark[2] = bank_mark[3] = (ga[-1],)
        lam_init = 0.8 - 0.6 * float(np.exp(-0.3 * 0))
        lam, pr = tiny(2), xn[:, 0, SLAB:SLAB + P]
        for i in range(2):
            a = DVE.run([*qn], dve.tensor_tensor, pr[:, 64 * i:64 * (i + 1)], row(f"ev_lam_q{i + 1}_2"),
                        row(f"ev_lam_k{i + 1}_2"), ALU.mult)
        a = DVE.run([a], dve.reduce_sum, lam, pr.rearrange("p (i d) -> p i d", i=2), axis=AX.X)
        a = ACT.run([a], act.activation, lam, lam, ACTF.Exp)
        a = DVE.run([a], dve.tensor_tensor, lam[:, 0:1], lam[:, 0:1], lam[:, 1:2], ALU.subtract)
        a = DVE.run([a], dve.tensor_scalar, lam[:, 0:1], lam[:, 0:1], lam_init, None, ALU.add)
        t8 = turn_heads(lambda t, j: proj[:, t, 1024 + j * P:1024 + (j + 1) * P], 8, P, rt)
        pv = attention(4, P, lambda h, mp, t: qkT[64 * mp:64 * mp + 64, h, t * P:(t + 1) * P],
                       lambda h, mp: qkT[64 * mp:64 * mp + 64, 4 + h, :],
                       lambda h, kc: proj[:, kc, 2048 + h * P:2048 + (h + 1) * P], 64 ** -0.5, None,
                       [*t8, *m, a], pair=lam[:, 0:1])
        o_b = bank_group_norm(4, P, lambda t: xn[:, t, SLAB:], [*pv, a])
        sub = tiny(1)
        sm = DVE.run([cols_in], dve.tensor_scalar, sub, col("ev_sub_norm_2", 0), 1.0 - lam_init, None, ALU.mult)
        marks = turn_to_aT(lambda t, k: xn[:, t, k * P:(k + 1) * P], KD, [*ga, *o_b, sm],
                           lambda k: 1.0 if k < 4 else sub)
        project_out(io["ev_w_out_2"][0], marks)

    def odd_mixer():
        marks = normed(lambda k: col("od_norm_2", k))
        del out_marks[:]
        project(io["od_w_in_2"][0], 1184, marks)
        m = list(out_marks)
        CQ, CKV, KPE, GQ, GK, GV, UQ, UKV = 0, 256, 384, 416, 928, 1056, 1184, 1952
        ss = tiny(2 * NT)
        a = [ACT.run(m, act.activation, xn[:, t, SLAB + c0:SLAB + c0 + n], proj[:, t, c0:c0 + n], ACTF.Square,
                     accum_out=ss[:, NT * i + t:NT * i + t + 1])
             for i, (c0, n) in enumerate(((CQ, 256), (CKV, 128))) for t in range(NT)]
        cn = []
        for i, (c0, n) in enumerate(((CQ, 256), (CKV, 128))):
            r, mk = rstd_of(ss[:, NT * i:NT * (i + 1)], n, NT, a)
            for t in range(NT):
                cn.append(DVE.run([mk], dve.tensor_scalar, xn[:, t, c0:c0 + n], proj[:, t, c0:c0 + n],
                                  r[:, t:t + 1], None, ALU.mult))
        marks = turn_to_aT(lambda t, k: xn[:, t, k * P:(k + 1) * P], 3, cn,
                           lambda k: col("od_cq_norm_2", k) if k < 2 else col("od_ckv_norm_2", 0))
        project(io["od_w_uq_2"][0], 768, marks, kd=2, at=UQ)
        load((lambda r: r[:, :], io["od_w_ukv_2"][0]))
        u = st["use"]
        split_to(u + 1)
        PE.need(marks[2])
        pe.wait_ge(lo_done, u + 1)
        kvm = []
        for i in range(4):
            half, t = i // 2, i % 2
            PE.need(*bank_mark[i])
            ins = passes(psum[i][:, :], [z[:, 2, t * P:(t + 1) * P] for z in aT],
                         [z[:, half * SLAB:(half + 1) * SLAB] for z in unit(u, 1, 1024)[0:2]]
                         if False else [z[u % SPL][:, half * SLAB:(half + 1) * SLAB] for z in (hi, lo)], True, True)
            if i < 3:
                mk = PE.did(ins)
            else:
                ins.then_inc(unit_free, 1)
                mk = (unit_free, u + 1)
                st["use"] += 1
            dst = proj[:, t, UKV + half * SLAB:UKV + (half + 1) * SLAB]
            kvm.append(ACT.run([mk], act.activation, dst, psum[i][:, :], ACTF.Copy) if t == 0 else
                       DVE.run([mk], dve.tensor_copy, dst, psum[i][:, :]))
            bank_mark[i] = (kvm[-1],)
        split_to(u + 1 + 4)
        m2 = [*out_marks, *kvm]
        kf = k_full[:, :, :].rearrange("p t (n d) -> p t n d", n=8)
        kv = proj[:, :, UKV:UKV + 1024].rearrange("p t (n d) -> p t n d", n=8)
        km = []
        for t in range(NT):
            km.append(DVE.run(m2, dve.tensor_copy, kf[:, t, :, 0:64], kv[:, t, :, 0:64]))
            km.append(ACT.run(m2, act.activation, kf[:, t, :, 64:96],
                              proj[:, t, KPE:KPE + 32].unsqueeze(1).to_broadcast([P, 8, 32]), ACTF.Copy))
        qv = proj[:, :, UQ:UQ + 768].rearrange("p t (n d) -> p t n d", n=8)
        rt, prev = [], m2
        for v, g in ((qv, "od_mla_q_norm_2"), (kf, "od_mla_k_norm_2")):
            gn = group_norm(v, 8, 96, [*prev, *km], [(v[:, t], row(g).unsqueeze(1).to_broadcast([P, 8, 96])) for t in range(NT)])
            for t in range(NT):
                c, s = (tab2(n, 16)[:, t, :].unsqueeze(1).to_broadcast([P, 8, 16]) for n in ("mla_cos", "mla_sin"))
                rt.append(rope(v[:, t, :, 64:80], v[:, t, :, 80:96], c, s, [P, 8, 16], [*gn, *rt]))
            prev = rt
        gv = proj[:, :, GQ:GV].rearrange("p t (n d) -> p t n d", n=10)
        gn = group_norm(gv, 10, 64, [*m, *rt],
                        [(gv[:, t, a0:a1], row(g).unsqueeze(1).to_broadcast([P, a1 - a0, 64])) for t in range(NT)
                         for a0, a1, g in ((0, 8, "od_gqa_q_norm_2"), (8, 10, "od_gqa_k_norm_2"))])
        for t in range(NT):
            for part in range(2):
                c, s = (tab2(n, 32)[:, t, 16 * part:16 * part + 16].unsqueeze(1).to_broadcast([P, 10, 16])
                        for n in ("gqa_cos", "gqa_sin"))
                o = 32 * part
                rt.append(rope(gv[:, t, :, o:o + 16], gv[:, t, :, o + 16:o + 32], c, s, [P, 10, 16], [*gn, *rt]))
        tq = turn_heads(lambda t, j: qv[:, t, j, :], 8, 96, rt)
        tk = turn_heads(lambda t, j: kf[:, t, j, :], 8, 96, rt, at=8)
        o_c = attention(8, 64, lambda h, mp, t: qkT[0:96, h, t * P:(t + 1) * P], lambda h, mp: qkT[0:96, 8 + h, :],
                        lambda h, kc: kv[:, kc, h, 64:128], 96 ** -0.5, lambda t: xn[:, t, 0:SLAB], [*tq, *tk, *m2])
        tq = turn_heads(lambda t, j: gq_pairs[:, t, j, :], 4, P, repack(gv, rt))
        tk = turn_heads(lambda t, j: proj[:, t, GK:GK + P], 1, P, rt, at=4)
        o_d = attention(8, 64, lambda h, mp, t: qkT[64 * (h // 4):64 * (h // 4) + 64, h % 4, t * P:(t + 1) * P],
                        lambda h, mp: qkT[64 * (h // 4):64 * (h // 4) + 64, 4, :],
                        lambda h, kc: proj[:, kc, GV + 64 * (h // 4):GV + 64 * (h // 4) + 64], 64 ** -0.5,
                        lambda t: xn[:, t, SLAB:], [*tq, *tk, *o_c])
        marks = turn_to_aT(lambda t, k: xn[:, t, k * P:(k + 1) * P], KD, [*o_c, *o_d], lambda k: 1.0)
        project_out(io["od_w_out_2"][0], marks)

    def repack(gv, marks):
        src = gv[:, :, 0:8, :]
        return [DVE.run(marks, dve.tensor_copy, gq_pairs[:, t, :, :].rearrange("p c (r d) -> p c r d", r=2),
                        src[:, t].rearrange("p (r c) d -> p c r d", r=2)) for t in range(NT)]

    def route():
        rm = fetch("router_in", (router[:, :, :], io["router_w"][0].rearrange("(k p) e -> p k e", p=P)))
        marks = normed(lambda k: gain_cols[:, 8 + k:9 + k], lambda k: mod_cols[:, 16 + k:17 + k])
        PE.need(rm, *marks, *bank_mark[3])
        for t in range(NT):
            for k in range(KD):
                ins = pe.matmul(psum[3][:, t * NE:(t + 1) * NE], hT_full[:, k, t * P:(t + 1) * P],
                                router[:, k, :], start=k == 0, stop=k == KD - 1)
        m = PE.did(ins)
        for t in range(NT):
            lg, top, idx = tiny(NE), tiny(NE), tiny(NE)
            a = DVE.run([m], dve.tensor_copy, lg, psum[3][:, t * NE:(t + 1) * NE])
            b = DVE.run([a], dve.max, top, lg)
            iu = top_idx[:, :]
            b = DVE.run([b], dve.max_index, iu, top, lg)
            b = DVE.run([b], dve.tensor_copy, idx, iu)
            e, r = tiny(2), tiny(2)
            a = DVE.run([b], dve.tensor_tensor, e[:, 0:1], top[:, 1:2], top[:, 0:1], ALU.subtract)
            a = ACT.run([a], act.activation, e[:, 0:1], e[:, 0:1], ACTF.Exp)
            a = DVE.run([a], dve.tensor_scalar, e[:, 1:2], e[:, 0:1], 1.0, None, ALU.add)
            a = DVE.run([a], dve.reciprocal, r[:, 0:1], e[:, 1:2])
            a = DVE.run([a], dve.tensor_tensor, r[:, 1:2], r[:, 0:1], e[:, 0:1], ALU.mult)
            w = [tiny(NE), tiny(NE)]
            for i in range(2):
                a = DVE.run([a, b], dve.tensor_scalar, w[i], table("iota8"), idx[:, i:i + 1], r[:, i:i + 1],
                            ALU.is_equal, ALU.mult)
            wt = DVE.run([a], dve.tensor_tensor, expert_w[:, t:2 * NE:2], w[0], w[1], ALU.add)
        bank_mark[3] = (a,)
        a = DVE.run([wt], dve.tensor_scalar, picked[:, :], expert_w[:, :], 0.0, None, ALU.is_gt)
        PE.need(a)
        for c0, terms in ((16, (("before", 0),)), (24, ((None, 0), ("before", 1))), (32, ((None, 0), (None, 1)))):
            for n, (left, t) in enumerate(terms):
                ins = pe.matmul(psum[3][:, c0:c0 + NE], table(left) if left else ones_sq[:, :],
                                picked[:, t:2 * NE:2], start=n == 0, stop=n == len(terms) - 1)
        m = PE.did(ins)
        for t in range(NT):
            DVE.run([m], dve.scalar_tensor_tensor, out=slot_of[:, t:2 * NE:2], in0=psum[3][:, 16 + 8 * t:24 + 8 * t],
                    scalar=1.0, in1=picked[:, t:2 * NE:2], op0=ALU.add, op1=ALU.mult)
        DVE.run([m], dve.memset, slot_of[:, 2 * NE:], 0.0)
        a = DVE.run([m], dve.reduce_max, busiest[:, :], psum[3][:, 32:32 + NE], axis=AX.X)
        bank_mark[3] = (a,)
        b = DVE.run([a], dve.tensor_scalar, slot_of[:, :], slot_of[:, :], 1.0, None, ALU.subtract)
        b = DVE.run([b], dve.tensor_copy, busiest_i[:, :], busiest[:, :])
        return [*marks, wt, b]

    def moe(marks):
        gate, up, down = (io[n][0].rearrange("(q z) r c -> q z r c", z=2) for n in ("moe_w_gate", "moe_w_up", "moe_w_down"))
        pair_rounds = 2 * FFN_UNITS // RAW
        base, sp_lap = st["load"], st["sp_lap"]
        with sp.Fori(0, NE // 2) as q:
            st["sp_lap"] = sp_lap + pair_rounds * q
            for z in range(2):
                ffn_load(*(lambda c, k, w=w: w[ds(q, 1), z, k * P:(k + 2) * P, ds(c * STEP_F, STEP_F)]
                           .rearrange("a (k p) n -> p (a k) n", p=P) for w in (gate, up)),
                         lambda c, f: down[ds(q, 1), z, ds(c * STEP_F + f * P, P), :].rearrange("a p n -> p (a n)"))
        st["load"], st["sp_lap"] = base + NE * FFN_UNITS, sp_lap
        marks = [*marks, *(m for b in range(8) for m in bank_mark[b])]
        for e in (PE, ACT, DVE):
            e.need(*marks)
        most = nc.values_load(busiest_i[0:1, 0:1], engines=compute, min_val=0, max_val=S)
        before = dict(st)
        with nc.If(most > SLOTS):
            experts_on_all_tokens(pair_rounds)
        after = dict(st)
        st.update(before)
        with nc.Else():
            experts_on_slots(pair_rounds)
        assert st == after
        ffn["ev"] = ev_dense
        for b in range(8):
            bank_mark[b] = ()
        for t in range(NT):
            a = DVE.run([], dve.tensor_tensor, xn[:, t, :], ysum[:, t, :], gates[:, 1, :], ALU.mult)
            x_mark[0] = DVE.run([a, x_mark[0]], dve.tensor_tensor, x[:, t, :], x[:, t, :], xn[:, t, :], ALU.add)
        for b in range(8):
            bank_mark[b] = (x_mark[0],)

    def experts_on_all_tokens(pair_rounds):
        g0, ffn["g"], ffn["ev"] = ffn["g"], 0, ev_all
        u, split = st["use"], st["split"]
        pe_end, dve_end = Rounds(nc, pe, "all_pe_end", 1), Rounds(nc, dve, "all_dve_end", 4)
        zero_y([])
        with nc.Fori(0, NE // 2, engines=compute) as q:
            for z in range(2):
                st["lap"] = pair_rounds * q
                ffn_steps(weight=lambda t: expert_w[:, ds(4 * q + 2 * z + t, 1)])
        st["lap"], st["split"], st["use"] = 0, split + NE * FFN_UNITS, u + NE * FFN_UNITS
        ffn["g"] = g0
        m = close_y(pe_end)
        for t in range(NT):
            for half in range(2):
                m2 = dve_end.run([m], dve.tensor_copy, ysum[:, t, half * SLAB:(half + 1) * SLAB],
                                 psum[4 + 2 * t + half][:, :])
        dve_end.need(m2)

    def experts_on_slots(pair_rounds):
        ev = ev_slots
        once = Rounds(nc, act, "slots_xn_hi", 4), Rounds(nc, dve, "slots_xn_lo", 2)

        h = once[0].run([], act.activation, xn_split[0][:, :, :], xn[:, :, :], ACTF.Copy)
        m = once[1].run([h], dve.tensor_tensor, xn_split[1][:, :, :], xn[:, :, :],
                        xn_split[0][:, :, :].bitcast(F32), ALU.subtract)
        zero = once[1].run([], dve.memset, ysum[:, :, :], 0.0)
        pe.wait_ge(*m)
        dve.wait_ge(*zero)
        act.wait_ge(*zero)

        def gate_up(j0, u, g, lap, z):
            if j0 == 0 and g > 1:
                pe.wait_ge(ev.hid, g - 1 + 2 * lap)
            for j in (j0, j0 + 1):
                pe.wait_ge(lo_done, u + j + 1 + 12 * lap)
                w = unit(u + j)
                for kk in range(2):
                    k = 2 * j + kk
                    ins = passes(psum[g % 2][:, :], [a[:, k, z * P:(z + 1) * P] for a in aT],
                                 [r[:, kk, :] for r in w], k == 0, k == KD - 1)
                ins.then_inc(unit_free, 1)

        def hidden(u_end, g, lap):
            act.wait_ge(unit_free, u_end + 12 * lap)
            if g > 1:
                act.wait_ge(ev.hid, g - 1 + 2 * lap)
            act.activation(silu_g[:, g % 2, :], psum[g % 2][:, 0:STEP_F], ACTF.Silu).then_inc(ev.silu, 1)
            dve.wait_ge(ev.silu, g + 1 + 2 * lap)
            if g > 1:
                dve.wait_ge(ev.turned, g - 1 + 2 * lap)
            dve.tensor_tensor(hid[:, g % 2, :], silu_g[:, g % 2, :], psum[g % 2][:, STEP_F:], ALU.mult)\
               .then_inc(ev.hid, 1)

        def turn(g, lap):
            pe.wait_ge(ev.hid, g + 1 + 2 * lap)
            if g > 0:
                pe.wait_ge(ev.lo, g + 2 * lap)
            for f in range(2):
                ins = pe.transpose(psum[2][:, f * P:(f + 1) * P], hid[:, g % 2, f * P:(f + 1) * P], ident)
            ins.then_inc(ev.turned, 1)

        def turned_split(u_before, g, lap):
            act.wait_ge(ev.turned, g + 1 + 2 * lap)
            act.wait_ge(unit_free, u_before + 12 * lap)
            act.activation(hidT[0][:, 0:S], psum[2][:, 0:S], ACTF.Copy).then_inc(ev.hi, 1)
            dve.wait_ge(ev.hi, g + 1 + 2 * lap)
            dve.tensor_tensor(hidT[1][:, 0:S], psum[2][:, 0:S], hidT[0][:, 0:S].bitcast(F32),
                              ALU.subtract).then_inc(ev.lo, 1)

        def down(u, g, lap):
            pe.wait_ge(ev.lo, g + 1 + 2 * lap)
            for f in range(2):
                pe.wait_ge(lo_done, u + f + 1 + 12 * lap)
                for half in range(2):
                    ins = passes(psum[4 + half][:, :], [a[:, f * P:(f + 1) * P] for a in hidT],
                                 [s[(u + f) % SPL][:, half * SLAB:(half + 1) * SLAB] for s in (hi, lo)], False, False)
                ins.then_inc(unit_free, 1)

        def one_hots(V, z, c):
            V.run([], dve.tensor_copy, next_w[:, :], expert_w[:, c(0, 2)])
            for t in range(NT):
                m = V.run([], dve.tensor_scalar, onehot[:, z, t, :], table("iota"), slot_of[:, c(t, 1)], None,
                          ALU.is_equal)
            return m

        def turn_one_hots(B, z, m):
            B.need(m)
            for t in range(NT):
                pe.transpose(psum[3][:, t * P:(t + 1) * P], onehot[:, z, t, :].bitcast(F32), ident)
            for t in range(NT):
                ins = pe.matmul(psum[3][:, S:S + 1], onehot[:, z, t, :].bitcast(F32), next_w[:, t:t + 1],
                                start=t == 0, stop=t == 1)
            return B.did(ins)

        def keep_turned(A, z, m):
            A.run([m], act.activation, slot_w[:, z:z + 1], psum[3][:, S:S + 1], ACTF.Copy)
            return A.run([m], act.activation, onehotT[:, z * S:(z + 1) * S], psum[3][:, 0:S], ACTF.Copy)

        def gather(B, z):
            for k in range(KD):
                for n, (t, part) in enumerate(((0, 0), (0, 1), (1, 0), (1, 1))):
                    ins = pe.matmul(psum[6 + k // 4][:, (k % 4) * P:(k % 4 + 1) * P],
                                    xn_split[part][:, t, k * P:(k + 1) * P], onehot[:, z, t, :],
                                    start=n == 0, stop=n == 3)
            return B.did(ins)

        def modulate(A, V, z, m):
            V.need(m)
            for k in range(KD):
                f = V.run([], dve.tensor_scalar, x_full[:, k, :], psum[6 + k // 4][:, (k % 4) * P:(k % 4 + 1) * P],
                          gain_cols[:, 8 + k:9 + k], mod_cols[:, 16 + k:17 + k], ALU.mult, ALU.add)
            h = A.run([f], act.activation, aT[0][:, :, z * P:(z + 1) * P], x_full[:, :, :], ACTF.Copy)
            return V.run([h], dve.tensor_tensor, aT[1][:, :, z * P:(z + 1) * P], x_full[:, :, :],
                         aT[0][:, :, z * P:(z + 1) * P].bitcast(F32), ALU.subtract)

        def weigh(A, V, z, y_mark):
            for half in range(2):
                part = slice(half * SLAB, (half + 1) * SLAB)
                h = A.run([y_mark], act.activation, y_split[0][:, part], psum[4 + half][:, :], ACTF.Identity,
                          scale=slot_w[:, z:z + 1])
                m = V.run([h], dve.scalar_tensor_tensor, out=y_split[1][:, part], in0=psum[4 + half][:, :],
                          scalar=slot_w[:, z:z + 1], in1=y_split[0][:, part].bitcast(F32), op0=ALU.mult,
                          op1=ALU.subtract)
            return m

        def give_back(B, V, z, m, spare):
            B.need(m)
            done = []
            for t, banks in enumerate(((6, 7), spare)):
                for half in range(2):
                    for part in range(2):
                        ins = pe.matmul(psum[banks[half]][:, :], onehotT[:, z * S + t * P:z * S + (t + 1) * P],
                                        y_split[part][:, half * SLAB:(half + 1) * SLAB], start=part == 0, stop=part == 1)
                given = B.did(ins)
                for half in range(2):
                    ys = ysum[:, t, half * SLAB:(half + 1) * SLAB]
                    m = V.run([given], dve.tensor_tensor, ys, ys, psum[banks[half]][:, :], ALU.add)
                done.append(m)
            return given, done

        A0, B0, V0 = Rounds(nc, act, "first_act", 3), Rounds(nc, pe, "first_pe", 2), Rounds(nc, dve, "first_dve", 12)
        m = turn_one_hots(B0, 0, one_hots(V0, 0, lambda t, n: slice(t, t + n)))
        kept = keep_turned(A0, 0, m)
        ready = modulate(A0, V0, 0, gather(B0, 0))
        B0.need(kept, ready)

        per_expert = {"act": 2 + 1 + 2, "pe": 1 + 1 + 2 + 1, "dve": 3 + 2 * NT + KD + 1 + 2}
        A, B, V = (Rounds(nc, q, "slots_" + n, 2 * per_expert[n]) for q, n in ((act, "act"), (pe, "pe"), (dve, "dve")))
        u, split = st["use"], st["split"]
        zy = [once[0].run([], act.activation, y_split[i][:, :], ysum[:, :, :].rearrange("p t d -> p (t d)")[:, 0:D], ACTF.Copy)
              for i in range(2)]
        zo = once[0].run([], act.activation, onehotT[:, S:2 * S], ysum[:, 0, 0:S], ACTF.Copy)
        pe.wait_ge(*zo)
        with nc.Fori(0, NE // 2, engines=compute) as q:
            for r in (A, B, V):
                r.count, r.round = 0, q
            lap = pair_rounds * q
            st["lap"] = lap
            for z in range(2):
                g, un = STEPS * z, u + FFN_UNITS * z
                next_hot = one_hots(V, 1 - z, lambda t, n: ds(4 * q + 2 * (z + 1) + t, n))
                gate_up(0, un, g, lap, z)
                gate_up(2, un, g, lap, z)
                turned = turn_one_hots(B, 1 - z, next_hot)
                given, back = give_back(B, V, 1 - z, weighed if z else (V.sem, 3 + V.per_round * q), ((g + 1) % 2, 2))
                look_ahead(UNITS_GU)
                A.need(given)
                keep_turned(A, 1 - z, turned)
                B.need(back[0])
                got = gather(B, 1 - z)
                B.need(back[1])
                zero_y([], (4, 5))
                g, un = g + 1, un + UNITS_GU
                ready = modulate(A, V, 1 - z, got)
                here = st["split"]
                with nc.Fori(0, (STEPS - 1) // 2, engines=compute) as i:
                    for b in range(2):
                        gg, uu, ll = g + b, un + 6 * b, lap + i
                        st["lap"] = ll
                        gate_up(0, uu, gg, ll, z)
                        hidden(uu, gg - 1, ll)
                        turn(gg - 1, ll)
                        look_ahead(UNITS_D)
                        turned_split(uu, gg - 1, ll)
                        gate_up(2, uu, gg, ll, z)
                        look_ahead(UNITS_GU)
                        down(uu + UNITS_GU, gg - 1, ll)
                st["lap"], st["split"] = lap, here + RAW * (STEPS - 1) // 2
                g, un = g + STEPS - 1, un + 6 * (STEPS - 1)
                hidden(un, g - 1, lap)
                turn(g - 1, lap)
                turned_split(un, g - 1, lap)
                look_ahead(UNITS_D)
                down(un, g - 1, lap)
                B.need(ready)
                weighed = weigh(A, V, z, close_y(B, (4, 5)))
            for r in (A, B, V):
                assert r.count == r.per_round, (r.sem.name, r.count)
        Bl, Vl = Rounds(nc, pe, "last_pe", 2), Rounds(nc, dve, "last_dve", 4)
        V.round, V.count = NE // 2 - 1, V.per_round
        _, back = give_back(Bl, Vl, 1, (V.sem, V.per_round * (NE // 2)), (1, 2))
        Vl.need(back[1])
        st["lap"], st["split"], st["use"] = 0, split + NE * FFN_UNITS, u + NE * FFN_UNITS

    def final_norm():
        fm = fetch("final_g_in", (final_g[:, :], io["final_norm_g"].rearrange("(a n) -> a n", a=1).to_broadcast([P, D])))
        ss = tiny(NT)
        sq = [ACT.run([x_mark[0]], act.activation, xn[:, t, :], x[:, t, :], ACTF.Square,
                      accum_out=ss[:, t:t + 1]) for t in range(NT)]
        r, m = rstd_of(ss, D, NT, sq)
        for t in range(NT):
            x_mark[0] = DVE.run([m, fm], dve.scalar_tensor_tensor, out=x[:, t, :], in0=x[:, t, :],
                                scalar=r[:, t:t + 1], in1=final_g[:, :], op0=ALU.mult, op1=ALU.mult)

    def ffn_2(name, layer):
        marks = normed(lambda k: col(f"{name}_norm_2", 8 * layer + k))
        gu, dn = io[f"{name}_w_gu_2"][layer], io[f"{name}_w_down_2"][layer]
        dense_ffn(lambda c, k: cols_of(gu, c, k), lambda c, k: cols_of(gu, c, k, FF),
                  lambda c, f: rows_of(dn, c, f), marks, factor=0.5)

    def block_1_ffn():
        marks = normed(lambda k: gain_cols[:, 8 + k:9 + k], lambda k: mod_cols[:, 16 + k:17 + k])
        dense_ffn(lambda c, k: cols_of(io["ffn_w_gate"][0], c, k), lambda c, k: cols_of(io["ffn_w_up"][0], c, k),
                  lambda c, f: rows_of(io["ffn_w_down"][0], c, f), marks, g=1)

    stages = [lambda: conditioning(0), lambda: hybrid_mixer(0), block_1_ffn,
              lambda: conditioning(1), lambda: hybrid_mixer(1), lambda: moe(route()), final_norm,
              lambda: ffn_2("ffn1", 0), even_mixer, lambda: ffn_2("ffn2", 0),
              lambda: ffn_2("ffn1", 1), odd_mixer, lambda: ffn_2("ffn2", 1)]
    for stage in stages[:upto]:
        stage()
    assert st["use"] == st["load"] == st["split"] == total, (st, total)
    store_x()


def tables_of_shapes():
    f = np.float32
    pos = np.arange(S)
    out = {"ident": np.eye(P, dtype=f)}
    causal = np.where(pos[None, :] <= pos[:, None], 0.0, -1e30).astype(f)
    out["causal"] = causal.reshape(NT, P, S).transpose(1, 0, 2)
    gamma = np.log(1.0 - 2.0 ** (-5.0 - np.arange(4, dtype=np.float64)))
    diff = pos[None, :] - np.arange(P)[:, None]
    out["decay"] = (np.where(diff >= 0, np.exp(np.maximum(diff, 0)[None] * gamma[:, None, None]), 0.0)
                    * P ** -0.5).astype(f).transpose(1, 0, 2)

    def angles(p, dim):
        inv = f(10000.0) ** (-np.arange(dim // 2, dtype=f) / f(dim // 2))
        ang = p.astype(f)[:, None] * inv.astype(f)[None, :]
        return [g(ang).astype(f).reshape(NT, P, dim // 2).transpose(1, 0, 2) for g in (np.cos, np.sin)]

    for name, dim in (("ret", 128), ("diff", 64), ("mla", 32)):
        out[name + "_cos"], out[name + "_sin"] = angles(pos, dim)
    row_angle, col_angle = angles(pos // 64, 32), angles(pos % 64, 32)
    for i, n in enumerate(("gqa_cos", "gqa_sin")):
        out[n] = np.concatenate([row_angle[i], col_angle[i]], axis=2)
    out["iota8"] = np.tile(np.arange(NE, dtype=f), (P, 1))
    out["iota"] = np.tile(np.arange(P, dtype=f), (P, 1))
    out["before"] = np.triu(np.ones((P, P), f), 1)
    return np.concatenate([np.ascontiguousarray(out[n]).reshape(P, -1) for n in TABLES], axis=1).astype(f)


def kernel(**inputs):
    import concourse.bacc as bacc
    from concourse.bass_utils import run_bass_kernel_spmd

    nc = bacc.Bacc("TRN2", target_bir_lowering=False, num_devices=1)
    arrays = {name: np.ascontiguousarray(a) for name, a in inputs.items()}
    arrays["tables"] = tables_of_shapes()
    io = {name: nc.dram_tensor(name, a.shape, mybir.dt.from_np(a.dtype), kind="ExternalInput").ap()
          for name, a in arrays.items()}
    out = nc.dram_tensor("out", (1, S, D), F32, kind="ExternalOutput").ap()
    program(nc, io, out)
    result = run_bass_kernel_spmd(nc, [arrays], core_ids=[0])
    return result.results[0]["out"]
```

```python
import numpy as np
import concourse.bass as bass
import concourse.mybir as mybir
from concourse.alu_op_type import AluOpType as ALU

F32 = mybir.dt.float32
F32R = mybir.dt.float32r
BF16 = mybir.dt.bfloat16
U32 = mybir.dt.uint32
ACTF = mybir.ActivationFunctionType
AX = mybir.AxisListType
ds = bass.ds

P = 128
S = 256
NT = S // P
D = 1024
KD = D // P
FF = 2816
STEP_F = 256
STEPS = FF // STEP_F
NE = 8
SLAB = 512
RAW, SPL = 12, 6
UNITS_GU, UNITS_D = 4, 2
FFN_UNITS = STEPS * (UNITS_GU + UNITS_D)
EPS = 1e-6
SLOTS = P

TABLES = {"ident": P, "causal": NT * S, "decay": 4 * S, "ret_cos": NT * 64, "ret_sin": NT * 64,
          "diff_cos": NT * 32, "diff_sin": NT * 32, "mla_cos": NT * 16, "mla_sin": NT * 16,
          "gqa_cos": NT * 32, "gqa_sin": NT * 32, "iota8": NE,
          "iota": P, "before": P}
COLUMNS = [("norm_mix_g", 16), ("norm_ffn_g", 16), ("ffn1_norm_2", 16), ("ffn2_norm_2", 16),
           ("ev_norm_2", 8), ("od_norm_2", 8), ("att_out_g", 8), ("ret_out_g", 8),
           ("ev_b_s_2", 8), ("ev_sub_norm_2", 1), ("od_cq_norm_2", 2), ("od_ckv_norm_2", 1)]
ROWS = [("ev_q_norm_2", 64), ("ev_k_norm_2", 64), ("ev_sgu_norm_2", 512), ("od_mla_q_norm_2", 96),
        ("od_mla_k_norm_2", 96), ("od_gqa_q_norm_2", 64), ("od_gqa_k_norm_2", 64),
        ("ev_lam_q1_2", 64), ("ev_lam_k1_2", 64), ("ev_lam_q2_2", 64), ("ev_lam_k2_2", 64)]


class Rounds:

    def __init__(self, nc, queue, name, per_round):
        self.q, self.sem, self.per_round, self.count, self.round = queue, nc.alloc_semaphore(name), per_round, 0, 0

    def need(self, *marks):
        for sem, value in marks:
            self.q.wait_ge(sem, value)

    def run(self, marks, op, *args, **kw):
        self.need(*marks)
        return self.did(op(*args, **kw))

    def did(self, ins):
        ins.then_inc(self.sem, 1)
        self.count += 1
        return (self.sem, self.count + self.per_round * self.round)


class Engine:

    def __init__(self, nc, queue, name):
        self.q, self.sem, self.count, self.seen = queue, nc.alloc_semaphore(name), 0, {}

    def need(self, *marks):
        for sem, value in marks:
            if self.seen.get(sem.name, 0) < value:
                self.q.wait_ge(sem, value)
                self.seen[sem.name] = value

    def did(self, ins):
        ins.then_inc(self.sem, 1)
        self.count += 1
        return (self.sem, self.count)

    def run(self, marks, op, *args, **kw):
        self.need(*marks)
        return self.did(op(*args, **kw))


def program(nc, io, out, upto=12):
    sp, act, pe, dve = nc.sync, nc.scalar, nc.tensor, nc.vector
    SP, ACT, PE, DVE = (Engine(nc, q, n) for q, n in
                        ((sp, "sp_count"), (act, "act_count"), (pe, "pe_count"), (dve, "dve_count")))
    compute = (mybir.EngineType.Activation, mybir.EngineType.PE, mybir.EngineType.DVE)

    def sb(name, shape, dt=F32):
        return nc.alloc_sbuf_tensor(name, shape, dt)

    def over(name, shape, base, skip=0, dt=F32):
        return nc.alloc_sbuf_tensor_at(name, shape, dt, offset=base + skip)

    def sem(name):
        return nc.alloc_semaphore(name)

    raw = [sb(f"raw{i}", [P, 1024]) for i in range(RAW)]
    hi = [sb(f"hi{i}", [P, 1024], F32R) for i in range(SPL)]
    lo = [sb(f"lo{i}", [P, 1024], F32R) for i in range(SPL)]
    x = sb("x_res", [P, NT, D])
    gates = sb("gates", [P, 2, D])
    at_gates = nc.sbuf_base - 8192
    xn = sb("xn", [P, NT, D])
    at_xn = nc.sbuf_base - 8192
    aT = [sb("aT_hi", [P, KD, S], F32R), sb("aT_lo", [P, KD, S], F32R)]
    at = nc.sbuf_base
    proj = sb("proj", [P, NT, 3584])
    at_proj = at
    at = nc.sbuf_base
    qkT = sb("qkT", [P, 16, S])
    at_qkT = at
    at = nc.sbuf_base
    probs = sb("probs", [P, 2, NT * S])
    at_probs = at
    probsT = sb("probsT", [P, 2, NT * S])
    tables = sb("tables_sb", [P, sum(TABLES.values())])
    cols = sb("cols_sb", [P, P])
    rows = sb("rows", [P, sum(n for _, n in ROWS)])
    c_row = over("c_row", [1, D], at_xn)
    small = sb("small", [P, 256])
    c_cols = sb("c_cols", [P, KD])
    gain_cols = sb("gain_cols", [P, 16])
    mod_cols = sb("mod_cols", [P, 32])
    zeros = sb("zeros", [1, SLAB], BF16)
    ones = sb("ones", [1, P])
    mod_rows = over("mod_rows", [P, 6 * D], at_proj)
    cs_wide = over("cs_wide", [P, KD, P], at_proj, 24 * 1024)
    silu_g = over("silu_g", [P, NT, STEP_F], at_qkT, 8192)
    hid = over("hid", [P, NT, STEP_F], at_qkT, 10240)
    hidT = [over("hidT_hi", [P, 2 * S], at_qkT, 12288, F32R), over("hidT_lo", [P, 2 * S], at_qkT, 14336, F32R)]
    ada_slot = [over(f"ada_slot{i}", [P, 2, SLAB], at_qkT, 4096 * i) for i in range(2)]
    ada_sum = [over(f"ada_sum{i}", [P, SLAB], at_proj, 24 * 1024 + 2048 * i) for i in range(2)]
    cT = [over("cT_hi", [P, KD, P], at_qkT, 0, F32R), over("cT_lo", [P, KD, P], at_qkT, 4096, F32R)]
    vec_rows = over("vec_rows", [P, P], at_xn, 4096)
    bias_pieces = sb("bias_pieces", [32, P])
    rope_tmp = over("rope_tmp", [P, 2048], at_qkT, 8192)
    k_full = over("k_full", [P, NT, 768], at_gates)
    probs_d = over("probs_d", [P, 4, NT * S], at_gates)
    gq_pairs = over("gq_pairs", [P, NT, 4, P], at_probs, 4096)
    codesT = [over("codesT_hi", [P, 3, S], at_qkT, 0, F32R), over("codesT_lo", [P, 3, S], at_qkT, 3072, F32R)]
    expert_w = sb("expert_w", [P, 2 * NE + 2])
    top_idx = sb("top_idx", [P, 8], U32)
    xn_split = [over("xn_hi", [P, NT, D], at_proj, 8192, F32R), over("xn_lo", [P, NT, D], at_proj, 16384, F32R)]
    onehot = over("onehot", [P, 2, NT, P], at_proj, 24576, F32R)
    onehotT = over("onehotT", [P, 2 * NT * P], at_proj, 26624, F32R)
    x_full = over("x_full", [P, KD, P], at_probs, 4096)
    ysum = over("ysum", [P, NT, D], at_qkT)
    y_split = [over("y_hi", [P, D], at_proj, 0, F32R), over("y_lo", [P, D], at_proj, 4096, F32R)]
    ones_sq = sb("ones_sq", [P, P])
    picked = sb("picked", [P, 2 * NE + 2])
    slot_of = sb("slot_of", [P, 2 * NE + 2])
    busiest = sb("busiest", [P, 1])
    busiest_i = sb("busiest_i", [P, 1], mybir.dt.int32)
    next_w = sb("next_w", [P, NT])
    slot_w = sb("slot_w", [P, 2])
    router = over("router_sb", [P, KD, NE], at_qkT)
    hT_full = over("hT_full", [P, KD, S], at_probs)
    w_s = over("w_s", [P, 8, P], at_probs)
    w_sT = over("w_sT", [P, 8, P], at_probs, 4096)
    final_g = over("final_g", [P, D], at_probs)
    psum = [nc.alloc_psum_tensor(f"bank{i}", [P, 512], F32) for i in range(8)]

    col_at, n = {}, 0
    for name, k in COLUMNS:
        col_at[name] = n
        n += k
    n_cols = n
    row_at, n = {}, 0
    for name, k in ROWS:
        row_at[name] = n
        n += k
    tab_at, n = {}, 0
    for name, k in TABLES.items():
        tab_at[name] = n
        n += k

    def table(name):
        return tables[:, tab_at[name]:tab_at[name] + TABLES[name]]

    def col(name, k):
        return cols[:, col_at[name] + k:col_at[name] + k + 1]

    def row(name):
        return rows[:, row_at[name]:row_at[name] + dict(ROWS)[name]]

    ident = table("ident")

    small_used = [0]

    def tiny(n):
        if small_used[0] + n > 256:
            small_used[0] = 0
        a = small[:, small_used[0]:small_used[0] + n]
        small_used[0] += n
        return a

    raw_full = [sem(f"raw_full{i}") for i in range(RAW)]
    hi_done, lo_done, unit_free = sem("hi_done"), sem("lo_done"), sem("unit_free")
    stage_units = [48, 36, FFN_UNITS, 36, NE * FFN_UNITS, 0, FFN_UNITS, 28, FFN_UNITS, FFN_UNITS, 23, FFN_UNITS]
    total = sum(stage_units[:upto])
    st = {"load": 0, "split": 0, "use": 0, "lap": 0, "sp_lap": 0}

    def load(*parts):
        u, lap = st["load"], st["sp_lap"]
        st["load"] += 1
        slot = u % RAW
        if u >= RAW:
            sp.wait_ge(lo_done, u - RAW + 1 + 12 * lap)
        for dst, src in parts:
            sp.dma_start(dst(raw[slot]), src).then_inc(raw_full[slot], 32 // len(parts))

    def split_one():
        u, lap = st["split"], st["lap"]
        st["split"] += 1
        act.wait_ge(raw_full[u % RAW], 32 * (u // RAW + 1) + 32 * lap)
        if u >= SPL:
            act.wait_ge(unit_free, u - SPL + 1 + 12 * lap)
        act.activation(hi[u % SPL][:, :], raw[u % RAW][:, :], ACTF.Copy).then_inc(hi_done, 1)
        dve.wait_ge(hi_done, u + 1 + 12 * lap)
        dve.tensor_tensor(lo[u % SPL][:, :], raw[u % RAW][:, :], hi[u % SPL][:, :].bitcast(F32),
                          ALU.subtract).then_inc(lo_done, 1)

    def split_to(n):
        while st["split"] < min(n, total):
            split_one()

    def unit(u, k=2, width=512):
        return [s[u % SPL][:, 0:k * width].rearrange("p (k n) -> p k n", k=k) for s in (hi, lo)]

    def passes(bank, left, right, first, last):
        for n, (a, b) in enumerate(((0, 0), (0, 1), (1, 0))):
            ins = pe.matmul(bank, left[a], right[b], start=first and n == 0, stop=last and n == 2)
        return ins

    def proj_load(w, c0, width, kd=KD):
        v = w[:, c0:c0 + width].rearrange("(k p) n -> p k n", p=P)
        for k in range(0, kd, 2):
            load((lambda r: r[:, :].rearrange("p (k n) -> p k n", k=2)[:, :, 0:width], v[:, k:k + 2, :]))

    bank_mark = [()] * 8

    def slab(width, evacuate, marks=(), kd=KD, left=aT):
        u = st["use"]
        n_units = kd // 2
        split_to(u + n_units)
        for t in range(NT):
            PE.need(*bank_mark[t])
            for j in range(n_units):
                if t == 0:
                    pe.wait_ge(lo_done, u + j + 1)
                w = unit(u + j)
                for kk in range(2):
                    k = 2 * j + kk
                    if t == 0 and marks:
                        PE.need(marks[k])
                    ins = passes(psum[t][:, 0:width], [a[:, k, t * P:(t + 1) * P] for a in left],
                                 [r[:, kk, 0:width] for r in w], k == 0, k == kd - 1)
                if t == NT - 1:
                    ins.then_inc(unit_free, 1)
            if t == 0:
                mark0 = PE.did(ins)
                bank_mark[0] = evacuate(0, psum[0][:, 0:width], mark0)
                st["use"] += n_units
                split_to(u + n_units + 4)
        bank_mark[1] = evacuate(1, psum[1][:, 0:width], (unit_free, u + n_units))

    class Events:

        def __init__(self, name):
            self.gu, self.silu, self.hid = sem(name + "_gu"), sem(name + "_silu"), sem(name + "_hid")
            self.turned, self.hi, self.lo = sem(name + "_turned"), sem(name + "_hidT_hi"), sem(name + "_hidT_lo")

    ev_dense, ev_all, ev_slots = Events("dense"), Events("all_tokens"), Events("slots")
    ffn = {"g": 0, "ev": ev_dense}

    def pe_gate_up(t, u, g, lap, marks=()):
        if g > 0:
            pe.wait_ge(ffn["ev"].hid, 2 * (g - 1) + t + 1 + 4 * lap)
        for j in range(UNITS_GU):
            if t == 0:
                pe.wait_ge(lo_done, u + j + 1 + 12 * lap)
            w = unit(u + j)
            for kk in range(2):
                k = 2 * j + kk
                if marks:
                    PE.need(marks[k])
                ins = passes(psum[t][:, :], [a[:, k, t * P:(t + 1) * P] for a in aT],
                             [r[:, kk, :] for r in w], k == 0, k == KD - 1)
            if t == 1:
                ins.then_inc(unit_free, 1)
        if t == 0:
            ins.then_inc(ffn["ev"].gu, 1)

    def silu_mul(t, u_end, g, lap, weight):
        if t == 0:
            act.wait_ge(ffn["ev"].gu, g + 1 + 2 * lap)
        else:
            act.wait_ge(unit_free, u_end + 12 * lap)
        if g > 0:
            act.wait_ge(ffn["ev"].hid, 2 * (g - 1) + t + 1 + 4 * lap)
        act.activation(silu_g[:, t, :], psum[t][:, 0:STEP_F], ACTF.Silu).then_inc(ffn["ev"].silu, 1)
        dve.wait_ge(ffn["ev"].silu, 2 * g + t + 1 + 4 * lap)
        if g > 0:
            dve.wait_ge(ffn["ev"].turned, g + 2 * lap)
        up = psum[t][:, STEP_F:2 * STEP_F]
        if weight is None:
            ins = dve.tensor_tensor(hid[:, t, :], silu_g[:, t, :], up, ALU.mult)
        else:
            ins = dve.scalar_tensor_tensor(out=hid[:, t, :], in0=silu_g[:, t, :], scalar=weight(t),
                                           in1=up, op0=ALU.mult, op1=ALU.mult)
        ins.then_inc(ffn["ev"].hid, 1)

    def pe_turn(g, lap):
        pe.wait_ge(ffn["ev"].hid, 2 * g + 2 + 4 * lap)
        if g > 0:
            pe.wait_ge(ffn["ev"].lo, g + 2 * lap)
        for f in range(2):
            for t in range(NT):
                ins = pe.transpose(psum[2][:, f * S + t * P:f * S + (t + 1) * P],
                                   hid[:, t, f * P:(f + 1) * P], ident)
        ins.then_inc(ffn["ev"].turned, 1)

    def hidT_split(u_before, g, lap):
        act.wait_ge(ffn["ev"].turned, g + 1 + 2 * lap)
        act.wait_ge(unit_free, u_before + 12 * lap)
        act.activation(hidT[0][:, :], psum[2][:, :], ACTF.Copy).then_inc(ffn["ev"].hi, 1)
        dve.wait_ge(ffn["ev"].hi, g + 1 + 2 * lap)
        dve.tensor_tensor(hidT[1][:, :], psum[2][:, :], hidT[0][:, :].bitcast(F32),
                          ALU.subtract).then_inc(ffn["ev"].lo, 1)

    def pe_down(u, g, lap, last=False):
        pe.wait_ge(ffn["ev"].lo, g + 1 + 2 * lap)
        for f in range(2):
            pe.wait_ge(lo_done, u + f + 1 + 12 * lap)
            w = [s[(u + f) % SPL] for s in (hi, lo)]
            for t in range(NT):
                for half in range(2):
                    ins = passes(psum[4 + 2 * t + half][:, :],
                                 [a[:, f * S + t * P:f * S + (t + 1) * P] for a in hidT],
                                 [r[:, half * SLAB:(half + 1) * SLAB] for r in w], False,
                                 last and f == 1)
            ins.then_inc(unit_free, 1)

    def ffn_load(gate, up, down):
        def gu(c):
            for k in range(UNITS_GU):
                load((lambda r: r[:, :].rearrange("p (k n) -> p k n", k=2)[:, :, 0:STEP_F], gate(c, 2 * k)),
                     (lambda r: r[:, :].rearrange("p (k n) -> p k n", k=2)[:, :, STEP_F:], up(c, 2 * k)))

        def dn(c):
            for f in range(2):
                load((lambda r: r[:, :], down(c, f)))

        gu(0)
        base, lap = st["load"], st["sp_lap"]
        with sp.Fori(0, (STEPS - 1) // 2) as i:
            st["sp_lap"] = lap + i
            for b in range(2):
                gu(2 * i + b + 1)
                dn(2 * i + b)
        st["load"], st["sp_lap"] = base + 12 * ((STEPS - 1) // 2), lap
        dn(STEPS - 1)

    def look_ahead(n):
        for _ in range(n):
            if st["split"] < total:
                split_one()

    def zero_y(marks, banks=range(4, 8)):
        for mark in marks:
            pe.wait_ge(*mark)
        for b in banks:
            pe.matmul(psum[b][:, :], zeros[:, 0:P], zeros[:, :], start=True, stop=False)

    def close_y(counter, banks=range(4, 8)):
        for b in banks:
            ins = pe.matmul(psum[b][:, :], zeros[:, 0:P], zeros[:, :], start=False, stop=True)
        return counter.did(ins)

    def ffn_steps(marks=(), weight=None, final=False, aside=None):
        begin, end = aside or (lambda *n: None, lambda *n: None)
        g0, u0, lap = ffn["g"], st["use"], st["lap"]
        rounds = (STEPS - 1) // 2
        looped = rounds - 1 if final else rounds

        def step(g, u, lap, n, i):
            pe_gate_up(0, u, g, lap)
            silu_mul(1, u, g - 1, lap, weight)
            look_ahead(UNITS_D)
            pe_turn(g - 1, lap)
            hidT_split(u, g - 1, lap)
            end(n - 1, i)
            begin(n, i, 0)
            pe_gate_up(1, u, g, lap)
            silu_mul(0, None, g, lap, weight)
            look_ahead(UNITS_GU)
            pe_down(u + UNITS_GU, g - 1, lap)
            begin(n, i, 1)

        def round_of(g, u, lap, i=0):
            for b in range(2):
                step(g + b, u + b * (UNITS_GU + UNITS_D), lap, 1 + b, 2 * i)

        pe_gate_up(0, u0, g0, lap, marks)
        silu_mul(0, None, g0, lap, weight)
        pe_gate_up(1, u0, g0, lap)
        look_ahead(UNITS_GU)
        begin(0, 0, 0)
        begin(0, 0, 1)
        g, u, split = g0 + 1, u0 + UNITS_GU, st["split"]
        with nc.Fori(0, looped, engines=compute) as i:
            st["lap"] = lap + i
            round_of(g, u, lap + i, i)
        st["lap"], st["split"] = lap, split + RAW * looped
        g, u = g + 2 * looped, u + RAW * looped
        if final:
            round_of(g, u, lap, looped)
            g, u = g + 2, u + RAW
        silu_mul(1, u, g - 1, lap, weight)
        pe_turn(g - 1, lap)
        hidT_split(u, g - 1, lap)
        end(STEPS - 1)
        look_ahead(UNITS_D)
        pe_down(u, g - 1, lap)
        ffn["g"], st["use"] = g, u + UNITS_D


    x_mark = []
    mod_marks = []
    mod_rest = []

    def fetch(name, *copies):
        landed = sem(name)
        ACT.need(*x_mark)
        for dst, src in copies:
            act.dma_start(dst, src).then_inc(landed, 16)
        return (landed, 16 * len(copies))

    def flat(name):
        v = io[name]
        return v.rearrange({1: "a -> a", 2: "a b -> (a b)", 3: "a b c -> (a b c)"}[len(v.shape)])

    c_in = fetch("c_in", (c_row[:, :], io["c"]))
    small_in = sem("small_in")
    smalls = [(tables[:, :], io["tables"]), (x[:, :, :], io["x"][0].rearrange("(t p) d -> p t d", p=P)),
              *((vec_rows[col_at[n]:col_at[n] + k, :], flat(n).rearrange("(k p) -> k p", p=P)) for n, k in COLUMNS),
              *((rows[:, row_at[n]:row_at[n] + k], flat(n).rearrange("(a n) -> a n", a=1).to_broadcast([P, k]))
                for n, k in ROWS)]
    for dst, src in smalls:
        nc.gpsimd.dma_start(dst, src).then_inc(small_in, 16)
    start = (small_in, 16 * len(smalls))
    z = DVE.did(dve.memset(zeros[:, :], 0.0))
    DVE.did(dve.memset(ones_sq[:, :], 1.0))
    DVE.did(dve.memset(expert_w[:, 2 * NE:], 0.0))
    o = DVE.did(dve.memset(ones[:, :], 1.0))
    PE.need(o, c_in)
    for k in range(KD):
        ins = pe.matmul(psum[3][:, k:k + 1], c_row[:, k * P:(k + 1) * P], ones[:, 0:1], start=True, stop=True)
    m = PE.did(ins)
    m = ACT.run([m], act.activation, c_cols[:, :], psum[3][:, 0:KD], ACTF.Silu)
    bank_mark[3] = (m,)
    x_mark[:] = [m]

    def vectors_to_columns():
        PE.need(z, start, *bank_mark[3])
        m = PE.did(pe.transpose(psum[3][:, 0:n_cols], vec_rows[0:n_cols, :], ident[0:n_cols, 0:n_cols]))
        m = DVE.run([m], dve.tensor_copy, cols[:, 0:n_cols], psum[3][:, 0:n_cols])
        bank_mark[3] = (m,)
        cols_in[:] = [m]
        x_mark[:] = [start]
    cols_in = []

    def rstd_of(ss, n, width, marks):
        v, r = tiny(width), tiny(width)
        a = DVE.run(marks, dve.tensor_scalar, v, ss, 1.0 / n, EPS, ALU.mult, ALU.add)
        b = ACT.run([a], act.activation, v, v, ACTF.Sqrt)
        return r, DVE.run([b], dve.reciprocal, r, v)

    def turn_to_aT(src, nk, marks, gain, bias=None, full=None, free=(), dst=aT):
        PE.need(*marks)
        for b in range(4, 8):
            PE.need(*bank_mark[b])
        done = []
        for k0 in range(0, nk, 2):
            b = 4 + k0 // 2
            ks = range(k0, min(k0 + 2, nk))
            bank = {k: psum[b][:, (k - k0) * S:(k - k0 + 1) * S] for k in ks}
            for k in ks:
                for t in range(NT):
                    ins = pe.transpose(bank[k][:, t * P:(t + 1) * P], src(t, k), ident)
            m = PE.did(ins)
            if bias is None:
                for k in ks:
                    h = ACT.run([m, *free], act.activation, dst[0][:, k, :], bank[k], ACTF.Identity, scale=gain(k))
                for k in ks:
                    done.append(DVE.run([h], dve.scalar_tensor_tensor, out=dst[1][:, k, :], in0=bank[k],
                                        scalar=gain(k), in1=dst[0][:, k, :].bitcast(F32), op0=ALU.mult,
                                        op1=ALU.subtract))
                bank_mark[b] = (done[-1],)
            else:
                for k in ks:
                    a = DVE.run([m, *free], dve.tensor_scalar, full[:, k, :], bank[k], gain(k), bias(k),
                                ALU.mult, ALU.add)
                bank_mark[b] = (a,)
                for k in ks:
                    h = ACT.run([a], act.activation, dst[0][:, k, :], full[:, k, :], ACTF.Copy)
                    done.append(DVE.run([h], dve.tensor_tensor, dst[1][:, k, :], full[:, k, :],
                                        dst[0][:, k, :].bitcast(F32), ALU.subtract))
        return done

    def normed(gain, bias=None, free=()):
        ss = tiny(NT)
        sq = [ACT.run([x_mark[0], *free], act.activation, xn[:, t, :], x[:, t, :], ACTF.Square,
                      accum_out=ss[:, t:t + 1]) for t in range(NT)]
        r, m = rstd_of(ss, D, NT, sq)
        for t in range(NT):
            m = DVE.run([m], dve.tensor_scalar, xn[:, t, :], x[:, t, :], r[:, t:t + 1], None, ALU.mult)
        return turn_to_aT(lambda t, k: xn[:, t, k * P:(k + 1) * P], KD, [m], gain, bias,
                          hT_full if bias else None)

    def gated_add(t, half, bank, mark, gate=None, factor=1.0):
        xs = x[:, t, half * SLAB:(half + 1) * SLAB]
        if gate is None:
            x_mark[0] = DVE.run([mark, x_mark[0]], dve.scalar_tensor_tensor, out=xs, in0=bank,
                                scalar=factor, in1=xs, op0=ALU.mult, op1=ALU.add)
        else:
            tmp = xn[:, t, half * SLAB:(half + 1) * SLAB]
            a = DVE.run([mark], dve.tensor_tensor, tmp, bank,
                        gates[:, gate, half * SLAB:(half + 1) * SLAB], ALU.mult)
            x_mark[0] = DVE.run([a, x_mark[0]], dve.tensor_tensor, xs, xs, tmp, ALU.add)
        return (x_mark[0],)

    def add_ffn(mark, gate=None, factor=1.0):
        for t in range(NT):
            for half in range(2):
                b = 4 + 2 * t + half
                bank_mark[b] = gated_add(t, half, psum[b][:, :], mark, gate, factor)
        for b in range(3):
            bank_mark[b] = bank_mark[7]

    def dense_ffn(gate, up, down, marks, g=None, factor=1.0, aside=None, ahead=None):
        final = st["use"] + FFN_UNITS == total
        ffn_load(gate, up, down)
        zero_y([m for b in range(4, 8) for m in bank_mark[b]])
        for b in range(3):
            PE.need(*bank_mark[b])
        ffn_steps(marks, final=final, aside=aside)
        if ahead:
            ahead()
        add_ffn(close_y(PE), g, factor)

    def cols_of(w, c, k, c0=0):
        return w[k * P:(k + 2) * P, ds(c * STEP_F + c0, STEP_F)].rearrange("(k p) n -> p k n", p=P)

    def rows_of(w, c, f):
        return w[ds(c * STEP_F + f * P, P), :]

    mod_done = sem("mod_done")

    ada_full = [sem("ada_full0"), sem("ada_full1")]
    ada_steps, ada_added, ada_rows = sem("ada_steps"), sem("ada_added"), sem("ada_rows")
    ADA_SLABS = 6 * D // SLAB

    def load_ada(marks):
        pool, w = nc.gpsimd, io["ada_w"][1]
        for m in marks:
            pool.wait_ge(*m)
        def slab_of(n, i=0):
            v = w[:, ds((n + i) * SLAB, SLAB)].rearrange("(k p) n -> p k n", p=P)
            for j in range(4):
                if n or j > 1:
                    pool.wait_ge(ada_steps, 8 * n + 2 * j - 2 + 8 * i)
                pool.dma_start(ada_slot[j % 2][:, :, :], v[:, 2 * j:2 * j + 2, :]).then_inc(ada_full[j % 2], 16)
        slab_of(0)
        with pool.Fori(0, ADA_SLABS - 1) as i:
            slab_of(1, i)

    def ada_sums(n, i, half):
        acc = ada_sum[n % 2]
        if n and half == 0:
            dve.wait_ge(ada_rows, n + i)
        for k in range(half * KD // 2, (half + 1) * KD // 2):
            j, kk = k // 2, k % 2
            src, c = ada_slot[j % 2][:, kk, :], c_cols[:, k:k + 1]
            if kk == 0:
                dve.wait_ge(ada_full[j % 2], 16 * (2 * n + j // 2 + 1) + 32 * i)
            if k == 0:
                ins = dve.tensor_scalar(acc[:, :], src, c, None, ALU.mult)
            else:
                dve.wait_ge(ada_steps, 8 * n + k + 8 * i)
                ins = dve.scalar_tensor_tensor(out=acc[:, :], in0=src, scalar=c, in1=acc[:, :],
                                               op0=ALU.mult, op1=ALU.add)
            ins.then_inc(ada_steps, 1)

    def ada_out(n, i=0):
        pe.wait_ge(ada_steps, 8 * n + 8 + 8 * i)
        pe.matmul(psum[3][:, :], ones_sq[:, :], ada_sum[n % 2][:, :], start=True, stop=True).then_inc(ada_added, 1)
        act.wait_ge(ada_added, n + 1 + i)
        act.activation(mod_rows[:, ds((n + i) * SLAB, SLAB)], psum[3][:, :], ACTF.Copy).then_inc(ada_rows, 1)

    bias_in, gates_in = [], []

    def fetch_bias(layer):
        b = io["ada_b"][layer:layer + 1, :]
        bias_in[:] = [fetch(f"bias_in{layer}", *((bias_pieces[16 * i:16 * i + 16, :], b[:, c * D:(c + 2) * D]
                                                 .rearrange("a (k p) -> (a k) p", p=P)) for i, c in enumerate((0, 3))))]

    def fetch_gates(layer):
        b = io["ada_b"][layer:layer + 1, :]
        gates_in[:] = [fetch(f"gates_in{layer}", *((gates[:, g, :], b[:, c * D:(c + 1) * D].to_broadcast([P, D]))
                                                   for g, c in enumerate((2, 5))))]

    def first_conditioning():
        w = io["ada_w"][0]
        def load_round(c):
            for s in range(3):
                v = w[:, ds((3 * c + s) * SLAB, SLAB)].rearrange("(k p) n -> p k n", p=P)
                for k in range(0, KD, 2):
                    load((lambda r: r[:, :].rearrange("p (k n) -> p k n", k=2), v[:, k:k + 2, :]))
        n_rounds = 6 * D // SLAB // 3
        load_round(0)
        base, sp_lap = st["load"], st["sp_lap"]
        with sp.Fori(0, n_rounds - 1) as i:
            st["sp_lap"] = sp_lap + i
            load_round(i + 1)
        st["load"], st["sp_lap"] = base + 12 * (n_rounds - 1), sp_lap

        a = DVE.run([x_mark[0]], dve.tensor_copy, cs_wide[:, :, :], c_cols[:, :].unsqueeze(2).to_broadcast([P, KD, P]))
        h = ACT.run([a, *bank_mark[0], *bank_mark[1]], act.activation, cT[0][:, :, :], cs_wide[:, :, :], ACTF.Copy)
        left_mark = DVE.run([h], dve.tensor_tensor, cT[1][:, :, :], cs_wide[:, :, :],
                            cT[0][:, :, :].bitcast(F32), ALU.subtract)
        fetch_bias(0)
        PE.need(left_mark)
        def round_of(c, n, u, lap):
            for s in range(3):
                bank = psum[s]
                nn = n * 3 + s
                if nn >= 3:
                    pe.wait_ge(mod_done, nn - 2 + 3 * lap)
                for j in range(4):
                    pe.wait_ge(lo_done, u + 4 * s + j + 1 + 12 * lap)
                    wv = unit(u + 4 * s + j)
                    for kk in range(2):
                        k = 2 * j + kk
                        ins = passes(bank[:, :], [a[:, k, :] for a in cT], [r[:, kk, :] for r in wv],
                                     k == 0, k == KD - 1)
                    ins.then_inc(unit_free, 1)
                for _ in range(4):
                    split_one()
                act.wait_ge(unit_free, u + 4 * s + 4 + 12 * lap)
                act.activation(mod_rows[:, ds((3 * c + s) * SLAB, SLAB)], bank[:, :], ACTF.Copy).then_inc(mod_done, 1)
        for b in range(3):
            PE.need(*bank_mark[b])
        u = st["use"]
        split_to(u + 4)
        round_of(0, 0, u, st["lap"])
        split = st["split"]
        with nc.Fori(0, n_rounds - 1, engines=compute) as i:
            st["lap"] = i
            round_of(i + 1, 1, u + 12, i)
        st["lap"], st["split"] = 0, split + 12 * (n_rounds - 1)
        st["use"] = u + 12 * n_rounds
        vectors_to_columns()
        for b in range(3):
            bank_mark[b] = ((mod_done, ADA_SLABS),)
        conditioning(0, lambda k: (mod_done, ADA_SLABS))

    def conditioning(layer, rows_in):
        PE.need(bias_in[0], *bank_mark[3])
        bias = PE.did(pe.transpose(psum[3][:, 0:32], bias_pieces[:, :], ident[0:32, 0:32]))
        DVE.need(bias)

        def columns_of(half, norm_gain):
            k = slice(16 * half, 16 * half + 16)
            v = mod_rows[:, 3 * D * half:(3 * half + 2) * D].rearrange("p (k n) -> p k n", k=16)
            DVE.need(rows_in((4, 10)[half]))
            a = DVE.run([], dve.tensor_tensor, v, v, ident.unsqueeze(1).to_broadcast([P, 16, P]), ALU.mult)
            a = DVE.run([a], dve.reduce_sum, mod_cols[:, k], v, axis=AX.X)
            cm = DVE.run([a], dve.tensor_tensor, mod_cols[:, k], mod_cols[:, k], psum[3][:, k], ALU.add)
            gain = cols[:, col_at[norm_gain] + 8 * layer:col_at[norm_gain] + 8 * layer + 8]
            gm = DVE.run([cm], dve.scalar_tensor_tensor, out=gain_cols[:, 8 * half:8 * half + 8],
                         in0=mod_cols[:, 16 * half + 8:16 * half + 16], scalar=1.0, in1=gain, op0=ALU.add, op1=ALU.mult)
            return [cm, gm]

        def second_columns():
            bank_mark[3] = (columns_of(1, "norm_ffn_g")[0],)
            fetch_gates(layer)

        def last_slab():
            if layer:
                ada_sums(ADA_SLABS - 1, 0, 0)
                ada_sums(ADA_SLABS - 1, 0, 1)

        def last_rows():
            if layer:
                PE.need(*bank_mark[3])
                ada_out(ADA_SLABS - 1)
                bank_mark[3] = ((ada_rows, ADA_SLABS),)
            add_gates()

        def add_gates():
            DVE.need(rows_in(ADA_SLABS), gates_in[0])
            for g in range(2):
                last = DVE.run([], dve.tensor_tensor, gates[:, g, :], gates[:, g, :],
                               mod_rows[:, (2 + 3 * g) * D:(3 + 3 * g) * D], ALU.add)
            ACT.need(last)

        mod_marks[:] = columns_of(0, "norm_mix_g")
        mod_rest[:] = [second_columns, last_slab, last_rows]

    def store_x():
        y = out[0].rearrange("(t p) d -> p t d", p=P)
        SP.need(x_mark[0])
        sp.dma_start(y, x[:, :, :]).then_inc(out_sem, 16)
        sp.wait_ge(out_sem, 16)
    out_sem = sem("out_stored")
    def project(w, slabs, marks, kd=KD, at=0, func=None, after={}, left=aT):
        for i, (c, n) in enumerate(slabs):
            proj_load(w, c, n, kd)
            f = func(c) if func else None

            def out_of_bank(t, bank, mark, c=c, n=n, f=f):
                dst = proj[:, t, at + c:at + c + n]
                if f is not None or t == 0:
                    m = ACT.run([mark], act.activation, dst, bank, f or ACTF.Copy)
                else:
                    m = DVE.run([mark], dve.tensor_copy, dst, bank)
                out_marks.append(m)
                return (m,)
            slab(n, out_of_bank, marks, kd, left)
            marks = ()
            if i in after:
                after[i]()

    def project_out(w, marks, gate=None):
        for half in range(2):
            proj_load(w, half * SLAB, SLAB)
            slab(SLAB, lambda t, bank, mark, half=half: gated_add(t, half, bank, mark, gate), marks)
            marks = ()

    def turn_heads(src, n, width, marks, at=0):
        done = []
        PE.need(*marks)
        for j in range(0, n, 2):
            b = 4 + (j // 2) % 4
            k = min(2, n - j)
            PE.need(*bank_mark[b])
            for jj in range(k):
                for t in range(NT):
                    ins = pe.transpose(psum[b][0:width, jj * S + t * P:jj * S + (t + 1) * P],
                                       src(t, j + jj), ident)
            m = PE.did(ins)
            dst = qkT[0:width, at + j:at + j + k, :].rearrange("p j s -> p (j s)")
            if (j // 2) % 2:
                m = ACT.run([m, *marks], act.activation, dst, psum[b][0:width, 0:k * S], ACTF.Copy)
            else:
                m = DVE.run([m, *marks], dve.tensor_copy, dst, psum[b][0:width, 0:k * S])
            bank_mark[b] = (m,)
            done.append(m)
        return done

    def rope(x1, x2, cos, sin, shape, marks):
        n = int(np.prod(shape[1:]))
        names = {3: "p (a b) -> p a b", 4: "p (a b c) -> p a b c"}[len(shape)]
        dims = dict(zip("abc", shape[1:]))
        tmp = [rope_tmp[:, i * n:(i + 1) * n].rearrange(names, **dims) for i in range(4)]
        a = [DVE.run(marks, dve.tensor_tensor, tmp[i], p, q, ALU.mult)
             for i, (p, q) in enumerate(((x1, cos), (x2, sin), (x1, sin), (x2, cos)))]
        DVE.run(a, dve.tensor_tensor, x1, tmp[0], tmp[1], ALU.subtract)
        return DVE.run(a, dve.tensor_tensor, x2, tmp[2], tmp[3], ALU.add)

    def group_norm(view, n, d, marks, gains=()):
        sq = xn[:, :, 0:n * d].rearrange("p t (n d) -> p t n d", n=n)
        a = [ACT.run(marks, act.activation, sq[:, t], view[:, t], ACTF.Square) for t in range(NT)]
        ss = tiny(NT * n)
        m = DVE.run(a, dve.reduce_sum, ss.rearrange("p (t n) -> p t n", t=NT), sq, axis=AX.X)
        r, m = rstd_of(ss, d, NT * n, [m])
        r = r.rearrange("p (t n) -> p t n", t=NT).unsqueeze(3).to_broadcast([P, NT, n, d])
        m = DVE.run([m], dve.tensor_tensor, view, view, r, ALU.mult)
        done = [m]
        for v, g in gains:
            done.append(DVE.run([m], dve.tensor_tensor, v, v, g, ALU.mult))
        return done

    def attention(n, width, q, k, v, scale, dst, marks, causal=False, pair=None, between=()):
        maps = 2 if pair is not None else 1
        bufs = [probs_d[:, i, :] for i in range(4)] if maps == 2 else [probs[:, i, :] for i in range(2)]
        rs, rr = tiny(NT * n * maps), tiny(NT * n * maps)
        nmax = tiny(2 * NT * maps)
        turned_of, pv_of, ready = {}, {}, {}

        def scores(h):
            for mp in range(maps):
                i = (h * maps + mp) % len(bufs)
                b = 4 + (h * maps + mp) % 2
                e = bufs[i].rearrange("p (t s) -> p t s", t=NT)
                PE.need(*bank_mark[b], *(marks if h == 0 else ()))
                for t in range(NT):
                    ins = pe.matmul(psum[b][:, t * S:(t + 1) * S], q(h, mp, t), k(h, mp), start=True, stop=True)
                m = PE.did(ins)
                sc = psum[b][:, :].rearrange("p (t s) -> p t s", t=NT)
                old = turned_of.get(h - len(bufs) // maps, ())
                nm = nmax[:, (i % (2 * maps)) * NT:(i % (2 * maps)) * NT + NT]
                olde = ready.get(h - 2, ())
                if causal:
                    m = DVE.run([m, *old], dve.scalar_tensor_tensor, out=e, in0=sc, scalar=scale,
                                in1=table("causal").rearrange("p (t s) -> p t s", t=NT), op0=ALU.mult, op1=ALU.add)
                    bank_mark[b] = (m,)
                    m = DVE.run([m, *olde], dve.tensor_reduce, nm, e, AX.X, ALU.max, negate=True)
                    src, k_scale = e, 1.0
                else:
                    m = DVE.run([m, *olde], dve.tensor_reduce, nm, sc, AX.X, ALU.max, negate=True)
                    m = DVE.run([m], dve.tensor_scalar, nm, nm, scale, None, ALU.mult)
                    src, k_scale = sc, scale
                ex = []
                for t in range(NT):
                    j = (t * maps + mp) * n + h
                    ex.append(ACT.run([m, *old], act.activation, e[:, t, :], src[:, t, :], ACTF.Exp,
                                      bias=nm[:, t:t + 1], scale=k_scale, accum_out=rs[:, j:j + 1]))
                if not causal:
                    bank_mark[b] = (ex[-1],)
                ready[h] = (*ready.get(h, ()), *ex) if mp else tuple(ex)
            if maps == 2:
                i = (h * 2) % len(bufs)
                w = []
                for t in range(NT):
                    j0, j1 = (t * 2) * n + h, (t * 2 + 1) * n + h
                    a0 = DVE.run(ready[h], dve.reciprocal, rr[:, j0:j0 + 1], rs[:, j0:j0 + 1])
                    a1 = DVE.run(ready[h], dve.reciprocal, rr[:, j1:j1 + 1], rs[:, j1:j1 + 1])
                    a1 = DVE.run([a1], dve.tensor_tensor, rr[:, j1:j1 + 1], rr[:, j1:j1 + 1], pair, ALU.mult)
                    e0, e1 = (bufs[i + z].rearrange("p (t s) -> p t s", t=NT)[:, t, :] for z in (0, 1))
                    a1 = DVE.run([a1], dve.tensor_scalar, e1, e1, rr[:, j1:j1 + 1], None, ALU.mult)
                    w.append(DVE.run([a0, a1], dve.scalar_tensor_tensor, out=e0, in0=e0,
                                     scalar=rr[:, j0:j0 + 1], in1=e1, op0=ALU.mult, op1=ALU.subtract))
                ready[h] = tuple(w)

        def turn(h):
            b = 2 + h % 2
            e = bufs[(h * maps) % len(bufs)]
            PE.need(*ready[h], *bank_mark[b])
            for kc in range(NT):
                for t in range(NT):
                    ins = pe.transpose(psum[b][:, kc * S + t * P:kc * S + (t + 1) * P],
                                       e[:, t * S + kc * P:t * S + (kc + 1) * P], ident)
            m = PE.did(ins)
            turned_of[h] = (m,)
            old = pv_of.get(h - 2, ())
            if causal:
                m = ACT.run([m, *old], act.activation, probsT[:, h % 2, :], psum[b][:, :], ACTF.Copy)
            else:
                m = DVE.run([m, *old], dve.tensor_copy, probsT[:, h % 2, :], psum[b][:, :])
            bank_mark[b] = (m,)

        def values(h):
            PE.need(*bank_mark[2 + h % 2])
            if h == 0:
                PE.need(*bank_mark[6], *bank_mark[7])
            for t in range(NT):
                last = t if causal else NT - 1
                for kc in range(last + 1):
                    ins = pe.matmul(psum[6 + t][:, h * width:(h + 1) * width],
                                    probsT[:, h % 2, kc * S + t * P:kc * S + (t + 1) * P], v(h, kc),
                                    start=kc == 0, stop=kc == last)
            pv_of[h] = (PE.did(ins),)

        for h in range(n + 2):
            if h < n:
                scores(h)
            if h < len(between):
                between[h]()
            if 1 <= h <= n:
                turn(h - 1)
            if h >= 2:
                values(h - 2)
        done = []
        if maps == 1:
            a = DVE.run(ready[n - 1], dve.reciprocal, rr, rs)
            for t in range(NT):
                r = rr[:, t * n:(t + 1) * n].unsqueeze(2).to_broadcast([P, n, width])
                m = DVE.run([a, *pv_of[n - 1]], dve.tensor_tensor,
                            dst(t).rearrange("p (n w) -> p n w", n=n),
                            psum[6 + t][:, 0:n * width].rearrange("p (n w) -> p n w", n=n), r, ALU.mult)
                bank_mark[6 + t] = (m,)
                done.append(m)
            return done
        return list(pv_of[n - 1])

    def bank_group_norm(n, d, dst, marks):
        ss = tiny(NT * n)
        a = [ACT.run(marks, act.activation, dst(t), psum[6 + t][:, 0:n * d], ACTF.Square) for t in range(NT)]
        s = [DVE.run([a[t]], dve.reduce_sum, ss[:, t * n:(t + 1) * n],
                     dst(t).rearrange("p (n d) -> p n d", n=n), axis=AX.X) for t in range(NT)]
        r, m = rstd_of(ss, d, NT * n, s)
        done = []
        for t in range(NT):
            rb = r[:, t * n:(t + 1) * n].unsqueeze(2).to_broadcast([P, n, d])
            m = DVE.run([m], dve.tensor_tensor, dst(t).rearrange("p (n d) -> p n d", n=n),
                        psum[6 + t][:, 0:n * d].rearrange("p (n d) -> p n d", n=n), rb, ALU.mult)
            bank_mark[6 + t] = (m,)
            done.append(m)
        return done

    out_marks = []

    def tab2(name, k):
        return table(name).rearrange("p (t k) -> p t k", t=NT)

    def hybrid_mixer(layer):
        marks = normed(lambda k: gain_cols[:, k:k + 1], lambda k: mod_cols[:, k:k + 1], mod_marks)
        split_to(st["use"] + SPL)
        mod_rest[0]()
        del out_marks[:]
        m = out_marks
        t_att, t_ret, rt = [], [], []

        def turn_attention():
            t_att.extend(turn_heads(lambda t, j: proj[:, t, j * P:(j + 1) * P], 8, P, m[0:4]))

        def rotate(t):
            v4 = proj[:, t, 1536:2560].rearrange("p (n d) -> p n d", n=8)
            c, s = (tab2(n, 64)[:, t, :].unsqueeze(1).to_broadcast([P, 8, 64]) for n in ("ret_cos", "ret_sin"))
            rt.append(rope(v4[:, :, 0:64], v4[:, :, 64:128], c, s, [P, 8, 64], [*m[4:8], *rt]))

        def turn_retention():
            t_ret.extend(turn_heads(lambda t, j: proj[:, t, 1536 + j * P:1536 + (j + 1) * P], 8, P, rt, at=8))

        project(io["w_in"][layer], [(c * SLAB, SLAB) for c in (0, 1, 3, 4, 2, 5, 6)], marks,
                func=lambda c: ACTF.Silu if c == 3072 else None,
                after={0: mod_rest[1], 1: mod_rest[2], 2: turn_attention, 3: lambda: rotate(0), 4: lambda: rotate(1), 5: turn_retention})
        o_a = attention(8, 64, lambda h, mp, t: qkT[64 * (h % 2):64 * (h % 2) + 64, h // 2, t * P:(t + 1) * P],
                        lambda h, mp: qkT[64 * (h % 2):64 * (h % 2) + 64, 4 + h // 2, :],
                        lambda h, kc: proj[:, kc, 1024 + 64 * h:1024 + 64 * (h + 1)],
                        64 ** -0.5, lambda t: xn[:, t, 0:SLAB], [*t_att, *m[8:10]], causal=True)
        ss = tiny(NT)
        a = [ACT.run([o_a[t]], act.activation, xn[:, t, SLAB:], xn[:, t, 0:SLAB], ACTF.Square,
                     accum_out=ss[:, t:t + 1]) for t in range(NT)]
        r, a2 = rstd_of(ss, SLAB, NT, a)
        o_a = [DVE.run([a2], dve.tensor_scalar, xn[:, t, 0:SLAB], xn[:, t, 0:SLAB], r[:, t:t + 1], None, ALU.mult)
               for t in range(NT)]
        pv = {}
        PE.need(*t_ret, *m[10:12])

        def ret_scores(h):
            b = 4 + h % 2
            PE.need(*bank_mark[b])
            pe.matmul(psum[b][:, 0:S], qkT[:, 12 + h, 0:P], qkT[:, 8 + h, :], start=True, stop=True)
            mk = PE.did(pe.matmul(psum[b][:, S:S + P], qkT[:, 12 + h, P:S], qkT[:, 8 + h, P:S], start=True, stop=True))
            dec = table("decay").rearrange("p (h s) -> p h s", h=4)[:, h, :]
            a = DVE.run([mk, *o_a, *pv.get(h - 2, ())], dve.tensor_tensor, probsT[:, h % 2, 0:S], psum[b][:, 0:S], dec, ALU.mult)
            a = DVE.run([mk], dve.tensor_tensor, probsT[:, h % 2, S:S + P], psum[b][:, S:S + P], dec[:, 0:P], ALU.mult)
            bank_mark[b] = (a,)
            return a

        def ret_values(h, mark):
            PE.need(mark, *bank_mark[6], *bank_mark[7]) if h == 0 else PE.need(mark)
            vr = [proj[:, kc, 2560 + h * P:2560 + (h + 1) * P] for kc in range(NT)]
            sT = probsT[:, h % 2, :]
            pe.matmul(psum[6][:, h * P:(h + 1) * P], sT[:, 0:P], vr[0], start=True, stop=True)
            pe.matmul(psum[7][:, h * P:(h + 1) * P], sT[:, P:S], vr[0], start=True, stop=False)
            pv[h] = (PE.did(pe.matmul(psum[7][:, h * P:(h + 1) * P], sT[:, S:S + P], vr[1], start=False, stop=True)),)

        mk = {0: ret_scores(0)}
        for h in range(4):
            if h < 3:
                mk[h + 1] = ret_scores(h + 1)
            ret_values(h, mk[h])
        o_r = bank_group_norm(4, P, lambda t: xn[:, t, SLAB:], [*pv[3], *o_a])
        o_r = [DVE.run([o_r[t], *m[12:14]], dve.tensor_tensor, xn[:, t, SLAB:], xn[:, t, SLAB:],
                       proj[:, t, 3072:3584], ALU.mult) for t in range(NT)]
        marks = turn_to_aT(lambda t, k: xn[:, t, k * P:(k + 1) * P], KD, [*o_a, *o_r],
                           lambda k: col("att_out_g", 4 * layer + k) if k < 4 else col("ret_out_g", 4 * layer + k - 4))
        project_out(io["w_out"][layer], marks, gate=0)

    def even_mixer():
        marks = normed(lambda k: col("ev_norm_2", k))
        ws_in = fetch("w_s_in", (w_s[:, :, :], io["ev_w_s_2"][0].rearrange("g i j -> i g j")))
        del out_marks[:]
        m = out_marks
        wT, qn, rt, vn, t8 = [], [], [], [], []

        def turn_w_s():
            PE.need(ws_in, *bank_mark[2], *bank_mark[3])
            for g in range(8):
                ins = pe.transpose(psum[2 + g // 4][:, (g % 4) * P:(g % 4 + 1) * P], w_s[:, g, :], ident)
            a = PE.did(ins)
            wT.extend(DVE.run([a], dve.tensor_copy, w_sT[:, 4 * i:4 * i + 4, :].rearrange("p g j -> p (g j)"),
                              psum[2 + i][:, :]) for i in range(2))

        qk = proj[:, :, 1024:2048].rearrange("p t (n d) -> p t n d", n=16)

        def norm_qk():
            gains = [(qk[:, t, 8 * i:8 * i + 8, :], row(g).unsqueeze(1).to_broadcast([P, 8, 64]))
                     for i, g in enumerate(("ev_q_norm_2", "ev_k_norm_2")) for t in range(NT)]
            qn.extend(group_norm(qk, 16, 64, m[0:4], gains))

        def rotate_qk():
            for t in range(NT):
                c, s = (tab2(n, 32)[:, t, :].unsqueeze(1).to_broadcast([P, 16, 32]) for n in ("diff_cos", "diff_sin"))
                rt.append(rope(qk[:, t, :, 0:32], qk[:, t, :, 32:64], c, s, [P, 16, 32], [*qn, *rt]))

        def norm_v():
            vn.extend(group_norm(proj[:, :, 512:1024].rearrange("p t (n d) -> p t n d", n=8), 8, 64, [*m[4:6], *qn],
                                 [(proj[:, :, 512:1024], row("ev_sgu_norm_2").unsqueeze(1).to_broadcast([P, NT, 512]))]))
            t8.extend(turn_heads(lambda t, j: proj[:, t, 1024 + j * P:1024 + (j + 1) * P], 8, P, rt))

        project(io["ev_w_in_2"][0], [(c * SLAB, SLAB) for c in (2, 3, 1, 0, 4)], marks,
                func=lambda c: ACTF.Gelu_apprx_tanh if c < 1024 else None,
                after={0: turn_w_s, 1: norm_qk, 2: rotate_qk, 3: norm_v})
        PE.need(*wT, *vn)
        for g in range(8):
            ins = pe.matmul(psum[2 + g // 4][:, (g % 4) * P:(g % 4 + 1) * P], w_sT[:, g, :],
                            proj[:, :, 512 + 64 * g:512 + 64 * (g + 1)], start=True, stop=True)
        a = PE.did(ins)
        ga = []
        for g in range(8):
            mixed = psum[2 + g // 4][:, (g % 4) * P:(g % 4 + 1) * P].rearrange("p (t d) -> p t d", t=NT)
            ga.append(DVE.run([a, *vn, *m[6:8]], dve.scalar_tensor_tensor, out=xn[:, :, 64 * g:64 * (g + 1)], in0=mixed,
                              scalar=col("ev_b_s_2", g), in1=proj[:, :, 64 * g:64 * (g + 1)], op0=ALU.add, op1=ALU.mult))
        bank_mark[2] = bank_mark[3] = (ga[-1],)
        lam_init = 0.8 - 0.6 * float(np.exp(-0.3 * 0))
        lam, pr = tiny(2), xn[:, 0, SLAB:SLAB + P]
        for i in range(2):
            a = DVE.run([*vn], dve.tensor_tensor, pr[:, 64 * i:64 * (i + 1)], row(f"ev_lam_q{i + 1}_2"),
                        row(f"ev_lam_k{i + 1}_2"), ALU.mult)
        a = DVE.run([a], dve.reduce_sum, lam, pr.rearrange("p (i d) -> p i d", i=2), axis=AX.X)
        a = ACT.run([a], act.activation, lam, lam, ACTF.Exp)
        a = DVE.run([a], dve.tensor_tensor, lam[:, 0:1], lam[:, 0:1], lam[:, 1:2], ALU.subtract)
        a = DVE.run([a], dve.tensor_scalar, lam[:, 0:1], lam[:, 0:1], lam_init, None, ALU.add)
        pv = attention(4, P, lambda h, mp, t: qkT[64 * mp:64 * mp + 64, h, t * P:(t + 1) * P],
                       lambda h, mp: qkT[64 * mp:64 * mp + 64, 4 + h, :],
                       lambda h, kc: proj[:, kc, 2048 + h * P:2048 + (h + 1) * P], 64 ** -0.5, None,
                       [*t8, *m, a], pair=lam[:, 0:1])
        o_b = bank_group_norm(4, P, lambda t: xn[:, t, SLAB:], [*pv, a])
        sub = tiny(1)
        sm = DVE.run(cols_in, dve.tensor_scalar, sub, col("ev_sub_norm_2", 0), 1.0 - lam_init, None, ALU.mult)
        marks = turn_to_aT(lambda t, k: xn[:, t, k * P:(k + 1) * P], KD, [*ga, *o_b, sm],
                           lambda k: 1.0 if k < 4 else sub)
        project_out(io["ev_w_out_2"][0], marks)

    def odd_mixer():
        marks = normed(lambda k: col("od_norm_2", k))
        del out_marks[:]
        m = out_marks
        CQ, CKV, KPE, GQ, GK, GV, UQ, UKV = 0, 256, 384, 416, 928, 1056, 1184, 1952
        cn, turned, gn, grt = [], [], [], []

        def norm_codes():
            ss = tiny(2 * NT)
            codes = ((CQ, 256), (CKV, 128))
            a = [ACT.run(m[0:2], act.activation, xn[:, t, SLAB + c0:SLAB + c0 + n], proj[:, t, c0:c0 + n], ACTF.Square,
                         accum_out=ss[:, NT * i + t:NT * i + t + 1]) for i, (c0, n) in enumerate(codes) for t in range(NT)]
            for i, (c0, n) in enumerate(codes):
                r, mk = rstd_of(ss[:, NT * i:NT * (i + 1)], n, NT, a)
                for t in range(NT):
                    cn.append(DVE.run([mk], dve.tensor_scalar, xn[:, t, c0:c0 + n], proj[:, t, c0:c0 + n],
                                      r[:, t:t + 1], None, ALU.mult))

        def turn_codes():
            turned.extend(turn_to_aT(lambda t, k: xn[:, t, k * P:(k + 1) * P], 3, cn,
                                     lambda k: col("od_cq_norm_2", k) if k < 2 else col("od_ckv_norm_2", 0), dst=codesT))

        gv = proj[:, :, GQ:GV].rearrange("p t (n d) -> p t n d", n=10)

        def norm_gqa(first, last, gain, marks):
            v, n = gv[:, :, first:last], last - first
            gn.extend(group_norm(v, n, 64, [*marks, *turned, *gn, *grt],
                                 [(v[:, t], row(gain).unsqueeze(1).to_broadcast([P, n, 64])) for t in range(NT)]))
            for t in range(NT):
                for part in range(2):
                    c, s = (tab2(name, 32)[:, t, 16 * part:16 * part + 16].unsqueeze(1).to_broadcast([P, n, 16])
                            for name in ("gqa_cos", "gqa_sin"))
                    o = 32 * part
                    grt.append(rope(v[:, t, :, o:o + 16], v[:, t, :, o + 16:o + 32], c, s, [P, n, 16], [*gn, *grt]))

        def behind_gq():
            turn_codes()
            norm_gqa(0, 8, "od_gqa_q_norm_2", m[2:4])

        project(io["od_w_in_2"][0], [(CQ, GQ - CQ), (GQ, GK - GQ), (GK, UQ - GK)], marks,
                after={0: norm_codes, 1: behind_gq, 2: lambda: norm_gqa(8, 10, "od_gqa_k_norm_2", m[4:6])})
        project(io["od_w_uq_2"][0], [(0, SLAB), (SLAB, 256)], turned, kd=2, at=UQ, left=codesT)
        load((lambda r: r[:, :], io["od_w_ukv_2"][0]))
        u = st["use"]
        split_to(u + 1)
        PE.need(turned[2])
        pe.wait_ge(lo_done, u + 1)
        kvm = []
        for i in range(4):
            half, t = i // 2, i % 2
            PE.need(*bank_mark[i])
            ins = passes(psum[i][:, :], [z[:, 2, t * P:(t + 1) * P] for z in codesT],
                         [z[u % SPL][:, half * SLAB:(half + 1) * SLAB] for z in (hi, lo)], True, True)
            if i < 3:
                mk = PE.did(ins)
            else:
                ins.then_inc(unit_free, 1)
                mk = (unit_free, u + 1)
                st["use"] += 1
            dst = proj[:, t, UKV + half * SLAB:UKV + (half + 1) * SLAB]
            kvm.append(ACT.run([mk], act.activation, dst, psum[i][:, :], ACTF.Copy) if t == 0 else
                       DVE.run([mk], dve.tensor_copy, dst, psum[i][:, :]))
            bank_mark[i] = (kvm[-1],)
        split_to(u + 1 + 4)
        m2 = [*out_marks, *kvm]
        kf = k_full[:, :, :].rearrange("p t (n d) -> p t n d", n=8)
        kv = proj[:, :, UKV:UKV + 1024].rearrange("p t (n d) -> p t n d", n=8)
        qv = proj[:, :, UQ:UQ + 768].rearrange("p t (n d) -> p t n d", n=8)
        km, rt, mn = [], [], []

        def whole_k():
            for t in range(NT):
                km.append(DVE.run(m2, dve.tensor_copy, kf[:, t, :, 0:64], kv[:, t, :, 0:64]))
                km.append(ACT.run(m2, act.activation, kf[:, t, :, 64:96],
                                  proj[:, t, KPE:KPE + 32].unsqueeze(1).to_broadcast([P, 8, 32]), ACTF.Copy))

        def norm_mla(v, gain):
            mn.extend(group_norm(v, 8, 96, [*m2, *km, *gn, *mn],
                                 [(v[:, t], row(gain).unsqueeze(1).to_broadcast([P, 8, 96])) for t in range(NT)]))

        def rotate_mla(v):
            for t in range(NT):
                c, s = (tab2(n, 16)[:, t, :].unsqueeze(1).to_broadcast([P, 8, 16]) for n in ("mla_cos", "mla_sin"))
                rt.append(rope(v[:, t, :, 64:80], v[:, t, :, 80:96], c, s, [P, 8, 16], [*mn, *grt, *rt]))

        tq = turn_heads(lambda t, j: gq_pairs[:, t, j, :], 4, P, repack(gv, grt))
        tk = turn_heads(lambda t, j: proj[:, t, GK:GK + P], 1, P, grt, at=4)
        o_d = attention(8, 64, lambda h, mp, t: qkT[64 * (h // 4):64 * (h // 4) + 64, h % 4, t * P:(t + 1) * P],
                        lambda h, mp: qkT[64 * (h // 4):64 * (h // 4) + 64, 4, :],
                        lambda h, kc: proj[:, kc, GV + 64 * (h // 4):GV + 64 * (h // 4) + 64], 64 ** -0.5,
                        lambda t: xn[:, t, SLAB:], [*tq, *tk, *m2],
                        between=[whole_k, lambda: norm_mla(kf, "od_mla_k_norm_2"), lambda: rotate_mla(kf),
                                 lambda: norm_mla(qv, "od_mla_q_norm_2"), lambda: rotate_mla(qv)])
        tq = turn_heads(lambda t, j: qv[:, t, j, :], 8, 96, [*rt, *o_d])
        tk = turn_heads(lambda t, j: kf[:, t, j, :], 8, 96, rt, at=8)
        o_c = attention(8, 64, lambda h, mp, t: qkT[0:96, h, t * P:(t + 1) * P], lambda h, mp: qkT[0:96, 8 + h, :],
                        lambda h, kc: kv[:, kc, h, 64:128], 96 ** -0.5, lambda t: xn[:, t, 0:SLAB], [*tq, *tk])
        marks = turn_to_aT(lambda t, k: xn[:, t, k * P:(k + 1) * P], KD, [*o_c, *o_d], lambda k: 1.0)
        project_out(io["od_w_out_2"][0], marks)

    def repack(gv, marks):
        src = gv[:, :, 0:8, :]
        return [DVE.run(marks, dve.tensor_copy, gq_pairs[:, t, :, :].rearrange("p c (r d) -> p c r d", r=2),
                        src[:, t].rearrange("p (r c) d -> p c r d", r=2)) for t in range(NT)]

    def route():
        rm = fetch("router_in", (router[:, :, :], io["router_w"][0].rearrange("(k p) e -> p k e", p=P)))
        marks = normed(lambda k: gain_cols[:, 8 + k:9 + k], lambda k: mod_cols[:, 16 + k:17 + k])
        PE.need(rm, *marks, *bank_mark[3])
        for t in range(NT):
            for k in range(KD):
                ins = pe.matmul(psum[3][:, t * NE:(t + 1) * NE], hT_full[:, k, t * P:(t + 1) * P],
                                router[:, k, :], start=k == 0, stop=k == KD - 1)
        m = PE.did(ins)
        for t in range(NT):
            lg, top, idx = tiny(NE), tiny(NE), tiny(NE)
            a = DVE.run([m], dve.tensor_copy, lg, psum[3][:, t * NE:(t + 1) * NE])
            b = DVE.run([a], dve.max, top, lg)
            iu = top_idx[:, :]
            b = DVE.run([b], dve.max_index, iu, top, lg)
            b = DVE.run([b], dve.tensor_copy, idx, iu)
            e, r = tiny(2), tiny(2)
            a = DVE.run([b], dve.tensor_tensor, e[:, 0:1], top[:, 1:2], top[:, 0:1], ALU.subtract)
            a = ACT.run([a], act.activation, e[:, 0:1], e[:, 0:1], ACTF.Exp)
            a = DVE.run([a], dve.tensor_scalar, e[:, 1:2], e[:, 0:1], 1.0, None, ALU.add)
            a = DVE.run([a], dve.reciprocal, r[:, 0:1], e[:, 1:2])
            a = DVE.run([a], dve.tensor_tensor, r[:, 1:2], r[:, 0:1], e[:, 0:1], ALU.mult)
            w = [tiny(NE), tiny(NE)]
            for i in range(2):
                a = DVE.run([a, b], dve.tensor_scalar, w[i], table("iota8"), idx[:, i:i + 1], r[:, i:i + 1],
                            ALU.is_equal, ALU.mult)
            wt = DVE.run([a], dve.tensor_tensor, expert_w[:, t:2 * NE:2], w[0], w[1], ALU.add)
        bank_mark[3] = (a,)
        a = DVE.run([wt], dve.tensor_scalar, picked[:, :], expert_w[:, :], 0.0, None, ALU.is_gt)
        PE.need(a)
        for c0, terms in ((16, (("before", 0),)), (24, ((None, 0), ("before", 1))), (32, ((None, 0), (None, 1)))):
            for n, (left, t) in enumerate(terms):
                ins = pe.matmul(psum[3][:, c0:c0 + NE], table(left) if left else ones_sq[:, :],
                                picked[:, t:2 * NE:2], start=n == 0, stop=n == len(terms) - 1)
        m = PE.did(ins)
        for t in range(NT):
            DVE.run([m], dve.scalar_tensor_tensor, out=slot_of[:, t:2 * NE:2], in0=psum[3][:, 16 + 8 * t:24 + 8 * t],
                    scalar=1.0, in1=picked[:, t:2 * NE:2], op0=ALU.add, op1=ALU.mult)
        DVE.run([m], dve.memset, slot_of[:, 2 * NE:], 0.0)
        a = DVE.run([m], dve.reduce_max, busiest[:, :], psum[3][:, 32:32 + NE], axis=AX.X)
        bank_mark[3] = (a,)
        b = DVE.run([a], dve.tensor_scalar, slot_of[:, :], slot_of[:, :], 1.0, None, ALU.subtract)
        b = DVE.run([b], dve.tensor_copy, busiest_i[:, :], busiest[:, :])
        return [*marks, wt, b]

    def moe(marks):
        gate, up, down = (io[n][0].rearrange("(q z) r c -> q z r c", z=2) for n in ("moe_w_gate", "moe_w_up", "moe_w_down"))
        pair_rounds = 2 * FFN_UNITS // RAW
        base, sp_lap = st["load"], st["sp_lap"]
        with sp.Fori(0, NE // 2) as q:
            st["sp_lap"] = sp_lap + pair_rounds * q
            for z in range(2):
                ffn_load(*(lambda c, k, w=w: w[ds(q, 1), z, k * P:(k + 2) * P, ds(c * STEP_F, STEP_F)]
                           .rearrange("a (k p) n -> p (a k) n", p=P) for w in (gate, up)),
                         lambda c, f: down[ds(q, 1), z, ds(c * STEP_F + f * P, P), :].rearrange("a p n -> p (a n)"))
        st["load"], st["sp_lap"] = base + NE * FFN_UNITS, sp_lap
        marks = [*marks, *(m for b in range(8) for m in bank_mark[b])]
        for e in (PE, ACT, DVE):
            e.need(*marks)
        most = nc.values_load(busiest_i[0:1, 0:1], engines=compute, min_val=0, max_val=S)
        before = dict(st)
        with nc.If(most > SLOTS):
            experts_on_all_tokens(pair_rounds)
        after = dict(st)
        st.update(before)
        with nc.Else():
            experts_on_slots(pair_rounds)
        assert st == after
        ffn["ev"] = ev_dense
        for b in range(8):
            bank_mark[b] = ()
        for t in range(NT):
            a = DVE.run([], dve.tensor_tensor, xn[:, t, :], ysum[:, t, :], gates[:, 1, :], ALU.mult)
            x_mark[0] = DVE.run([a, x_mark[0]], dve.tensor_tensor, x[:, t, :], x[:, t, :], xn[:, t, :], ALU.add)
        for b in range(8):
            bank_mark[b] = (x_mark[0],)

    def experts_on_all_tokens(pair_rounds):
        g0, ffn["g"], ffn["ev"] = ffn["g"], 0, ev_all
        u, split = st["use"], st["split"]
        pe_end, dve_end = Rounds(nc, pe, "all_pe_end", 1), Rounds(nc, dve, "all_dve_end", 4)
        zero_y([])
        with nc.Fori(0, NE // 2, engines=compute) as q:
            for z in range(2):
                st["lap"] = pair_rounds * q
                ffn_steps(weight=lambda t: expert_w[:, ds(4 * q + 2 * z + t, 1)])
        st["lap"], st["split"], st["use"] = 0, split + NE * FFN_UNITS, u + NE * FFN_UNITS
        ffn["g"] = g0
        m = close_y(pe_end)
        for t in range(NT):
            for half in range(2):
                m2 = dve_end.run([m], dve.tensor_copy, ysum[:, t, half * SLAB:(half + 1) * SLAB],
                                 psum[4 + 2 * t + half][:, :])
        dve_end.need(m2)

    def experts_on_slots(pair_rounds):
        ev = ev_slots
        once = Rounds(nc, act, "slots_xn_hi", 4), Rounds(nc, dve, "slots_xn_lo", 2)

        h = once[0].run([], act.activation, xn_split[0][:, :, :], xn[:, :, :], ACTF.Copy)
        m = once[1].run([h], dve.tensor_tensor, xn_split[1][:, :, :], xn[:, :, :],
                        xn_split[0][:, :, :].bitcast(F32), ALU.subtract)
        zero = once[1].run([], dve.memset, ysum[:, :, :], 0.0)
        pe.wait_ge(*m)
        dve.wait_ge(*zero)
        act.wait_ge(*zero)

        def gate_up(j0, u, g, lap, z):
            if j0 == 0 and g > 1:
                pe.wait_ge(ev.hid, g - 1 + 2 * lap)
            for j in (j0, j0 + 1):
                pe.wait_ge(lo_done, u + j + 1 + 12 * lap)
                w = unit(u + j)
                for kk in range(2):
                    k = 2 * j + kk
                    ins = passes(psum[g % 2][:, :], [a[:, k, z * P:(z + 1) * P] for a in aT],
                                 [r[:, kk, :] for r in w], k == 0, k == KD - 1)
                ins.then_inc(unit_free, 1)

        def hidden(u_end, g, lap):
            act.wait_ge(unit_free, u_end + 12 * lap)
            if g > 1:
                act.wait_ge(ev.hid, g - 1 + 2 * lap)
            act.activation(silu_g[:, g % 2, :], psum[g % 2][:, 0:STEP_F], ACTF.Silu).then_inc(ev.silu, 1)
            dve.wait_ge(ev.silu, g + 1 + 2 * lap)
            if g > 1:
                dve.wait_ge(ev.turned, g - 1 + 2 * lap)
            dve.tensor_tensor(hid[:, g % 2, :], silu_g[:, g % 2, :], psum[g % 2][:, STEP_F:], ALU.mult)\
               .then_inc(ev.hid, 1)

        def turn(g, lap):
            pe.wait_ge(ev.hid, g + 1 + 2 * lap)
            if g > 0:
                pe.wait_ge(ev.lo, g + 2 * lap)
            for f in range(2):
                ins = pe.transpose(psum[2][:, f * P:(f + 1) * P], hid[:, g % 2, f * P:(f + 1) * P], ident)
            ins.then_inc(ev.turned, 1)

        def turned_split(u_before, g, lap):
            act.wait_ge(ev.turned, g + 1 + 2 * lap)
            act.wait_ge(unit_free, u_before + 12 * lap)
            act.activation(hidT[0][:, 0:S], psum[2][:, 0:S], ACTF.Copy).then_inc(ev.hi, 1)
            dve.wait_ge(ev.hi, g + 1 + 2 * lap)
            dve.tensor_tensor(hidT[1][:, 0:S], psum[2][:, 0:S], hidT[0][:, 0:S].bitcast(F32),
                              ALU.subtract).then_inc(ev.lo, 1)

        def down(u, g, lap):
            pe.wait_ge(ev.lo, g + 1 + 2 * lap)
            for f in range(2):
                pe.wait_ge(lo_done, u + f + 1 + 12 * lap)
                for half in range(2):
                    ins = passes(psum[4 + half][:, :], [a[:, f * P:(f + 1) * P] for a in hidT],
                                 [s[(u + f) % SPL][:, half * SLAB:(half + 1) * SLAB] for s in (hi, lo)], False, False)
                ins.then_inc(unit_free, 1)

        def one_hots(V, z, c):
            V.run([], dve.tensor_copy, next_w[:, :], expert_w[:, c(0, 2)])
            for t in range(NT):
                m = V.run([], dve.tensor_scalar, onehot[:, z, t, :], table("iota"), slot_of[:, c(t, 1)], None,
                          ALU.is_equal)
            return m

        def turn_one_hots(B, z, m):
            B.need(m)
            for t in range(NT):
                pe.transpose(psum[3][:, t * P:(t + 1) * P], onehot[:, z, t, :].bitcast(F32), ident)
            for t in range(NT):
                ins = pe.matmul(psum[3][:, S:S + 1], onehot[:, z, t, :].bitcast(F32), next_w[:, t:t + 1],
                                start=t == 0, stop=t == 1)
            return B.did(ins)

        def keep_turned(A, z, m):
            A.run([m], act.activation, slot_w[:, z:z + 1], psum[3][:, S:S + 1], ACTF.Copy)
            return A.run([m], act.activation, onehotT[:, z * S:(z + 1) * S], psum[3][:, 0:S], ACTF.Copy)

        def gather(B, z):
            for k in range(KD):
                for n, (t, part) in enumerate(((0, 0), (0, 1), (1, 0), (1, 1))):
                    ins = pe.matmul(psum[6 + k // 4][:, (k % 4) * P:(k % 4 + 1) * P],
                                    xn_split[part][:, t, k * P:(k + 1) * P], onehot[:, z, t, :],
                                    start=n == 0, stop=n == 3)
            return B.did(ins)

        def modulate(A, V, z, m):
            V.need(m)
            for k in range(KD):
                f = V.run([], dve.tensor_scalar, x_full[:, k, :], psum[6 + k // 4][:, (k % 4) * P:(k % 4 + 1) * P],
                          gain_cols[:, 8 + k:9 + k], mod_cols[:, 16 + k:17 + k], ALU.mult, ALU.add)
            h = A.run([f], act.activation, aT[0][:, :, z * P:(z + 1) * P], x_full[:, :, :], ACTF.Copy)
            return V.run([h], dve.tensor_tensor, aT[1][:, :, z * P:(z + 1) * P], x_full[:, :, :],
                         aT[0][:, :, z * P:(z + 1) * P].bitcast(F32), ALU.subtract)

        def weigh(A, V, z, y_mark):
            for half in range(2):
                part = slice(half * SLAB, (half + 1) * SLAB)
                h = A.run([y_mark], act.activation, y_split[0][:, part], psum[4 + half][:, :], ACTF.Identity,
                          scale=slot_w[:, z:z + 1])
                m = V.run([h], dve.scalar_tensor_tensor, out=y_split[1][:, part], in0=psum[4 + half][:, :],
                          scalar=slot_w[:, z:z + 1], in1=y_split[0][:, part].bitcast(F32), op0=ALU.mult,
                          op1=ALU.subtract)
            return m

        def give_back(B, V, z, m, spare):
            B.need(m)
            done = []
            for t, banks in enumerate(((6, 7), spare)):
                for half in range(2):
                    for part in range(2):
                        ins = pe.matmul(psum[banks[half]][:, :], onehotT[:, z * S + t * P:z * S + (t + 1) * P],
                                        y_split[part][:, half * SLAB:(half + 1) * SLAB], start=part == 0, stop=part == 1)
                given = B.did(ins)
                for half in range(2):
                    ys = ysum[:, t, half * SLAB:(half + 1) * SLAB]
                    m = V.run([given], dve.tensor_tensor, ys, ys, psum[banks[half]][:, :], ALU.add)
                done.append(m)
            return given, done

        A0, B0, V0 = Rounds(nc, act, "first_act", 3), Rounds(nc, pe, "first_pe", 2), Rounds(nc, dve, "first_dve", 12)
        m = turn_one_hots(B0, 0, one_hots(V0, 0, lambda t, n: slice(t, t + n)))
        kept = keep_turned(A0, 0, m)
        ready = modulate(A0, V0, 0, gather(B0, 0))
        B0.need(kept, ready)

        per_expert = {"act": 2 + 1 + 2, "pe": 1 + 1 + 2 + 1, "dve": 3 + 2 * NT + KD + 1 + 2}
        A, B, V = (Rounds(nc, q, "slots_" + n, 2 * per_expert[n]) for q, n in ((act, "act"), (pe, "pe"), (dve, "dve")))
        u, split = st["use"], st["split"]
        zy = [once[0].run([], act.activation, y_split[i][:, :], ysum[:, :, :].rearrange("p t d -> p (t d)")[:, 0:D], ACTF.Copy)
              for i in range(2)]
        zo = once[0].run([], act.activation, onehotT[:, S:2 * S], ysum[:, 0, 0:S], ACTF.Copy)
        pe.wait_ge(*zo)
        with nc.Fori(0, NE // 2, engines=compute) as q:
            for r in (A, B, V):
                r.count, r.round = 0, q
            lap = pair_rounds * q
            st["lap"] = lap
            for z in range(2):
                g, un = STEPS * z, u + FFN_UNITS * z
                next_hot = one_hots(V, 1 - z, lambda t, n: ds(4 * q + 2 * (z + 1) + t, n))
                gate_up(0, un, g, lap, z)
                gate_up(2, un, g, lap, z)
                turned = turn_one_hots(B, 1 - z, next_hot)
                given, back = give_back(B, V, 1 - z, weighed if z else (V.sem, 3 + V.per_round * q), ((g + 1) % 2, 2))
                look_ahead(UNITS_GU)
                A.need(given)
                keep_turned(A, 1 - z, turned)
                B.need(back[0])
                got = gather(B, 1 - z)
                B.need(back[1])
                zero_y([], (4, 5))
                g, un = g + 1, un + UNITS_GU
                ready = modulate(A, V, 1 - z, got)
                here = st["split"]
                with nc.Fori(0, (STEPS - 1) // 2, engines=compute) as i:
                    for b in range(2):
                        gg, uu, ll = g + b, un + 6 * b, lap + i
                        st["lap"] = ll
                        gate_up(0, uu, gg, ll, z)
                        hidden(uu, gg - 1, ll)
                        turn(gg - 1, ll)
                        look_ahead(UNITS_D)
                        turned_split(uu, gg - 1, ll)
                        gate_up(2, uu, gg, ll, z)
                        look_ahead(UNITS_GU)
                        down(uu + UNITS_GU, gg - 1, ll)
                st["lap"], st["split"] = lap, here + RAW * (STEPS - 1) // 2
                g, un = g + STEPS - 1, un + 6 * (STEPS - 1)
                hidden(un, g - 1, lap)
                turn(g - 1, lap)
                turned_split(un, g - 1, lap)
                look_ahead(UNITS_D)
                down(un, g - 1, lap)
                B.need(ready)
                weighed = weigh(A, V, z, close_y(B, (4, 5)))
            for r in (A, B, V):
                assert r.count == r.per_round, (r.sem.name, r.count)
        Bl, Vl = Rounds(nc, pe, "last_pe", 2), Rounds(nc, dve, "last_dve", 4)
        V.round, V.count = NE // 2 - 1, V.per_round
        _, back = give_back(Bl, Vl, 1, (V.sem, V.per_round * (NE // 2)), (1, 2))
        Vl.need(back[1])
        st["lap"], st["split"], st["use"] = 0, split + NE * FFN_UNITS, u + NE * FFN_UNITS

    def final_norm():
        fm = fetch("final_g_in", (final_g[:, :], io["final_norm_g"].rearrange("(a n) -> a n", a=1).to_broadcast([P, D])))
        ss = tiny(NT)
        sq = [ACT.run([x_mark[0]], act.activation, xn[:, t, :], x[:, t, :], ACTF.Square,
                      accum_out=ss[:, t:t + 1]) for t in range(NT)]
        r, m = rstd_of(ss, D, NT, sq)
        for t in range(NT):
            x_mark[0] = DVE.run([m, fm], dve.scalar_tensor_tensor, out=x[:, t, :], in0=x[:, t, :],
                                scalar=r[:, t:t + 1], in1=final_g[:, :], op0=ALU.mult, op1=ALU.mult)

    def ffn_2(name, layer):
        marks = normed(lambda k: col(f"{name}_norm_2", 8 * layer + k))
        gu, dn = io[f"{name}_w_gu_2"][layer], io[f"{name}_w_down_2"][layer]
        dense_ffn(lambda c, k: cols_of(gu, c, k), lambda c, k: cols_of(gu, c, k, FF),
                  lambda c, f: rows_of(dn, c, f), marks, factor=0.5)

    def block_1_ffn():
        marks = normed(lambda k: gain_cols[:, 8 + k:9 + k], lambda k: mod_cols[:, 16 + k:17 + k])
        load_ada([*marks, x_mark[0]])
        fetch_bias(1)
        PE.need(*bank_mark[3])
        bank_mark[3] = ((ada_rows, ADA_SLABS - 1),)
        dense_ffn(lambda c, k: cols_of(io["ffn_w_gate"][0], c, k), lambda c, k: cols_of(io["ffn_w_up"][0], c, k),
                  lambda c, f: rows_of(io["ffn_w_down"][0], c, f), marks, g=1, aside=(ada_sums, ada_out),
                  ahead=lambda: conditioning(1, lambda k: (ada_rows, k)))

    stages = [first_conditioning, lambda: hybrid_mixer(0), block_1_ffn, lambda: hybrid_mixer(1), lambda: moe(route()), final_norm,
              lambda: ffn_2("ffn1", 0), even_mixer, lambda: ffn_2("ffn2", 0),
              lambda: ffn_2("ffn1", 1), odd_mixer, lambda: ffn_2("ffn2", 1)]
    for stage in stages[:upto]:
        stage()
    assert st["use"] == st["load"] == st["split"] == total, (st, total)
    store_x()


def tables_of_shapes():
    f = np.float32
    pos = np.arange(S)
    out = {"ident": np.eye(P, dtype=f)}
    causal = np.where(pos[None, :] <= pos[:, None], 0.0, -1e30).astype(f)
    out["causal"] = causal.reshape(NT, P, S).transpose(1, 0, 2)
    gamma = np.log(1.0 - 2.0 ** (-5.0 - np.arange(4, dtype=np.float64)))
    diff = pos[None, :] - np.arange(P)[:, None]
    out["decay"] = (np.where(diff >= 0, np.exp(np.maximum(diff, 0)[None] * gamma[:, None, None]), 0.0)
                    * P ** -0.5).astype(f).transpose(1, 0, 2)

    def angles(p, dim):
        inv = f(10000.0) ** (-np.arange(dim // 2, dtype=f) / f(dim // 2))
        ang = p.astype(f)[:, None] * inv.astype(f)[None, :]
        return [g(ang).astype(f).reshape(NT, P, dim // 2).transpose(1, 0, 2) for g in (np.cos, np.sin)]

    for name, dim in (("ret", 128), ("diff", 64), ("mla", 32)):
        out[name + "_cos"], out[name + "_sin"] = angles(pos, dim)
    row_angle, col_angle = angles(pos // 64, 32), angles(pos % 64, 32)
    for i, n in enumerate(("gqa_cos", "gqa_sin")):
        out[n] = np.concatenate([row_angle[i], col_angle[i]], axis=2)
    out["iota8"] = np.tile(np.arange(NE, dtype=f), (P, 1))
    out["iota"] = np.tile(np.arange(P, dtype=f), (P, 1))
    out["before"] = np.triu(np.ones((P, P), f), 1)
    return np.concatenate([np.ascontiguousarray(out[n]).reshape(P, -1) for n in TABLES], axis=1).astype(f)


def kernel(**inputs):
    import concourse.bacc as bacc
    from concourse.bass_utils import run_bass_kernel_spmd

    nc = bacc.Bacc("TRN2", target_bir_lowering=False, num_devices=1)
    arrays = {name: np.ascontiguousarray(a) for name, a in inputs.items()}
    arrays["tables"] = tables_of_shapes()
    io = {name: nc.dram_tensor(name, a.shape, mybir.dt.from_np(a.dtype), kind="ExternalInput").ap()
          for name, a in arrays.items()}
    out = nc.dram_tensor("out", (1, S, D), F32, kind="ExternalOutput").ap()
    program(nc, io, out)
    result = run_bass_kernel_spmd(nc, [arrays], core_ids=[0])
    return result.results[0]["out"]
```
